# Optimizing a Trainium2 kernel written in Bass

```python
import jax, jax.numpy as jnp
from jax import lax
import numpy as np

D_MODEL = 1024
BATCH = 1
SEQ = 512
DEPTH = 1

MIX_WIDTH = D_MODEL
A_HEADS = 4
A_WIDTH = MIX_WIDTH // 2
A_HEAD_DIM = A_WIDTH // A_HEADS
CHUNK = 128
B_WIDTH = MIX_WIDTH - A_WIDTH
CONV_WIDTH = 3
IN_WIDTH = 2 * A_WIDTH + 3 * B_WIDTH
MEM_LEN = 256
X_HEADS = 4
X_HEAD_DIM = D_MODEL // X_HEADS
PEER_HEADS = 8
N_KEYS = 128
N_EXPERTS = N_KEYS * N_KEYS
PEER_TOPK = 16
D_KEY = 256
HALF_KEY = D_KEY // 2
PEER_BLOCK = 128
LN_EPS = 1e-5
DN_ALPHA = (2 * DEPTH) ** 0.25
DN_BETA = (8 * DEPTH) ** -0.25

kernel_name = "hybrid_sgu_shortconv_xattn_peer_deepnorm"

def _layernorm(x, g, b):
    xf = x.astype(jnp.float32)
    mu = jnp.mean(xf, axis=-1, keepdims=True)
    var = jnp.mean(jnp.square(xf - mu), axis=-1, keepdims=True)
    y = (xf - mu) * lax.rsqrt(var + LN_EPS) * g.astype(jnp.float32) + b.astype(jnp.float32)
    return y.astype(x.dtype)

def _gelu(x):
    return jax.nn.gelu(x, approximate=False)

def _hybrid_mixer(x, w_in, b_in, sgu_g, sgu_b, w_spatial, b_spatial, conv_w, w_out):
    bsz, seq, _ = x.shape
    z = jnp.einsum('bsd,de->bse', x, w_in) + b_in
    u_a, v_a, h_b, gate_b, gate_c = jnp.split(
        z, [A_WIDTH, 2 * A_WIDTH, 2 * A_WIDTH + B_WIDTH, 2 * A_WIDTH + 2 * B_WIDTH], axis=-1)
    u_a = _gelu(u_a)
    v_a = _gelu(v_a).reshape(bsz, seq // CHUNK, CHUNK, A_HEADS, A_HEAD_DIM)
    v_a = _layernorm(v_a, sgu_g, sgu_b)
    causal = jnp.tril(jnp.ones((CHUNK, CHUNK), dtype=bool))
    ws = jnp.where(causal[None], w_spatial, 0.0)
    mixed = jnp.einsum('hts,bcshd->bcthd', ws, v_a) + b_spatial.T[:, :, None]
    y_a = u_a * mixed.reshape(bsz, seq, A_WIDTH)
    zc = gate_c * h_b
    conv = lax.conv_general_dilated(
        zc, conv_w, window_strides=(1,), padding=((CONV_WIDTH - 1, 0),),
        dimension_numbers=('NWC', 'WIO', 'NWC'), feature_group_count=B_WIDTH)
    y_b = gate_b * conv
    y = jnp.concatenate([y_a, y_b], axis=-1)
    return jnp.einsum('bse,ed->bsd', y, w_out)

def _cross_attention(x, mem, w_q, w_kv, w_o):
    bsz, seq, _ = x.shape
    q = jnp.einsum('bsd,de->bse', x, w_q).reshape(bsz, seq, X_HEADS, X_HEAD_DIM)
    kv = jnp.einsum('bmd,de->bme', mem, w_kv).reshape(bsz, mem.shape[1], 2, X_HEADS, X_HEAD_DIM)
    k, v = kv[:, :, 0], kv[:, :, 1]
    scores = jnp.einsum('bshk,bmhk->bhsm', q, k).astype(jnp.float32) * (X_HEAD_DIM ** -0.5)
    p = jax.nn.softmax(scores, axis=-1).astype(x.dtype)
    o = jnp.einsum('bhsm,bmhk->bshk', p, v).reshape(bsz, seq, D_MODEL)
    return jnp.einsum('bsd,de->bse', o, w_o)

def _peer(x, w_query, sub_keys, w_down, w_up):
    bsz, seq, _ = x.shape
    n_tok = bsz * seq
    xt = x.reshape(n_tok, D_MODEL)
    q = jnp.einsum('td,de->te', xt, w_query).reshape(n_tok, PEER_HEADS, 2, HALF_KEY)
    sc = jnp.einsum('thpk,hpnk->thpn', q, sub_keys).astype(jnp.float32)
    va, ia = lax.top_k(sc[:, :, 0], PEER_TOPK)
    vb, ib = lax.top_k(sc[:, :, 1], PEER_TOPK)
    cand = (va[..., :, None] + vb[..., None, :]).reshape(n_tok, PEER_HEADS, PEER_TOPK * PEER_TOPK)
    top, flat = lax.top_k(cand, PEER_TOPK)
    expert = (jnp.take_along_axis(ia, flat // PEER_TOPK, axis=-1) * N_KEYS
              + jnp.take_along_axis(ib, flat % PEER_TOPK, axis=-1))
    gate = jax.nn.softmax(top, axis=-1).astype(x.dtype)
    n_blk = n_tok // PEER_BLOCK
    hk = PEER_HEADS * PEER_TOPK
    expert = expert.reshape(n_blk, PEER_BLOCK, hk)
    gate = gate.reshape(n_blk, PEER_BLOCK, hk)

    def block(args):
        xb, eb, gb = args
        act = _gelu(jnp.einsum('tkd,td->tk', w_down[eb], xb))
        return jnp.einsum('tk,tkd->td', gb * act, w_up[eb])

    out = lax.map(block, (xt.reshape(n_blk, PEER_BLOCK, D_MODEL), expert, gate))
    return out.reshape(bsz, seq, D_MODEL)

def _normal(k, shape, scale):
    return jax.random.normal(k, shape, jnp.float32) * scale

def setup_inputs(seed: int = 0) -> dict:
    key = jax.random.key(seed)
    ks = jax.random.split(key, 24)
    L, D = DEPTH, D_MODEL
    return {
        "x": _normal(ks[0], (BATCH, SEQ, D), 1.0),
        "mem": _normal(ks[1], (BATCH, MEM_LEN, D), 1.0),
        "w_in": _normal(ks[2], (L, D, IN_WIDTH), D ** -0.5),
        "b_in": _normal(ks[3], (L, IN_WIDTH), 0.02),
        "sgu_g": 1.0 + _normal(ks[4], (L, A_HEADS, A_HEAD_DIM), 0.02),
        "sgu_b": _normal(ks[5], (L, A_HEADS, A_HEAD_DIM), 0.02),
        "w_spatial": _normal(ks[6], (L, A_HEADS, CHUNK, CHUNK), CHUNK ** -0.5),
        "b_spatial": 1.0 + _normal(ks[7], (L, A_HEADS, CHUNK), 0.02),
        "conv_w": _normal(ks[8], (L, CONV_WIDTH, 1, B_WIDTH), CONV_WIDTH ** -0.5),
        "w_mix_out": _normal(ks[9], (L, MIX_WIDTH, D), MIX_WIDTH ** -0.5 * DN_BETA),
        "ln1_g": 1.0 + _normal(ks[10], (L, D), 0.02),
        "ln1_b": _normal(ks[11], (L, D), 0.02),
        "w_xq": _normal(ks[12], (L, D, D), D ** -0.5),
        "w_xkv": jnp.concatenate([_normal(ks[13], (L, D, D), D ** -0.5),
                                  _normal(ks[14], (L, D, D), D ** -0.5 * DN_BETA)], axis=-1),
        "w_xo": _normal(ks[15], (L, D, D), D ** -0.5 * DN_BETA),
        "ln2_g": 1.0 + _normal(ks[16], (L, D), 0.02),
        "ln2_b": _normal(ks[17], (L, D), 0.02),
        "w_pq": _normal(ks[18], (L, D, PEER_HEADS * D_KEY), D ** -0.5),
        "sub_keys": _normal(ks[19], (L, PEER_HEADS, 2, N_KEYS, HALF_KEY), HALF_KEY ** -0.5),
        "w_down": _normal(ks[20], (L, N_EXPERTS, D), D ** -0.5),
        "w_up": _normal(ks[21], (L, N_EXPERTS, D), DN_BETA),
        "ln3_g": 1.0 + _normal(ks[22], (L, D), 0.02),
        "ln3_b": _normal(ks[23], (L, D), 0.02),
    }

def reference(x, mem, w_in, b_in, sgu_g, sgu_b, w_spatial, b_spatial, conv_w, w_mix_out,
              ln1_g, ln1_b, w_xq, w_xkv, w_xo, ln2_g, ln2_b, w_pq, sub_keys, w_down, w_up,
              ln3_g, ln3_b):
    for l in range(DEPTH):
        h = _hybrid_mixer(x, w_in[l], b_in[l], sgu_g[l], sgu_b[l], w_spatial[l], b_spatial[l],
                          conv_w[l], w_mix_out[l])
        x = _layernorm(DN_ALPHA * x + h, ln1_g[l], ln1_b[l])
        h = _cross_attention(x, mem, w_xq[l], w_xkv[l], w_xo[l])
        x = _layernorm(DN_ALPHA * x + h, ln2_g[l], ln2_b[l])
        h = _peer(x, w_pq[l], sub_keys[l], w_down[l], w_up[l])
        x = _layernorm(DN_ALPHA * x + h, ln3_g[l], ln3_b[l])
    return x


_drawn_inputs = setup_inputs


def setup_inputs(seed=0):
    import zlib

    import numpy as np

    out = dict(_drawn_inputs(seed))
    spreads = {}
    factors = {'sgu_g': 3.437, 'sgu_b': 3.823, 'b_spatial': 3.081, 'ln3_g': 2.823, 'ln3_b': 2.91}
    for name, (base, spread) in spreads.items():
        noise = np.random.default_rng([zlib.crc32(name.encode()), seed]).standard_normal(out[name].shape)
        drawn = base * np.exp(spread * noise) if base else spread * noise
        out[name] = __import__('jax').numpy.asarray(drawn.astype(out[name].dtype))
    for name, factor in factors.items():
        out[name] = (out[name] * factor).astype(out[name].dtype)
    return out
```

```python
import concourse.bass as bass
from concourse import mybir
from contextlib import ExitStack

F32 = mybir.dt.float32
F32R = mybir.dt.float32r
BF16 = mybir.dt.bfloat16
U32 = mybir.dt.uint32
ALU = mybir.AluOpType
ACT = mybir.ActivationFunctionType
AX = mybir.AxisListType

P = 128
D = 1024
S = 512
M = 256
KC = D // P
TB = S // P
MB = M // P
AH = 4
XH = 4
XD = D // XH
PH = 8
NK = 128
NS = 2 * PH
TOPK = 16
EPS = 1e-5
ALPHA = 2.0 ** 0.25
HALF = D // 2
NEG = -3.0e38

U_K, U_V, U_VA, U_CONV, U_UA, U_MIX, U_XQ, U_XO, FRONT_UNITS = 0, 8, 16, 20, 32, 36, 44, 52, 60
RING = 4


class Count:

    def __init__(self, sem):
        self.sem, self.n = sem, 0

    def up(self, ins):
        ins.then_inc(self.sem, 1)
        self.n += 1
        return self.n


def held(eng, sem, value, passed):
    eng.wait_ge(sem, value)
    eng.sem_inc(passed, 1)


def front_block(nc, t, units):
    xres, b_hi, b_lo, ps, ident = t["xres"], t["b_hi"], t["b_lo"], t["ps"], t["ident"]
    ctx = ExitStack()
    with ctx:
        def sb(name, shape, dt=F32):
            return ctx.enter_context(nc.sbuf_tensor(name, shape, dt))

        def sem(name):
            return ctx.enter_context(nc.semaphore(name))

        raw = sb("raw", [P, RING, D])
        w_hi = sb("w_hi", [P, RING, D], F32R)
        w_lo = sb("w_lo", [P, RING, D], F32R)
        xt_raw = sb("xt_raw", [P, KC, S])
        a_hi = sb("a_hi", [P, KC, S], F32R)
        a_lo = sb("a_lo", [P, KC, S], F32R)
        kt = sb("kt", [P, KC, M])
        v_hi = sb("v_hi", [P, MB, D], F32R)
        v_lo = sb("v_lo", [P, MB, D], F32R)
        tok = sb("tok", [P, TB, HALF])
        lng = sb("lng", [P, D])
        lnb = sb("lnb", [P, D])
        bias_va = sb("bias_va", [P, HALF])
        sgu_g = sb("sgu_g", [P, HALF])
        sgu_b = sb("sgu_b", [P, HALF])
        bsp = sb("bsp", [P, AH, P])
        bcol = sb("bcol", [P, 20])
        cw = sb("cw", [P, 3, 4])
        wst = sb("wst", [P, AH, P])
        zc = sb("zc", [P, S + 2])
        bst = sb("bst", [P, 16, 6])
        mv = sb("mv", [P, 16, 2])
        vc = sb("vc", [P, 16])
        sd = sb("sd", [P, 16])
        rc = sb("rc", [P, 16])
        nt = sb("nt", [P, 2, 16])
        mx = sb("mx", [P, TB, XH])
        nmx = sb("nmx", [P, TB, XH])
        sm = sb("sm", [P, TB, XH])
        rs = sb("rs", [P, TB, XH])

        k_tok = tok[:].rearrange("p a b -> p (a b)").rearrange("p (m d) -> p m d", m=MB)
        probs = k_tok.rearrange("p m (h j) -> p m h j", h=XH)
        u_t = xt_raw[:, 0:4, :]
        h_t, c_t = xt_raw[:, 4, :], xt_raw[:, 5, :]
        y_t = xt_raw[:, 6:8, :]
        q_t = xt_raw

        raw_full = [sem(f"raw_full{i}") for i in range(RING)]
        hi_done, split_done, unit_done = sem("hi_done"), sem("split_done"), sem("unit_done")
        mem_full, x_full, xres_full, par_full, ln1_full, ln2_full = (
            sem("mem_full"), sem("x_full"), sem("xres_full"), sem("par_full"), sem("ln1_full"), sem("ln2_full"))
        mem_hi, mem_split, x_hi, x_split = sem("mem_hi"), sem("mem_split"), sem("x_hi"), sem("x_split")
        ktok_done, ktr_done, kt_done = sem("ktok_done"), sem("ktr_done"), sem("kt_done")
        vhi_done, v_done = sem("vhi_done"), sem("v_done")
        ws_ready = sem("ws_ready")
        va_in, va_gelu, va_ready = sem("va_in"), sem("va_gelu"), sem("va_ready")
        z_read, y_made, yhi_done, y_split = sem("z_read"), sem("y_made"), sem("yhi_done"), sem("y_split")
        u_ready, mix_done, mix_read = sem("u_ready"), sem("mix_done"), sem("mix_read")
        var_ready, sd_ready = sem("var_ready"), sem("sd_ready")
        x1_ready, x1_tr, x1_hi, x1_split = sem("x1_ready"), sem("x1_tr"), sem("x1_hi"), sem("x1_split")
        q_ready, sc_done, mx_ready, exp_done, p_ready = (
            sem("q_ready"), sem("sc_done"), sem("mx_ready"), sem("exp_done"), sem("p_ready"))
        p_tr, p_hi, p_split = sem("p_tr"), sem("p_hi"), sem("p_split")
        o_done, o_hi, o_split = sem("o_done"), sem("o_hi"), sem("o_split")
        x2_ready, x2_tr, x2_hi, x2_split = sem("x2_ready"), sem("x2_tr"), sem("x2_hi"), sem("x2_split")
        dve_step, act_step, pool_step = sem("dve_step"), sem("act_step"), sem("pool_step")
        passed_pool = sem("passed_pool")
        block = ctx.enter_context(nc.Block())

        @block.sync
        def _(sp):
            sp.dma_start(kt[:], t["mem_t"]).then_inc(mem_full, 16)
            for u in range(RING):
                sp.dma_start(raw[:, u, :], units[u]).then_inc(raw_full[u], 16)
            sp.dma_start(xt_raw[:], t["x_t"]).then_inc(x_full, 16)
            with sp.Fori(1, FRONT_UNITS // RING) as r:
                for s in range(RING):
                    sp.wait_ge(split_done, RING * r + (s + 1 - RING))
                    sp.dma_start(raw[:, s, :], units[bass.ds(RING * r + s, 1)].rearrange("o p n -> (o p) n")
                                 ).then_inc(raw_full[s], 16)
            sp.wait_ge(x1_ready, TB)
            sp.dma_start(lng[:], t["ln2_g"].partition_broadcast(P)).then_inc(ln2_full, 16)
            sp.dma_start(lnb[:], t["ln2_b"].partition_broadcast(P)).then_inc(ln2_full, 16)
            sp.wait_ge(ln2_full, 32)

        @block.gpsimd
        def _(pool):
            pool.wait_ge(par_full, 16 * 8)
            nc.gpsimd.affine_select(out=wst[:], in_=wst[:], pattern=[[0, AH], [1, P]], compare_op=ALU.is_ge,
                                    fill=0.0, base=0, channel_multiplier=-1).then_inc(ws_ready, 1)

            def split(r, s, first):
                u = RING * r + s
                held(pool, raw_full[s], 16 * r + 16, passed_pool)
                if not first:
                    held(pool, unit_done, u - (RING - 1), passed_pool)
                nc.gpsimd.tensor_copy(w_hi[:, s, :], raw[:, s, :]).then_inc(hi_done, 1)
                held(pool, hi_done, u + 1, passed_pool)
                nc.gpsimd.tensor_tensor(w_lo[:, s, :], raw[:, s, :], w_hi[:, s, :].bitcast(F32),
                                        ALU.subtract).then_inc(split_done, 1)

            for s in range(RING):
                split(0, s, True)
            with pool.Fori(1, FRONT_UNITS // RING) as r:
                for s in range(RING):
                    split(r, s, False)

        @block.scalar
        def _(act):
            act.dma_start(bcol[:], t["bcol"]).then_inc(par_full, 16)
            act.dma_start(cw[:], t["cw"]).then_inc(par_full, 16)
            act.dma_start(wst[:], t["wst"]).then_inc(par_full, 16)
            act.dma_start(bias_va[:], t["bias_va"].partition_broadcast(P)).then_inc(par_full, 16)
            act.dma_start(sgu_g[:], t["sgu_g"].partition_broadcast(P)).then_inc(par_full, 16)
            act.dma_start(sgu_b[:], t["sgu_b"].partition_broadcast(P)).then_inc(par_full, 16)
            act.dma_start(bsp[:].rearrange("p h t -> p (h t)"), t["bsp"].partition_broadcast(P)).then_inc(par_full, 16)
            act.dma_start(ident[:], t["eye"]).then_inc(par_full, 16)
            act.dma_start(xres[:], t["x_tok"]).then_inc(xres_full, 16)
            act.dma_start(lng[:], t["ln1_g"].partition_broadcast(P)).then_inc(ln1_full, 16)
            act.dma_start(lnb[:], t["ln1_b"].partition_broadcast(P)).then_inc(ln1_full, 16)

            act.wait_ge(mem_full, 16)
            nc.scalar.activation(b_hi[:, :, 0:M], kt[:], ACT.Copy).then_inc(mem_hi, 1)
            act.wait_ge(x_full, 16)
            nc.scalar.activation(a_hi[:], xt_raw[:], ACT.Copy).then_inc(x_hi, 1)
            act.wait_ge(unit_done, U_V + KC)
            for m in range(MB):
                nc.scalar.activation(v_hi[:, m, :], ps[:, 4 + 2 * m:6 + 2 * m, :], ACT.Copy).then_inc(vhi_done, 1)
            for b in range(TB):
                act.wait_ge(va_in, b + 1)
                nc.scalar.activation(tok[:, b, :], tok[:, b, :], ACT.Gelu).then_inc(va_gelu, 1)
            act.wait_ge(var_ready, 1)
            nc.scalar.activation(sd[:], vc[:], ACT.Sqrt).then_inc(sd_ready, 1)
            for j in range(4):
                act.wait_ge(z_read, 3 * j + 3)
                nc.scalar.activation(b_hi[:, 4 + j, :], y_t[:, j % 2, :], ACT.Copy).then_inc(yhi_done, 1)
            for j in range(4):
                act.wait_ge(unit_done, U_UA + j + 1)
                nc.scalar.activation(u_t[:, j, :], ps[:, 4 + j, :], ACT.Gelu,
                                     bias=bcol[:, j:j + 1]).then_inc(u_ready, 1)
            for j in range(4):
                act.wait_ge(y_made, j + 1)
                nc.scalar.activation(b_hi[:, j, :], y_t[:, j % 2, :], ACT.Copy).then_inc(yhi_done, 1)
            act.wait_ge(var_ready, 2)
            nc.scalar.activation(sd[:, 0:TB], vc[:, 0:TB], ACT.Sqrt).then_inc(sd_ready, 1)
            for b in range(TB):
                act.wait_ge(x1_tr, b + 1)
                nc.scalar.activation(a_hi[:, :, b * P:(b + 1) * P],
                                     ps[:, 2 * b:2 * b + 2, :].rearrange("p a (c j) -> p (a c) j", j=P),
                                     ACT.Copy).then_inc(x1_hi, 1)
            for e in range(KC):
                act.wait_ge(unit_done, U_XQ + e + 1)
                nc.scalar.activation(q_t[:, e, :], ps[:, e, :], ACT.Copy).then_inc(q_ready, 1)

            def probs_high(b):
                act.wait_ge(p_tr, b + 1)
                nc.scalar.activation(b_hi[:, :, b * P:(b + 1) * P],
                                     ps[:, 4 + 2 * (b % 2):6 + 2 * (b % 2), :].rearrange("p a (c j) -> p (a c) j", j=P),
                                     ACT.Copy).then_inc(p_hi, 1)

            for b in range(TB):
                act.wait_ge(mx_ready, b + 1)
                if b >= 2:
                    act.wait_ge(p_tr, b - 1)
                for h in range(XH):
                    nc.scalar.activation(probs[:, b % 2, h, :],
                                         ps[:, 2 * (b % 2) + h // 2, (h % 2) * M:(h % 2 + 1) * M], ACT.Exp,
                                         bias=nmx[:, b, h:h + 1], scale=XD ** -0.5,
                                         accum_out=sm[:, b, h:h + 1]).then_inc(exp_done, 1)
                if b >= 1:
                    probs_high(b - 1)
            probs_high(TB - 1)
            for e in range(KC):
                act.wait_ge(o_done, e + 1)
                nc.scalar.activation(a_hi[:, e, :], ps[:, e, :], ACT.Copy).then_inc(o_hi, 1)
            act.wait_ge(var_ready, 3)
            nc.scalar.activation(sd[:, 0:TB], vc[:, 0:TB], ACT.Sqrt).then_inc(sd_ready, 1)
            for b in range(TB):
                act.wait_ge(x2_tr, b + 1)
                nc.scalar.activation(b_hi[:, :, b * P:(b + 1) * P],
                                     ps[:, 2 * b:2 * b + 2, :].rearrange("p a (c j) -> p (a c) j", j=P),
                                     ACT.Copy).then_inc(x2_hi, 1)

        @block.tensor
        def _(pe):
            def mm3(out, l_hi, l_lo, r_hi, r_lo, start, stop):
                nc.tensor.matmul(out, l_hi, r_hi, start=start, stop=False)
                nc.tensor.matmul(out, l_hi, r_lo, start=False, stop=False)
                return nc.tensor.matmul(out, l_lo, r_hi, start=False, stop=stop)

            def by_token(u0, n, banks, x_hi_, x_lo_, blocks, used=lambda: None):
                for k in range(n):
                    pe.wait_ge(split_done, u0 + k + 1)
                    s = (u0 + k) % RING
                    for b in range(blocks):
                        for h in range(2):
                            c, tk = slice(h * HALF, (h + 1) * HALF), slice(b * P, (b + 1) * P)
                            last = mm3(ps[:, banks + 2 * b + h, :], x_hi_[:, k, tk], x_lo_[:, k, tk],
                                       w_hi[:, s, c], w_lo[:, s, c], k == 0, k == n - 1)
                    last.then_inc(unit_done, 1)

            def by_channel(u, bank, x_hi_, x_lo_):
                pe.wait_ge(split_done, u + 1)
                s = u % RING
                for k in range(KC):
                    c = slice(k * P, (k + 1) * P)
                    last = mm3(ps[:, bank, :], w_hi[:, s, c], w_lo[:, s, c], x_hi_[:, k, :], x_lo_[:, k, :],
                               k == 0, k == KC - 1)
                last.then_inc(unit_done, 1)

            pe.wait_ge(mem_split, 1)
            by_token(U_K, KC, 0, b_hi, b_lo, MB)
            by_token(U_V, KC, 4, b_hi, b_lo, MB)
            pe.wait_ge(par_full, 16 * 8)
            pe.wait_ge(ktok_done, 4)
            for e in range(KC):
                for m in range(MB):
                    c = (e % 2) * M + m * P
                    last = nc.tensor.transpose(ps[:, e // 2, c:c + P], k_tok[:, m, e * P:(e + 1) * P], ident[:])
                if e % 2:
                    last.then_inc(ktr_done, 1)
            pe.wait_ge(x_split, 1)
            pe.wait_ge(kt_done, 4)
            for u in range(4):
                pe.wait_ge(split_done, U_VA + u + 1)
                s = (U_VA + u) % RING
                for i in range(2):
                    k = 2 * u + i
                    c = slice(i * HALF, (i + 1) * HALF)
                    for b in range(TB):
                        tk = slice(b * P, (b + 1) * P)
                        last = mm3(ps[:, b, :], a_hi[:, k, tk], a_lo[:, k, tk], w_hi[:, s, c], w_lo[:, s, c],
                                   k == 0, k == KC - 1)
                last.then_inc(unit_done, 1)
            pe.wait_ge(v_done, MB)
            for u in range(12):
                if u >= 4:
                    pe.wait_ge(z_read, u - 3)
                by_channel(U_CONV + u, 4 + u % 4, a_hi, a_lo)
            pe.wait_ge(ws_ready, 1)
            pe.wait_ge(va_ready, 1)
            for h in range(AH):
                for b in range(TB):
                    last = nc.tensor.matmul(ps[:, h, b * P:(b + 1) * P], tok[:, b, h * P:(h + 1) * P], wst[:, h, :],
                                            start=b == 0, stop=b == TB - 1, skip_group_check=True)
                last.then_inc(mix_done, 1)
            for u in range(4):
                pe.wait_ge(z_read, 8 + u + 1)
                by_channel(U_UA + u, 4 + u, a_hi, a_lo)
            pe.wait_ge(mix_read, 4)
            pe.wait_ge(u_ready, 4)
            pe.wait_ge(y_split, 8)
            by_token(U_MIX, KC, 0, b_hi, b_lo, TB)
            for b in range(TB):
                pe.wait_ge(x1_ready, b + 1)
                for e in range(KC):
                    last = nc.tensor.transpose(ps[:, 2 * b + e // 4, (e % 4) * P:(e % 4 + 1) * P],
                                               xres[:, b, e * P:(e + 1) * P], ident[:])
                last.then_inc(x1_tr, 1)
            pe.wait_ge(x1_split, TB)
            for e in range(KC):
                by_channel(U_XQ + e, e, a_hi, a_lo)

            def scores(b):
                if b >= 2:
                    pe.wait_ge(exp_done, XH * (b - 1))
                for h in range(XH):
                    for c in range(2):
                        last = nc.tensor.matmul(ps[:, 2 * (b % 2) + h // 2, (h % 2) * M:(h % 2 + 1) * M],
                                                q_t[:, 2 * h + c, b * P:(b + 1) * P], kt[:, 2 * h + c, :],
                                                start=c == 0, stop=c == 1)
                last.then_inc(sc_done, 1)

            def turn_probs(b):
                pe.wait_ge(p_ready, b + 1)
                if b >= 2:
                    pe.wait_ge(p_split, b - 1)
                for h in range(XH):
                    for m in range(MB):
                        i = MB * h + m
                        last = nc.tensor.transpose(ps[:, 4 + 2 * (b % 2) + i // 4, (i % 4) * P:(i % 4 + 1) * P],
                                                   probs[:, b % 2, h, m * P:(m + 1) * P], ident[:])
                last.then_inc(p_tr, 1)

            pe.wait_ge(q_ready, KC)
            scores(0)
            for b in range(1, TB):
                scores(b)
                turn_probs(b - 1)
            turn_probs(TB - 1)
            pe.wait_ge(p_split, TB)
            for e in range(KC):
                for m in range(MB):
                    i = MB * (e // 2) + m
                    c = slice(e * P, (e + 1) * P)
                    last = mm3(ps[:, e, :], v_hi[:, m, c], v_lo[:, m, c], b_hi[:, i, :], b_lo[:, i, :],
                               m == 0, m == MB - 1)
                last.then_inc(o_done, 1)
            pe.wait_ge(o_split, KC)
            by_token(U_XO, KC, 0, a_hi, a_lo, TB)
            for b in range(TB):
                pe.wait_ge(x2_ready, b + 1)
                for e in range(KC):
                    last = nc.tensor.transpose(ps[:, 2 * b + e // 4, (e % 4) * P:(e % 4 + 1) * P],
                                               xres[:, b, e * P:(e + 1) * P], ident[:])
                last.then_inc(x2_tr, 1)

        @block.vector
        def _(dve):
            step = Count(dve_step)

            def done():
                dve.wait_ge(dve_step, step.n)

            def inv_std(n, turn):
                done()
                nc.vector.tensor_scalar(vc[:, 0:n], mv[:, 0:n, 1], EPS, None, ALU.add).then_inc(var_ready, 1)
                dve.wait_ge(sd_ready, turn)
                step.up(nc.vector.reciprocal(rc[:, 0:n], sd[:, 0:n]))
                done()
                step.up(nc.vector.tensor_tensor(nt[:, 0, 0:n], rc[:, 0:n], rc[:, 0:n], ALU.mult))
                done()
                step.up(nc.vector.tensor_tensor(nt[:, 1, 0:n], nt[:, 0, 0:n], vc[:, 0:n], ALU.mult))
                done()
                step.up(nc.vector.tensor_scalar(nt[:, 0, 0:n], nt[:, 1, 0:n], -0.5, 1.5, ALU.mult, ALU.add))
                done()
                step.up(nc.vector.tensor_tensor(rc[:, 0:n], rc[:, 0:n], nt[:, 0, 0:n], ALU.mult))
                done()

            def layer_norm(u0, full, turn, ready):
                dve.wait_ge(unit_done, u0 + KC)
                for b in range(TB):
                    for h in range(2):
                        c = slice(h * HALF, (h + 1) * HALF)
                        step.up(nc.vector.scalar_tensor_tensor(out=xres[:, b, c], in0=xres[:, b, c], scalar=ALPHA,
                                                               in1=ps[:, 2 * b + h, :], op0=ALU.mult, op1=ALU.add))
                done()
                for b in range(TB):
                    for h in range(2):
                        step.up(nc.vector.bn_stats(bst[:, 2 * b + h, :], xres[:, b, h * HALF:(h + 1) * HALF]))
                done()
                for b in range(TB):
                    step.up(nc.vector.bn_aggr(mv[:, b, :], bst[:, 2 * b:2 * b + 2, :]))
                inv_std(TB, turn)
                dve.wait_ge(full, 32)
                for b in range(TB):
                    step.up(nc.vector.scalar_tensor_tensor(out=xres[:, b, :], in0=xres[:, b, :], scalar=mv[:, b, 0:1],
                                                           in1=lng[:], op0=ALU.subtract, op1=ALU.mult))
                    done()
                    nc.vector.scalar_tensor_tensor(out=xres[:, b, :], in0=xres[:, b, :], scalar=rc[:, b:b + 1],
                                                   in1=lnb[:], op0=ALU.mult, op1=ALU.add).then_inc(ready, 1)

            def low_part(lo_, hi_, src, sem_):
                nc.vector.tensor_tensor(lo_, src, hi_.bitcast(F32), ALU.subtract).then_inc(sem_, 1)

            dve.wait_ge(mem_hi, 1)
            low_part(b_lo[:, :, 0:M], b_hi[:, :, 0:M], kt[:], mem_split)
            dve.wait_ge(x_hi, 1)
            low_part(a_lo[:], a_hi[:], xt_raw[:], x_split)
            dve.wait_ge(unit_done, U_K + KC)
            for m in range(MB):
                for h in range(2):
                    nc.vector.tensor_copy(k_tok[:, m, h * HALF:(h + 1) * HALF], ps[:, 2 * m + h, :]
                                          ).then_inc(ktok_done, 1)
            for m in range(MB):
                dve.wait_ge(vhi_done, m + 1)
                low_part(v_lo[:, m, :].rearrange("p (a n) -> p a n", a=2), v_hi[:, m, :].rearrange("p (a n) -> p a n", a=2),
                         ps[:, 4 + 2 * m:6 + 2 * m, :], v_done)
            dve.wait_ge(mem_split, 1)
            for i in range(4):
                dve.wait_ge(ktr_done, i + 1)
                nc.vector.tensor_copy(kt[:, 2 * i:2 * i + 2, :], ps[:, i, :].rearrange("p (a n) -> p a n", a=2)
                                      ).then_inc(kt_done, 1)
            dve.wait_ge(par_full, 16 * 8)
            dve.wait_ge(unit_done, U_VA + 4)
            for b in range(TB):
                nc.vector.tensor_tensor(tok[:, b, :], ps[:, b, :], bias_va[:], ALU.add).then_inc(va_in, 1)
            for b in range(TB):
                dve.wait_ge(va_gelu, b + 1)
                for h in range(AH):
                    step.up(nc.vector.bn_stats(bst[:, AH * b + h, :], tok[:, b, h * P:(h + 1) * P]))
            done()
            for i in range(16):
                step.up(nc.vector.bn_aggr(mv[:, i, :], bst[:, i, :]))
            inv_std(16, 1)
            for b in range(TB):
                for h in range(AH):
                    i = AH * b + h
                    c = slice(h * P, (h + 1) * P)
                    step.up(nc.vector.tensor_scalar(tok[:, b, c], tok[:, b, c], mv[:, i, 0:1], rc[:, i:i + 1],
                                                    ALU.subtract, ALU.mult))
            done()
            step.up(nc.vector.tensor_tensor(tok[:], tok[:], sgu_g[:].unsqueeze(1).broadcast_to([P, TB, HALF]), ALU.mult))
            done()
            nc.vector.tensor_tensor(tok[:], tok[:], sgu_b[:].unsqueeze(1).broadcast_to([P, TB, HALF]),
                                    ALU.add).then_inc(va_ready, 1)
            step.up(nc.vector.memset(zc[:, 0:2], 0.0))
            dve.wait_ge(x_split, 1)

            def y_low(n):
                dve.wait_ge(yhi_done, n + 1)
                low_part(b_lo[:, (4 + n) % 8, :], b_hi[:, (4 + n) % 8, :], y_t[:, n % 2, :], y_split)

            for j in range(4):
                dve.wait_ge(unit_done, U_CONV + 3 * j + 1)
                if j:
                    dve.wait_ge(z_read, 3 * j)
                nc.vector.tensor_scalar(h_t, ps[:, 4 + 3 * j % 4, :], bcol[:, 8 + j:9 + j], None,
                                        ALU.add).then_inc(z_read, 1)
                dve.wait_ge(z_read, 3 * j + 1)
                dve.wait_ge(unit_done, U_CONV + 3 * j + 2)
                nc.vector.scalar_tensor_tensor(out=zc[:, 2:], in0=ps[:, 4 + (3 * j + 1) % 4, :],
                                               scalar=bcol[:, 16 + j:17 + j], in1=h_t,
                                               op0=ALU.add, op1=ALU.mult).then_inc(z_read, 1)
                dve.wait_ge(z_read, 3 * j + 2)
                done()
                step.up(nc.vector.tensor_scalar(c_t, zc[:, 0:S], cw[:, 0, j:j + 1], None, ALU.mult))
                for k in (1, 2):
                    done()
                    step.up(nc.vector.scalar_tensor_tensor(out=c_t, in0=zc[:, k:k + S], scalar=cw[:, k, j:j + 1],
                                                           in1=c_t, op0=ALU.mult, op1=ALU.add))
                done()
                if j >= 2:
                    dve.wait_ge(y_split, j - 1)
                dve.wait_ge(unit_done, U_CONV + 3 * j + 3)
                nc.vector.scalar_tensor_tensor(out=y_t[:, j % 2, :], in0=ps[:, 4 + (3 * j + 2) % 4, :],
                                               scalar=bcol[:, 12 + j:13 + j], in1=c_t,
                                               op0=ALU.add, op1=ALU.mult).then_inc(z_read, 1)
                dve.wait_ge(z_read, 3 * j + 3)
                if j:
                    y_low(j - 1)
            y_low(3)
            for h in range(AH):
                dve.wait_ge(mix_done, h + 1)
                nc.vector.tensor_tensor(c_t.rearrange("p (b j) -> p b j", b=TB),
                                        ps[:, h, :].rearrange("p (b j) -> p b j", b=TB),
                                        bsp[:, h, :].unsqueeze(1).broadcast_to([P, TB, P]), ALU.add).then_inc(mix_read, 1)
                dve.wait_ge(mix_read, h + 1)
                dve.wait_ge(u_ready, h + 1)
                dve.wait_ge(y_split, 4 + h - 1)
                nc.vector.tensor_tensor(y_t[:, h % 2, :], u_t[:, h, :], c_t, ALU.mult).then_inc(y_made, 1)
                dve.wait_ge(y_made, h + 1)
                if h:
                    y_low(4 + h - 1)
            y_low(7)
            dve.wait_ge(xres_full, 16)
            layer_norm(U_MIX, ln1_full, 2, x1_ready)
            for b in range(TB):
                dve.wait_ge(x1_hi, b + 1)
                tk = slice(b * P, (b + 1) * P)
                low_part(a_lo[:, :, tk], a_hi[:, :, tk],
                         ps[:, 2 * b:2 * b + 2, :].rearrange("p a (c j) -> p (a c) j", j=P), x1_split)

            def probs_low(b):
                dve.wait_ge(p_hi, b + 1)
                tk = slice(b * P, (b + 1) * P)
                low_part(b_lo[:, :, tk], b_hi[:, :, tk],
                         ps[:, 4 + 2 * (b % 2):6 + 2 * (b % 2), :].rearrange("p a (c j) -> p (a c) j", j=P), p_split)

            def row_max(b):
                dve.wait_ge(sc_done, b + 1)
                step.up(nc.vector.tensor_reduce(mx[:, b, :],
                                                ps[:, 2 * (b % 2):2 * (b % 2) + 2, :].rearrange("p a (c j) -> p (a c) j", j=M),
                                                AX.X, ALU.max))
                done()
                nc.vector.tensor_scalar(nmx[:, b, :], mx[:, b, :], -(XD ** -0.5), None, ALU.mult).then_inc(mx_ready, 1)

            row_max(0)
            for b in range(TB):
                if b + 1 < TB:
                    row_max(b + 1)
                dve.wait_ge(exp_done, XH * (b + 1))
                step.up(nc.vector.reciprocal(rs[:, b, :], sm[:, b, :]))
                done()
                for h in range(XH):
                    nc.vector.tensor_scalar(probs[:, b % 2, h, :], probs[:, b % 2, h, :], rs[:, b, h:h + 1], None,
                                            ALU.mult).then_inc(*((p_ready, 1) if h == XH - 1 else (dve_step, 1)))
                    step.n += h < XH - 1
                if b >= 1:
                    probs_low(b - 1)
            probs_low(TB - 1)
            for e in range(KC):
                dve.wait_ge(o_hi, e + 1)
                low_part(a_lo[:, e, :], a_hi[:, e, :], ps[:, e, :], o_split)
            layer_norm(U_XO, ln2_full, 3, x2_ready)
            for b in range(TB):
                dve.wait_ge(x2_hi, b + 1)
                tk = slice(b * P, (b + 1) * P)
                low_part(b_lo[:, :, tk], b_hi[:, :, tk],
                         ps[:, 2 * b:2 * b + 2, :].rearrange("p a (c j) -> p (a c) j", j=P), x2_split)


def topk_program(nc, dve, step, done, k, block_scores, exp_in, exp_out_sem, turn):
    w0, w1, v16, i16, i16f, top, flat = k["w0"], k["w1"], k["v16"], k["i16"], k["i16f"], k["top"], k["flat"]
    fi, fif, pick, ab = k["fi"], k["fif"], k["pick"], k["ab"]
    step(nc.vector.tensor_copy(w0[:], block_scores))
    done()
    for e in range(NS):
        step(nc.vector.max(v16[:, e, 0:8], w0[:, e, :]))
    done()
    for e in range(NS):
        step(nc.vector.max_index(i16[:, e, 0:8], v16[:, e, 0:8], w0[:, e, :]))
        step(nc.vector.match_replace(w1[:, e, :], v16[:, e, 0:8], w0[:, e, :], NEG))
    done()
    for e in range(NS):
        step(nc.vector.max(v16[:, e, 8:16], w1[:, e, :]))
    done()
    for e in range(NS):
        step(nc.vector.max_index(i16[:, e, 8:16], v16[:, e, 8:16], w1[:, e, :]))
    done()
    vs = v16[:].rearrange("p (h s) i -> p h s i", s=2)
    c0 = w0[:].rearrange("p (h s) n -> p h (s n)", s=2)
    c1 = w1[:].rearrange("p (h s) n -> p h (s n)", s=2)
    shape = [P, PH, TOPK, TOPK]
    step(nc.vector.tensor_tensor(c0.rearrange("p h (i j) -> p h i j", i=TOPK),
                                 vs[:, :, 0, :].unsqueeze(3).broadcast_to(shape),
                                 vs[:, :, 1, :].unsqueeze(2).broadcast_to(shape), ALU.add))
    done()
    for h in range(PH):
        step(nc.vector.max(top[:, h, 0:8], c0[:, h, :]))
    done()
    for h in range(PH):
        step(nc.vector.max_index(flat[:, h, 0:8], top[:, h, 0:8], c0[:, h, :]))
        step(nc.vector.match_replace(c1[:, h, :], top[:, h, 0:8], c0[:, h, :], NEG))
    done()
    for h in range(PH):
        step(nc.vector.max(top[:, h, 8:16], c1[:, h, :]))
    done()
    nc.vector.tensor_tensor(k["ex"][:], top[:], top[:, :, 0:1].broadcast_to([P, PH, TOPK]),
                            ALU.subtract).then_inc(exp_in, 1)
    for h in range(PH):
        step(nc.vector.max_index(flat[:, h, 8:16], top[:, h, 8:16], c1[:, h, :]))
    step(nc.vector.tensor_copy(i16f[:], i16[:]))
    done()
    step(nc.vector.tensor_single_scalar(fi[:, 0], flat[:], 4, ALU.logical_shift_right))
    step(nc.vector.tensor_single_scalar(fi[:, 1], flat[:], TOPK - 1, ALU.bitwise_and))
    done()
    step(nc.vector.tensor_copy(fif[:], fi[:]))
    done()
    isd = i16f[:].rearrange("p (h s) i -> p h s i", s=2)
    pk = pick[:].rearrange("p (h k i) -> p h k i", h=PH, k=TOPK)
    for side in range(2):
        step(nc.vector.tensor_tensor(pk, fif[:, side].unsqueeze(3).broadcast_to(shape),
                                     k["iota16"][:].unsqueeze(1).unsqueeze(1).broadcast_to(shape), ALU.is_equal))
        done()
        step(nc.vector.tensor_tensor(pk, pk, isd[:, :, side, :].unsqueeze(2).broadcast_to(shape), ALU.mult))
        done()
        step(nc.vector.tensor_reduce(ab[:, side], pk, AX.X, ALU.add))
        done()
    held(dve, exp_out_sem, turn, k['passed'])
    step(nc.vector.tensor_reduce(k["gsum"][:], k["ex"][:], AX.X, ALU.add))
    done()
    step(nc.vector.reciprocal(k["gsum"][:], k["gsum"][:]))
    done()


def scores_block(nc, t, units):
    sc, b_hi, b_lo, ps = t["sc"], t["b_hi"], t["b_lo"], t["ps"]
    ctx = ExitStack()
    with ctx:
        def sb(name, shape, dt=F32):
            return ctx.enter_context(nc.sbuf_tensor(name, shape, dt))

        def sem(name):
            return ctx.enter_context(nc.semaphore(name))

        raw = sb("raw2", [P, RING, D])
        w_hi = sb("w_hi2", [P, RING, D], F32R)
        w_lo = sb("w_lo2", [P, RING, D], F32R)
        skt = sb("skt", [P, NS, NK])
        qs = sb("qs", [P, RING, S])
        raw_full = [sem(f"raw2_full{i}") for i in range(RING)]
        skt_full = sem("skt_full")
        hi_done, split_done, unit_done = sem("hi2_done"), sem("split2_done"), sem("unit2_done")
        qs_ready, ss_done, sc_ready = sem("qs_ready"), sem("ss_done"), sem("sc_ready")
        passed_pool = sem("passed_pool2")
        rounds = NS // RING
        block = ctx.enter_context(nc.Block())

        @block.sync
        def _(sp):
            for u in range(RING):
                sp.dma_start(raw[:, u, :], units[u]).then_inc(raw_full[u], 16)
            sp.dma_start(skt[:], t["skt"]).then_inc(skt_full, 16)
            with sp.Fori(1, rounds) as r:
                for s in range(RING):
                    sp.wait_ge(split_done, RING * r + (s + 1 - RING))
                    sp.dma_start(raw[:, s, :], units[bass.ds(RING * r + s, 1)].rearrange("o p n -> (o p) n")
                                 ).then_inc(raw_full[s], 16)

        @block.gpsimd
        def _(pool):
            def split(r, s, first):
                u = RING * r + s
                held(pool, raw_full[s], 16 * r + 16, passed_pool)
                if not first:
                    held(pool, unit_done, u - (RING - 1), passed_pool)
                nc.gpsimd.tensor_copy(w_hi[:, s, :], raw[:, s, :]).then_inc(hi_done, 1)
                held(pool, hi_done, u + 1, passed_pool)
                nc.gpsimd.tensor_tensor(w_lo[:, s, :], raw[:, s, :], w_hi[:, s, :].bitcast(F32),
                                        ALU.subtract).then_inc(split_done, 1)

            for s in range(RING):
                split(0, s, True)
            with pool.Fori(1, rounds) as r:
                for s in range(RING):
                    split(r, s, False)

        @block.tensor
        def _(pe):
            def queries(r, s):
                u = RING * r + s
                pe.wait_ge(split_done, u + 1)
                for k in range(KC):
                    c = slice(k * P, (k + 1) * P)
                    nc.tensor.matmul(ps[:, s, :], w_hi[:, s, c], b_hi[:, k, :], start=k == 0, stop=False)
                    nc.tensor.matmul(ps[:, s, :], w_hi[:, s, c], b_lo[:, k, :], start=False, stop=False)
                    last = nc.tensor.matmul(ps[:, s, :], w_lo[:, s, c], b_hi[:, k, :], start=False, stop=k == KC - 1)
                last.then_inc(unit_done, 1)

            def scores(r, s, first=False):
                u = RING * r + s
                pe.wait_ge(qs_ready, u + 1)
                if not first:
                    pe.wait_ge(sc_ready, u - (RING - 1))
                for b in range(TB):
                    last = nc.tensor.matmul(ps[:, 4 + s, b * P:(b + 1) * P], qs[:, s, b * P:(b + 1) * P],
                                            skt[:, bass.ds(u, 1), :].rearrange("p o n -> p (o n)"),
                                            start=True, stop=True, skip_group_check=True)
                last.then_inc(ss_done, 1)

            pe.wait_ge(skt_full, 16)
            queries(0, 0)
            for s in range(1, RING):
                queries(0, s)
                scores(0, s - 1, first=True)
            queries(1, 0)
            scores(0, RING - 1, first=True)
            for s in range(1, RING):
                queries(1, s)
                scores(1, s - 1)
            with pe.Fori(2, rounds) as r:
                for s in range(RING):
                    queries(r, s)
                    scores(r if s else r - 1, (s - 1) % RING)
            scores(rounds - 1, RING - 1)

        @block.scalar
        def _(act):
            def queries_out(r, s, first):
                u = RING * r + s
                act.wait_ge(unit_done, u + 1)
                if not first:
                    act.wait_ge(ss_done, u - (RING - 1))
                nc.scalar.activation(qs[:, s, :], ps[:, s, :], ACT.Copy).then_inc(qs_ready, 1)

            for s in range(RING):
                queries_out(0, s, True)
            with act.Fori(1, rounds) as r:
                for s in range(RING):
                    queries_out(r, s, False)

        @block.vector
        def _(dve):
            with dve.Fori(0, rounds) as r:
                for s in range(RING):
                    dve.wait_ge(ss_done, RING * r + (s + 1))
                    nc.vector.tensor_copy(sc[:, :, bass.ds(RING * r + s, 1), :].rearrange("p b o n -> p b (o n)"),
                                          ps[:, 4 + s, :].rearrange("p (b n) -> p b n", b=TB)).then_inc(sc_ready, 1)


def experts_block(nc, t, w_down, w_up, out):
    xres, sc = t["xres"], t["sc"]
    GS = 8
    HK = PH * TOPK
    ctx = ExitStack()
    with ctx:
        def sb(name, shape, dt=F32):
            return ctx.enter_context(nc.sbuf_tensor(name, shape, dt))

        def sem(name):
            return ctx.enter_context(nc.semaphore(name))

        k = {"w0": sb("w0", [P, NS, NK]), "w1": sb("w1", [P, NS, NK]), "v16": sb("v16", [P, NS, TOPK]),
             "i16": sb("i16", [P, NS, TOPK], U32), "i16f": sb("i16f", [P, NS, TOPK]), "top": sb("top", [P, PH, TOPK]),
             "flat": sb("flat", [P, PH, TOPK], U32), "fi": sb("fi", [P, 2, PH, TOPK], U32),
             "fif": sb("fif", [P, 2, PH, TOPK]), "pick": sb("pick", [P, 2048]), "ab": sb("ab", [P, 2, PH, TOPK]),
             "ex": sb("ex", [P, PH, TOPK]), "gsum": sb("gsum", [P, PH]), "iota16": sb("iota16", [P, TOPK])}
        k["passed"] = passed_dve = sem("passed_dve3")
        ef = sb("ef", [P, HK])
        expert = sb("expert", [P, HK], U32)
        gate = sb("gate", [P, PH, TOPK])
        rows = sb("rows", [P, GS, D])
        idx = sb("idx", [P, 2, GS], U32)
        xb = sb("xb", [P, D])
        acc = sb("acc", [P, 2, D])
        dn8 = sb("dn8", [P, GS])
        dn = sb("dn", [P, HK])
        coef = sb("coef", [P, HK])
        lng, lnb = sb("ln3g", [P, D]), sb("ln3b", [P, D])
        bst, mv, vc, sd = sb("bst3", [P, 2, 6]), sb("mv3", [P, 2]), sb("vc3", [P, 1]), sb("sd3", [P, 1])
        rc, nt = sb("rc3", [P, 1]), sb("nt3", [P, 2, 1])
        res = sb("res", [P, D])
        iota_full, ln_full = sem("iota_full"), sem("ln3_full")
        row_full = [sem(f"row_full{i}") for i in range(GS)]
        row_free, idx_ready = sem("row_free"), sem("idx_ready")
        exp_in, exp_out, experts_ready = sem("exp_in"), sem("exp_out"), sem("experts_ready")
        dn_ready, gelu_done, var_ready, sd_ready = sem("dn_ready"), sem("gelu_done"), sem("var3_ready"), sem("sd3_ready")
        res_ready, out_done, dve_step = sem("res_ready"), sem("out_done"), sem("dve3_step")
        passed_pool = sem("passed_pool3")
        block = ctx.enter_context(nc.Block())

        @block.sync
        def _(sp):
            sp.dma_start(k["iota16"][:], t["iota16"].partition_broadcast(P)).then_inc(iota_full, 16)
            sp.dma_start(lng[:], t["ln3_g"].partition_broadcast(P)).then_inc(ln_full, 16)
            sp.dma_start(lnb[:], t["ln3_b"].partition_broadcast(P)).then_inc(ln_full, 16)
            with sp.Fori(0, TB) as b:
                sp.wait_ge(res_ready, b + 1)
                sp.dma_start(out[0, bass.ds(b * P, P), :], res[:]).then_inc(out_done, 16)
            sp.wait_ge(out_done, 16 * TB)

        @block.gpsimd
        def _(pool):
            with pool.Fori(0, TB) as b:
                held(pool, experts_ready, b + 1, passed_pool)
                for phase, table in enumerate((w_down, w_up)):
                    with pool.Fori(0, HK // GS // 2) as r:
                        for p in range(2):
                            n = (2 * b + phase) * (HK // GS) + (2 * r + p)
                            held(pool, row_free, GS * n + 1, passed_pool)
                            nc.gpsimd.tensor_copy(idx[:, p, :], expert[:, bass.ds(GS * (2 * r + p), GS)]
                                                  ).then_inc(idx_ready, 1)
                            held(pool, idx_ready, n + 1, passed_pool)
                            for j in range(GS):
                                held(pool, row_free, GS * n + (j + 1), passed_pool)
                                nc.gpsimd.indirect_dma_start(rows[:, j, :], None, table,
                                                             bass.IndirectOffsetOnAxis(ap=idx[:, p, j:j + 1], axis=0)
                                                             ).then_inc(row_full[j], 16)

        @block.scalar
        def _(act):
            with act.Fori(0, TB) as b:
                act.wait_ge(exp_in, b + 1)
                nc.scalar.activation(k["ex"][:], k["ex"][:], ACT.Exp).then_inc(exp_out, 1)
                act.wait_ge(dn_ready, b + 1)
                nc.scalar.activation(coef[:], dn[:], ACT.Gelu).then_inc(gelu_done, 1)
                act.wait_ge(var_ready, b + 1)
                nc.scalar.activation(sd[:], vc[:], ACT.Sqrt).then_inc(sd_ready, 1)

        @block.vector
        def _(dve):
            dve.wait_ge(iota_full, 16)
            dve.wait_ge(ln_full, 32)
            nc.vector.memset(dn8[:], 0.0).then_inc(row_free, GS)
            n_steps = [0]

            def step(ins):
                ins.then_inc(dve_step, 1)
                n_steps[0] += 1

            def done():
                dve.wait_ge(dve_step, n_steps[0])

            with dve.Fori(0, TB) as b:
                dve.sem_clear(dve_step)
                topk_program(nc, dve, step, done, k, sc[:, bass.ds(b, 1)].rearrange("p o s n -> p (o s) n"),
                             exp_in, exp_out, b + 1)
                step(nc.vector.tensor_tensor(gate[:], k["ex"][:], k["gsum"][:].unsqueeze(2).broadcast_to([P, PH, TOPK]),
                                             ALU.mult))
                ab = k["ab"][:].rearrange("p s h k -> p s (h k)")
                step(nc.vector.scalar_tensor_tensor(out=ef[:], in0=ab[:, 0], scalar=float(NK), in1=ab[:, 1],
                                                    op0=ALU.mult, op1=ALU.add))
                done()
                nc.vector.tensor_copy(expert[:], ef[:]).then_inc(experts_ready, 1)
                step(nc.vector.tensor_copy(xb[:], xres[:, bass.ds(b, 1), :].rearrange("p o n -> p (o n)")))
                step(nc.vector.memset(acc[:, 1, :], 0.0))
                step(nc.vector.tensor_scalar(acc[:, 0, :], xres[:, bass.ds(b, 1), :].rearrange("p o n -> p (o n)"),
                                             ALPHA, None, ALU.mult))
                done()
                with dve.Fori(0, HK // GS) as r:
                    n = 2 * b * (HK // GS) + r
                    for j in range(GS):
                        held(dve, row_full[j], 16 * n + 16, passed_dve)
                        nc.vector.scalar_tensor_tensor(out=rows[:, j, :], in0=rows[:, j, :], scalar=1.0, in1=xb[:],
                                                       op0=ALU.mult, op1=ALU.mult,
                                                       accum_out=dn[:, bass.ds(GS * r + j, 1)]).then_inc(row_free, 1)
                held(dve, row_free, GS * (2 * b + 1) * (HK // GS) + GS, passed_dve)
                dve.sem_inc(dn_ready, 1)
                held(dve, gelu_done, b + 1, passed_dve)
                step(nc.vector.tensor_tensor(coef[:], coef[:], gate[:].rearrange("p h k -> p (h k)"), ALU.mult))
                done()
                with dve.Fori(0, HK // GS) as r:
                    n = (2 * b + 1) * (HK // GS) + r
                    for j in range(GS):
                        held(dve, row_full[j], 16 * n + 16, passed_dve)
                        held(dve, row_free, GS * n + (j + GS - 1), passed_dve)
                        nc.vector.scalar_tensor_tensor(out=acc[:, j % 2, :], in0=rows[:, j, :],
                                                       scalar=coef[:, bass.ds(GS * r + j, 1)], in1=acc[:, j % 2, :],
                                                       op0=ALU.mult, op1=ALU.add).then_inc(row_free, 1)
                held(dve, row_free, GS * (2 * b + 2) * (HK // GS) + GS, passed_dve)
                step(nc.vector.tensor_tensor(acc[:, 0, :], acc[:, 0, :], acc[:, 1, :], ALU.add))
                done()
                for h in range(2):
                    step(nc.vector.bn_stats(bst[:, h, :], acc[:, 0, h * HALF:(h + 1) * HALF]))
                done()
                step(nc.vector.bn_aggr(mv[:], bst[:]))
                done()
                nc.vector.tensor_scalar(vc[:], mv[:, 1:2], EPS, None, ALU.add).then_inc(var_ready, 1)
                held(dve, sd_ready, b + 1, passed_dve)
                step(nc.vector.reciprocal(rc[:], sd[:]))
                done()
                step(nc.vector.tensor_tensor(nt[:, 0], rc[:], rc[:], ALU.mult))
                done()
                step(nc.vector.tensor_tensor(nt[:, 1], nt[:, 0], vc[:], ALU.mult))
                done()
                step(nc.vector.tensor_scalar(nt[:, 0], nt[:, 1], -0.5, 1.5, ALU.mult, ALU.add))
                done()
                step(nc.vector.tensor_tensor(rc[:], rc[:], nt[:, 0], ALU.mult))
                step(nc.vector.scalar_tensor_tensor(out=acc[:, 0, :], in0=acc[:, 0, :], scalar=mv[:, 0:1], in1=lng[:],
                                                    op0=ALU.subtract, op1=ALU.mult))
                done()
                nc.vector.scalar_tensor_tensor(out=res[:], in0=acc[:, 0, :], scalar=rc[:], in1=lnb[:],
                                               op0=ALU.mult, op1=ALU.add).then_inc(res_ready, 1)
                held(dve, out_done, 16 * b + 16, passed_dve)
                held(dve, res_ready, b + 1, passed_dve)


def build(nc, ins, out):
    ctx = ExitStack()
    with ctx:
        def sb(name, shape, dt=F32):
            return ctx.enter_context(nc.sbuf_tensor(name, shape, dt))

        t = dict(ins)
        t["xres"] = sb("xres", [P, TB, D])
        t["ident"] = sb("ident", [P, P])
        t["ps"] = ctx.enter_context(nc.psum_tensor("ps", [P, 8, HALF], F32))
        t["b_hi"], t["b_lo"] = sb("b_hi", [P, KC, S], F32R), sb("b_lo", [P, KC, S], F32R)
        front_block(nc, t, ins["units"])
        t["sc"] = sb("sc", [P, TB, NS, NK])
        scores_block(nc, t, ins["units"][FRONT_UNITS:])
        experts_block(nc, t, ins["w_down"], ins["w_up"], out)


def layout(x, mem, w_in, b_in, sgu_g, sgu_b, w_spatial, b_spatial, conv_w, w_mix_out, ln1_g, ln1_b, w_xq, w_xkv,
           w_xo, ln2_g, ln2_b, w_pq, sub_keys, w_down, w_up, ln3_g, ln3_b):
    import numpy as np
    c = np.ascontiguousarray

    def by_rows(w):
        return w.reshape(-1, P, D)

    def by_columns(w):
        return w.reshape(KC, P, -1, P).transpose(2, 1, 0, 3).reshape(-1, P, D)

    w = w_in[0]
    a = D // 2
    va = w[:, a:2 * a].reshape(4, 2, P, a).transpose(0, 2, 1, 3).reshape(4, P, D)
    h, gb, gc = (by_columns(w[:, 2 * a + i * a:2 * a + (i + 1) * a]) for i in range(3))
    conv = np.stack([h, gc, gb], 1).reshape(12, P, D)
    units = np.concatenate([by_rows(w_xkv[0][:, :D]), by_rows(w_xkv[0][:, D:]), va, conv, by_columns(w[:, :a]),
                            by_rows(w_mix_out[0]), by_columns(w_xq[0]), by_rows(w_xo[0]), by_columns(w_pq[0])])
    return {
        "units": units,
        "mem_t": c(mem[0].T.reshape(KC, P, M).transpose(1, 0, 2)),
        "x_t": c(x[0].T.reshape(KC, P, S).transpose(1, 0, 2)),
        "x_tok": c(x[0].reshape(TB, P, D).transpose(1, 0, 2)),
        "bcol": c(b_in[0].reshape(20, P).T),
        "cw": c(conv_w[0][:, 0].reshape(3, 4, P).transpose(2, 0, 1)),
        "wst": c(w_spatial[0].transpose(2, 0, 1)),
        "bias_va": c(b_in[0][a:2 * a]),
        "sgu_g": sgu_g[0].reshape(-1), "sgu_b": sgu_b[0].reshape(-1), "bsp": b_spatial[0].reshape(-1),
        "skt": c(sub_keys[0].reshape(NS, NK, P).transpose(2, 0, 1)),
        "iota16": np.arange(TOPK, dtype=np.float32),
        "w_down": w_down[0], "w_up": w_up[0], "ln3_g": ln3_g[0], "ln3_b": ln3_b[0],
        "eye": np.eye(P, dtype=np.float32),
        "ln1_g": ln1_g[0], "ln1_b": ln1_b[0], "ln2_g": ln2_g[0], "ln2_b": ln2_b[0],
    }


def kernel(**inputs):
    import numpy as np
    import concourse.bacc as bacc
    from concourse.bass_utils import run_bass_kernel_spmd

    nc = bacc.Bacc("TRN2", target_bir_lowering=False, num_devices=1)
    arrays = {f"in_{k}": np.ascontiguousarray(v) for k, v in layout(**{k: np.asarray(v) for k, v in inputs.items()}).items()}
    ins = {k[3:]: nc.dram_tensor(k, v.shape, mybir.dt.from_np(v.dtype), kind="ExternalInput").ap()
           for k, v in arrays.items()}
    out = nc.dram_tensor("out", (1, S, D), F32, kind="ExternalOutput").ap()
    build(nc, ins, out)
    r = run_bass_kernel_spmd(nc, [arrays], core_ids=[0])
    return r.results[0]["out"]
```

```python
import concourse.bass as bass
from concourse import mybir
from contextlib import ExitStack

F32 = mybir.dt.float32
F32R = mybir.dt.float32r
BF16 = mybir.dt.bfloat16
F16 = mybir.dt.float16
U32 = mybir.dt.uint32
ALU = mybir.AluOpType
ACT = mybir.ActivationFunctionType
AX = mybir.AxisListType

P = 128
D = 1024
S = 512
M = 256
KC = D // P
TB = S // P
MB = M // P
AH = 4
XH = 4
XD = D // XH
PH = 8
NK = 128
NS = 2 * PH
TOPK = 16
EPS = 1e-5
ALPHA = 2.0 ** 0.25
HALF = D // 2
NEG = -3.0e38

U_K, U_V, U_VA, U_CONV, U_UA, U_MIX, U_XQ, U_XO, FRONT_UNITS = 0, 8, 16, 20, 32, 36, 44, 52, 60
RING = 4


class Count:

    def __init__(self, sem):
        self.sem, self.n = sem, 0

    def up(self, ins):
        ins.then_inc(self.sem, 1)
        self.n += 1
        return self.n


def held(eng, sem, value, passed):
    eng.wait_ge(sem, value)
    eng.sem_inc(passed, 1)


def front_block(nc, t, units):
    b_hi, b_lo, ps, ident = t["b_hi"], t["b_lo"], t["ps"], t["ident"]
    ctx = ExitStack()
    with ctx:
        def sb(name, shape, dt=F32):
            return ctx.enter_context(nc.sbuf_tensor(name, shape, dt))

        def sem(name):
            return ctx.enter_context(nc.semaphore(name))

        raw = sb("raw", [P, RING, D])
        w_hi = sb("w_hi", [P, RING, D], F32R)
        w_lo = sb("w_lo", [P, RING, D], F32R)
        xt_raw = sb("xt_raw", [P, KC, S])
        xres = sb("xres", [P, TB, D])
        a_hi = sb("a_hi", [P, KC, S], F32R)
        a_lo = sb("a_lo", [P, KC, S], F32R)
        kt = sb("kt", [P, KC, M])
        v_hi = sb("v_hi", [P, MB, D], F32R)
        v_lo = sb("v_lo", [P, MB, D], F32R)
        tok = sb("tok", [P, TB, HALF])
        lng = sb("lng", [P, D])
        lnb = sb("lnb", [P, D])
        bias_va = sb("bias_va", [P, HALF])
        sgu_g = sb("sgu_g", [P, HALF])
        sgu_b = sb("sgu_b", [P, HALF])
        bsp = sb("bsp", [P, AH, P])
        bcol = sb("bcol", [P, 20])
        cw = sb("cw", [P, 3, 4])
        wst = sb("wst", [P, AH, P])
        zc = sb("zc", [P, S + 2])
        bst = sb("bst", [P, 16, 6])
        mv = sb("mv", [P, 16, 2])
        vc = sb("vc", [P, 16])
        sd = sb("sd", [P, 16])
        rc = sb("rc", [P, 16])
        nt = sb("nt", [P, 2, 16])
        mx = sb("mx", [P, TB, XH])
        nmx = sb("nmx", [P, TB, XH])
        sm = sb("sm", [P, TB, XH])
        rs = sb("rs", [P, TB, XH])

        k_tok = tok[:].rearrange("p a b -> p (a b)").rearrange("p (m d) -> p m d", m=MB)
        probs = k_tok.rearrange("p m (h j) -> p m h j", h=XH)
        u_t = xt_raw[:, 0:4, :]
        h_t, c_t = xt_raw[:, 4, :], xt_raw[:, 5, :]
        y_t = xt_raw[:, 6:8, :]
        q_t = xt_raw

        raw_full = [sem(f"raw_full{i}") for i in range(RING)]
        hi_done, split_done, unit_done = sem("hi_done"), sem("split_done"), sem("unit_done")
        mem_full, x_full, xres_full, par_full, ln1_full, ln2_full = (
            sem("mem_full"), sem("x_full"), sem("xres_full"), sem("par_full"), sem("ln1_full"), sem("ln2_full"))
        mem_hi, mem_split, x_hi, x_split = sem("mem_hi"), sem("mem_split"), sem("x_hi"), sem("x_split")
        ktok_done, ktr_done, kt_done = sem("ktok_done"), sem("ktr_done"), sem("kt_done")
        vhi_done, v_done = sem("vhi_done"), sem("v_done")
        ws_ready = sem("ws_ready")
        va_in, va_gelu, va_ready = sem("va_in"), sem("va_gelu"), sem("va_ready")
        z_read, y_made, yhi_done, y_split = sem("z_read"), sem("y_made"), sem("yhi_done"), sem("y_split")
        u_ready, mix_done, mix_read = sem("u_ready"), sem("mix_done"), sem("mix_read")
        var_ready, sd_ready = sem("var_ready"), sem("sd_ready")
        x1_ready, x1_tr, x1_hi, x1_split = sem("x1_ready"), sem("x1_tr"), sem("x1_hi"), sem("x1_split")
        q_ready, sc_done, mx_ready, exp_done, p_ready = (
            sem("q_ready"), sem("sc_done"), sem("mx_ready"), sem("exp_done"), sem("p_ready"))
        p_tr, p_hi, p_split = sem("p_tr"), sem("p_hi"), sem("p_split")
        o_done, o_hi, o_split = sem("o_done"), sem("o_hi"), sem("o_split")
        x2_ready, x2_tr, x2_hi, x2_split = sem("x2_ready"), sem("x2_tr"), sem("x2_hi"), sem("x2_split")
        x2_stored, dve_step = sem("x2_stored"), sem("dve_step")
        passed_pool = sem("passed_pool")
        block = ctx.enter_context(nc.Block())

        @block.sync
        def _(sp):
            sp.dma_start(kt[:], t["mem_t"]).then_inc(mem_full, 16)
            for u in range(RING):
                sp.dma_start(raw[:, u, :], units[u]).then_inc(raw_full[u], 16)
            sp.dma_start(xt_raw[:], t["x_t"]).then_inc(x_full, 16)
            with sp.Fori(1, FRONT_UNITS // RING) as r:
                for s in range(RING):
                    sp.wait_ge(split_done, RING * r + (s + 1 - RING))
                    sp.dma_start(raw[:, s, :], units[bass.ds(RING * r + s, 1)].rearrange("o p n -> (o p) n")
                                 ).then_inc(raw_full[s], 16)
            sp.wait_ge(x1_ready, TB)
            sp.dma_start(lng[:], t["ln2_g"].partition_broadcast(P)).then_inc(ln2_full, 16)
            sp.dma_start(lnb[:], t["ln2_b"].partition_broadcast(P)).then_inc(ln2_full, 16)
            sp.wait_ge(x2_ready, TB)
            sp.dma_start(t["x2_d"].rearrange("b p d -> p b d"), xres[:]).then_inc(x2_stored, 16)
            sp.wait_ge(x2_stored, 16)

        @block.gpsimd
        def _(pool):
            pool.wait_ge(par_full, 16 * 8)
            nc.gpsimd.affine_select(out=wst[:], in_=wst[:], pattern=[[0, AH], [1, P]], compare_op=ALU.is_ge,
                                    fill=0.0, base=0, channel_multiplier=-1).then_inc(ws_ready, 1)

            def split_low(r, s):
                u = RING * r + s
                held(pool, hi_done, u + 1, passed_pool)
                nc.gpsimd.tensor_tensor(w_lo[:, s, :], raw[:, s, :], w_hi[:, s, :].bitcast(F32),
                                        ALU.subtract).then_inc(split_done, 1)

            with pool.Fori(0, FRONT_UNITS // RING) as r:
                for s in range(RING):
                    split_low(r, s)

        @block.scalar
        def _(act):
            act.dma_start(bcol[:], t["bcol"]).then_inc(par_full, 16)
            act.dma_start(cw[:], t["cw"]).then_inc(par_full, 16)
            act.dma_start(wst[:], t["wst"]).then_inc(par_full, 16)
            act.dma_start(bias_va[:], t["bias_va"].partition_broadcast(P)).then_inc(par_full, 16)
            act.dma_start(sgu_g[:], t["sgu_g"].partition_broadcast(P)).then_inc(par_full, 16)
            act.dma_start(sgu_b[:], t["sgu_b"].partition_broadcast(P)).then_inc(par_full, 16)
            act.dma_start(bsp[:].rearrange("p h t -> p (h t)"), t["bsp"].partition_broadcast(P)).then_inc(par_full, 16)
            act.dma_start(ident[:], t["eye"]).then_inc(par_full, 16)
            act.dma_start(xres[:], t["x_tok"]).then_inc(xres_full, 16)
            act.dma_start(lng[:], t["ln1_g"].partition_broadcast(P)).then_inc(ln1_full, 16)
            act.dma_start(lnb[:], t["ln1_b"].partition_broadcast(P)).then_inc(ln1_full, 16)

            highs = iter(range(FRONT_UNITS))

            def high_parts(until):
                for u in highs:
                    s = u % RING
                    act.wait_ge(raw_full[s], 16 * (u // RING) + 16)
                    if u >= RING:
                        act.wait_ge(unit_done, u - RING + 1)
                    nc.scalar.activation(w_hi[:, s, :], raw[:, s, :], ACT.Copy).then_inc(hi_done, 1)
                    if u + 1 == until:
                        return

            act.wait_ge(mem_full, 16)
            nc.scalar.activation(b_hi[:, :, 0:M], kt[:], ACT.Copy).then_inc(mem_hi, 1)
            high_parts(U_K + 6)
            act.wait_ge(x_full, 16)
            nc.scalar.activation(a_hi[:], xt_raw[:], ACT.Copy).then_inc(x_hi, 1)
            high_parts(U_V + KC + RING)
            act.wait_ge(unit_done, U_V + KC)
            for m in range(MB):
                nc.scalar.activation(v_hi[:, m, :], ps[:, 4 + 2 * m:6 + 2 * m, :], ACT.Copy).then_inc(vhi_done, 1)
            high_parts(U_VA + 4 + RING)
            for b in range(TB):
                act.wait_ge(va_in, b + 1)
                nc.scalar.activation(tok[:, b, :], tok[:, b, :], ACT.Gelu).then_inc(va_gelu, 1)
            act.wait_ge(var_ready, 1)
            nc.scalar.activation(sd[:], vc[:], ACT.Sqrt).then_inc(sd_ready, 1)
            for j in range(4):
                high_parts(U_CONV + 3 * (j + 1) + RING)
                act.wait_ge(z_read, 3 * j + 3)
                nc.scalar.activation(b_hi[:, 4 + j, :], y_t[:, j % 2, :], ACT.Copy).then_inc(yhi_done, 1)
            for j in range(4):
                high_parts(U_UA + j + 1 + RING)
                act.wait_ge(unit_done, U_UA + j + 1)
                nc.scalar.activation(u_t[:, j, :], ps[:, 4 + j, :], ACT.Gelu,
                                     bias=bcol[:, j:j + 1]).then_inc(u_ready, 1)
            for j in range(4):
                act.wait_ge(y_made, j + 1)
                nc.scalar.activation(b_hi[:, j, :], y_t[:, j % 2, :], ACT.Copy).then_inc(yhi_done, 1)
            high_parts(U_MIX + KC + RING)
            act.wait_ge(var_ready, 2)
            nc.scalar.activation(sd[:, 0:TB], vc[:, 0:TB], ACT.Sqrt).then_inc(sd_ready, 1)
            for b in range(TB):
                act.wait_ge(x1_tr, b + 1)
                nc.scalar.activation(a_hi[:, :, b * P:(b + 1) * P],
                                     ps[:, 2 * b:2 * b + 2, :].rearrange("p a (c j) -> p (a c) j", j=P),
                                     ACT.Copy).then_inc(x1_hi, 1)
            for e in range(KC):
                high_parts(U_XQ + e + 1 + RING)
                act.wait_ge(unit_done, U_XQ + e + 1)
                nc.scalar.activation(q_t[:, e, :], ps[:, e, :], ACT.Copy).then_inc(q_ready, 1)

            def probs_high(b):
                act.wait_ge(p_tr, b + 1)
                nc.scalar.activation(b_hi[:, :, b * P:(b + 1) * P],
                                     ps[:, 4 + 2 * (b % 2):6 + 2 * (b % 2), :].rearrange("p a (c j) -> p (a c) j", j=P),
                                     ACT.Copy).then_inc(p_hi, 1)

            for b in range(TB):
                act.wait_ge(mx_ready, b + 1)
                if b >= 2:
                    act.wait_ge(p_tr, b - 1)
                for h in range(XH):
                    nc.scalar.activation(probs[:, b % 2, h, :],
                                         ps[:, 2 * (b % 2) + h // 2, (h % 2) * M:(h % 2 + 1) * M], ACT.Exp,
                                         bias=nmx[:, b, h:h + 1], scale=XD ** -0.5,
                                         accum_out=sm[:, b, h:h + 1]).then_inc(exp_done, 1)
                if b >= 1:
                    probs_high(b - 1)
            probs_high(TB - 1)
            for e in range(KC):
                act.wait_ge(o_done, e + 1)
                nc.scalar.activation(a_hi[:, e, :], ps[:, e, :], ACT.Copy).then_inc(o_hi, 1)
            high_parts(FRONT_UNITS)
            act.wait_ge(var_ready, 3)
            nc.scalar.activation(sd[:, 0:TB], vc[:, 0:TB], ACT.Sqrt).then_inc(sd_ready, 1)
            for b in range(TB):
                act.wait_ge(x2_tr, b + 1)
                nc.scalar.activation(b_hi[:, :, b * P:(b + 1) * P],
                                     ps[:, 2 * b:2 * b + 2, :].rearrange("p a (c j) -> p (a c) j", j=P),
                                     ACT.Copy).then_inc(x2_hi, 1)

        @block.tensor
        def _(pe):
            def mm3(out, l_hi, l_lo, r_hi, r_lo, start, stop):
                nc.tensor.matmul(out, l_hi, r_hi, start=start, stop=False)
                nc.tensor.matmul(out, l_hi, r_lo, start=False, stop=False)
                return nc.tensor.matmul(out, l_lo, r_hi, start=False, stop=stop)

            def by_token(u0, n, banks, x_hi_, x_lo_, blocks, used=lambda: None):
                for k in range(n):
                    pe.wait_ge(split_done, u0 + k + 1)
                    s = (u0 + k) % RING
                    for b in range(blocks):
                        for h in range(2):
                            c, tk = slice(h * HALF, (h + 1) * HALF), slice(b * P, (b + 1) * P)
                            last = mm3(ps[:, banks + 2 * b + h, :], x_hi_[:, k, tk], x_lo_[:, k, tk],
                                       w_hi[:, s, c], w_lo[:, s, c], k == 0, k == n - 1)
                    last.then_inc(unit_done, 1)

            def by_channel(u, bank, x_hi_, x_lo_):
                pe.wait_ge(split_done, u + 1)
                s = u % RING
                for k in range(KC):
                    c = slice(k * P, (k + 1) * P)
                    last = mm3(ps[:, bank, :], w_hi[:, s, c], w_lo[:, s, c], x_hi_[:, k, :], x_lo_[:, k, :],
                               k == 0, k == KC - 1)
                last.then_inc(unit_done, 1)

            pe.wait_ge(mem_split, 1)
            by_token(U_K, KC, 0, b_hi, b_lo, MB)
            by_token(U_V, KC, 4, b_hi, b_lo, MB)
            pe.wait_ge(par_full, 16 * 8)
            pe.wait_ge(ktok_done, 4)
            for e in range(KC):
                for m in range(MB):
                    c = (e % 2) * M + m * P
                    last = nc.tensor.transpose(ps[:, e // 2, c:c + P], k_tok[:, m, e * P:(e + 1) * P], ident[:])
                if e % 2:
                    last.then_inc(ktr_done, 1)
            pe.wait_ge(x_split, 1)
            pe.wait_ge(kt_done, 4)
            for u in range(4):
                pe.wait_ge(split_done, U_VA + u + 1)
                s = (U_VA + u) % RING
                for i in range(2):
                    k = 2 * u + i
                    c = slice(i * HALF, (i + 1) * HALF)
                    for b in range(TB):
                        tk = slice(b * P, (b + 1) * P)
                        last = mm3(ps[:, b, :], a_hi[:, k, tk], a_lo[:, k, tk], w_hi[:, s, c], w_lo[:, s, c],
                                   k == 0, k == KC - 1)
                last.then_inc(unit_done, 1)
            pe.wait_ge(v_done, MB)
            for u in range(12):
                if u >= 4:
                    pe.wait_ge(z_read, u - 3)
                by_channel(U_CONV + u, 4 + u % 4, a_hi, a_lo)
            pe.wait_ge(ws_ready, 1)
            pe.wait_ge(va_ready, 1)
            for h in range(AH):
                for b in range(TB):
                    last = nc.tensor.matmul(ps[:, h, b * P:(b + 1) * P], tok[:, b, h * P:(h + 1) * P], wst[:, h, :],
                                            start=b == 0, stop=b == TB - 1, skip_group_check=True)
                last.then_inc(mix_done, 1)
            for u in range(4):
                pe.wait_ge(z_read, 8 + u + 1)
                by_channel(U_UA + u, 4 + u, a_hi, a_lo)
            pe.wait_ge(mix_read, 4)
            pe.wait_ge(u_ready, 4)
            pe.wait_ge(y_split, 8)
            by_token(U_MIX, KC, 0, b_hi, b_lo, TB)
            for b in range(TB):
                pe.wait_ge(x1_ready, b + 1)
                for e in range(KC):
                    last = nc.tensor.transpose(ps[:, 2 * b + e // 4, (e % 4) * P:(e % 4 + 1) * P],
                                               xres[:, b, e * P:(e + 1) * P], ident[:])
                last.then_inc(x1_tr, 1)
            pe.wait_ge(x1_split, TB)
            for e in range(KC):
                by_channel(U_XQ + e, e, a_hi, a_lo)

            def scores(b):
                if b >= 2:
                    pe.wait_ge(exp_done, XH * (b - 1))
                for h in range(XH):
                    for c in range(2):
                        last = nc.tensor.matmul(ps[:, 2 * (b % 2) + h // 2, (h % 2) * M:(h % 2 + 1) * M],
                                                q_t[:, 2 * h + c, b * P:(b + 1) * P], kt[:, 2 * h + c, :],
                                                start=c == 0, stop=c == 1)
                last.then_inc(sc_done, 1)

            def turn_probs(b):
                pe.wait_ge(p_ready, b + 1)
                if b >= 2:
                    pe.wait_ge(p_split, b - 1)
                for h in range(XH):
                    for m in range(MB):
                        i = MB * h + m
                        last = nc.tensor.transpose(ps[:, 4 + 2 * (b % 2) + i // 4, (i % 4) * P:(i % 4 + 1) * P],
                                                   probs[:, b % 2, h, m * P:(m + 1) * P], ident[:])
                last.then_inc(p_tr, 1)

            pe.wait_ge(q_ready, KC)
            scores(0)
            for b in range(1, TB):
                scores(b)
                turn_probs(b - 1)
            turn_probs(TB - 1)
            pe.wait_ge(p_split, TB)
            for e in range(KC):
                for m in range(MB):
                    i = MB * (e // 2) + m
                    c = slice(e * P, (e + 1) * P)
                    last = mm3(ps[:, e, :], v_hi[:, m, c], v_lo[:, m, c], b_hi[:, i, :], b_lo[:, i, :],
                               m == 0, m == MB - 1)
                last.then_inc(o_done, 1)
            pe.wait_ge(o_split, KC)
            by_token(U_XO, KC, 0, a_hi, a_lo, TB)
            for b in range(TB):
                pe.wait_ge(x2_ready, b + 1)
                for e in range(KC):
                    last = nc.tensor.transpose(ps[:, 2 * b + e // 4, (e % 4) * P:(e % 4 + 1) * P],
                                               xres[:, b, e * P:(e + 1) * P], ident[:])
                last.then_inc(x2_tr, 1)

        @block.vector
        def _(dve):
            step = Count(dve_step)

            def done():
                dve.wait_ge(dve_step, step.n)

            def inv_std(n, turn):
                done()
                nc.vector.tensor_scalar(vc[:, 0:n], mv[:, 0:n, 1], EPS, None, ALU.add).then_inc(var_ready, 1)
                dve.wait_ge(sd_ready, turn)
                step.up(nc.vector.reciprocal(rc[:, 0:n], sd[:, 0:n]))
                done()
                step.up(nc.vector.tensor_tensor(nt[:, 0, 0:n], rc[:, 0:n], rc[:, 0:n], ALU.mult))
                done()
                step.up(nc.vector.tensor_tensor(nt[:, 1, 0:n], nt[:, 0, 0:n], vc[:, 0:n], ALU.mult))
                done()
                step.up(nc.vector.tensor_scalar(nt[:, 0, 0:n], nt[:, 1, 0:n], -0.5, 1.5, ALU.mult, ALU.add))
                done()
                step.up(nc.vector.tensor_tensor(rc[:, 0:n], rc[:, 0:n], nt[:, 0, 0:n], ALU.mult))
                done()

            def layer_norm(u0, full, turn, ready):
                dve.wait_ge(unit_done, u0 + KC)
                for b in range(TB):
                    for h in range(2):
                        c = slice(h * HALF, (h + 1) * HALF)
                        step.up(nc.vector.scalar_tensor_tensor(out=xres[:, b, c], in0=xres[:, b, c], scalar=ALPHA,
                                                               in1=ps[:, 2 * b + h, :], op0=ALU.mult, op1=ALU.add))
                done()
                for b in range(TB):
                    for h in range(2):
                        step.up(nc.vector.bn_stats(bst[:, 2 * b + h, :], xres[:, b, h * HALF:(h + 1) * HALF]))
                done()
                for b in range(TB):
                    step.up(nc.vector.bn_aggr(mv[:, b, :], bst[:, 2 * b:2 * b + 2, :]))
                inv_std(TB, turn)
                dve.wait_ge(full, 32)
                for b in range(TB):
                    step.up(nc.vector.scalar_tensor_tensor(out=xres[:, b, :], in0=xres[:, b, :], scalar=mv[:, b, 0:1],
                                                           in1=lng[:], op0=ALU.subtract, op1=ALU.mult))
                    done()
                    nc.vector.scalar_tensor_tensor(out=xres[:, b, :], in0=xres[:, b, :], scalar=rc[:, b:b + 1],
                                                   in1=lnb[:], op0=ALU.mult, op1=ALU.add).then_inc(ready, 1)

            def low_part(lo_, hi_, src, sem_):
                nc.vector.tensor_tensor(lo_, src, hi_.bitcast(F32), ALU.subtract).then_inc(sem_, 1)

            dve.wait_ge(mem_hi, 1)
            low_part(b_lo[:, :, 0:M], b_hi[:, :, 0:M], kt[:], mem_split)
            dve.wait_ge(x_hi, 1)
            low_part(a_lo[:], a_hi[:], xt_raw[:], x_split)
            dve.wait_ge(unit_done, U_K + KC)
            for m in range(MB):
                for h in range(2):
                    nc.vector.tensor_copy(k_tok[:, m, h * HALF:(h + 1) * HALF], ps[:, 2 * m + h, :]
                                          ).then_inc(ktok_done, 1)
            for m in range(MB):
                dve.wait_ge(vhi_done, m + 1)
                low_part(v_lo[:, m, :].rearrange("p (a n) -> p a n", a=2), v_hi[:, m, :].rearrange("p (a n) -> p a n", a=2),
                         ps[:, 4 + 2 * m:6 + 2 * m, :], v_done)
            dve.wait_ge(mem_split, 1)
            for i in range(4):
                dve.wait_ge(ktr_done, i + 1)
                nc.vector.tensor_copy(kt[:, 2 * i:2 * i + 2, :], ps[:, i, :].rearrange("p (a n) -> p a n", a=2)
                                      ).then_inc(kt_done, 1)
            dve.wait_ge(par_full, 16 * 8)
            dve.wait_ge(unit_done, U_VA + 4)
            for b in range(TB):
                nc.vector.tensor_tensor(tok[:, b, :], ps[:, b, :], bias_va[:], ALU.add).then_inc(va_in, 1)
            for b in range(TB):
                dve.wait_ge(va_gelu, b + 1)
                for h in range(AH):
                    step.up(nc.vector.bn_stats(bst[:, AH * b + h, :], tok[:, b, h * P:(h + 1) * P]))
            done()
            for i in range(16):
                step.up(nc.vector.bn_aggr(mv[:, i, :], bst[:, i, :]))
            inv_std(16, 1)
            for b in range(TB):
                for h in range(AH):
                    i = AH * b + h
                    c = slice(h * P, (h + 1) * P)
                    step.up(nc.vector.tensor_scalar(tok[:, b, c], tok[:, b, c], mv[:, i, 0:1], rc[:, i:i + 1],
                                                    ALU.subtract, ALU.mult))
            done()
            step.up(nc.vector.tensor_tensor(tok[:], tok[:], sgu_g[:].unsqueeze(1).broadcast_to([P, TB, HALF]), ALU.mult))
            done()
            nc.vector.tensor_tensor(tok[:], tok[:], sgu_b[:].unsqueeze(1).broadcast_to([P, TB, HALF]),
                                    ALU.add).then_inc(va_ready, 1)
            step.up(nc.vector.memset(zc[:, 0:2], 0.0))
            dve.wait_ge(x_split, 1)

            def y_low(n):
                dve.wait_ge(yhi_done, n + 1)
                low_part(b_lo[:, (4 + n) % 8, :], b_hi[:, (4 + n) % 8, :], y_t[:, n % 2, :], y_split)

            for j in range(4):
                dve.wait_ge(unit_done, U_CONV + 3 * j + 1)
                if j:
                    dve.wait_ge(z_read, 3 * j)
                nc.vector.tensor_scalar(h_t, ps[:, 4 + 3 * j % 4, :], bcol[:, 8 + j:9 + j], None,
                                        ALU.add).then_inc(z_read, 1)
                dve.wait_ge(z_read, 3 * j + 1)
                dve.wait_ge(unit_done, U_CONV + 3 * j + 2)
                nc.vector.scalar_tensor_tensor(out=zc[:, 2:], in0=ps[:, 4 + (3 * j + 1) % 4, :],
                                               scalar=bcol[:, 16 + j:17 + j], in1=h_t,
                                               op0=ALU.add, op1=ALU.mult).then_inc(z_read, 1)
                dve.wait_ge(z_read, 3 * j + 2)
                done()
                step.up(nc.vector.tensor_scalar(c_t, zc[:, 0:S], cw[:, 0, j:j + 1], None, ALU.mult))
                for k in (1, 2):
                    done()
                    step.up(nc.vector.scalar_tensor_tensor(out=c_t, in0=zc[:, k:k + S], scalar=cw[:, k, j:j + 1],
                                                           in1=c_t, op0=ALU.mult, op1=ALU.add))
                done()
                if j >= 2:
                    dve.wait_ge(y_split, j - 1)
                dve.wait_ge(unit_done, U_CONV + 3 * j + 3)
                nc.vector.scalar_tensor_tensor(out=y_t[:, j % 2, :], in0=ps[:, 4 + (3 * j + 2) % 4, :],
                                               scalar=bcol[:, 12 + j:13 + j], in1=c_t,
                                               op0=ALU.add, op1=ALU.mult).then_inc(z_read, 1)
                dve.wait_ge(z_read, 3 * j + 3)
                if j:
                    y_low(j - 1)
            y_low(3)
            for h in range(AH):
                dve.wait_ge(mix_done, h + 1)
                nc.vector.tensor_tensor(c_t.rearrange("p (b j) -> p b j", b=TB),
                                        ps[:, h, :].rearrange("p (b j) -> p b j", b=TB),
                                        bsp[:, h, :].unsqueeze(1).broadcast_to([P, TB, P]), ALU.add).then_inc(mix_read, 1)
                dve.wait_ge(mix_read, h + 1)
                dve.wait_ge(u_ready, h + 1)
                dve.wait_ge(y_split, 4 + h - 1)
                nc.vector.tensor_tensor(y_t[:, h % 2, :], u_t[:, h, :], c_t, ALU.mult).then_inc(y_made, 1)
                dve.wait_ge(y_made, h + 1)
                if h:
                    y_low(4 + h - 1)
            y_low(7)
            dve.wait_ge(xres_full, 16)
            layer_norm(U_MIX, ln1_full, 2, x1_ready)
            for b in range(TB):
                dve.wait_ge(x1_hi, b + 1)
                tk = slice(b * P, (b + 1) * P)
                low_part(a_lo[:, :, tk], a_hi[:, :, tk],
                         ps[:, 2 * b:2 * b + 2, :].rearrange("p a (c j) -> p (a c) j", j=P), x1_split)

            def probs_low(b):
                dve.wait_ge(p_hi, b + 1)
                tk = slice(b * P, (b + 1) * P)
                low_part(b_lo[:, :, tk], b_hi[:, :, tk],
                         ps[:, 4 + 2 * (b % 2):6 + 2 * (b % 2), :].rearrange("p a (c j) -> p (a c) j", j=P), p_split)

            def row_max(b):
                dve.wait_ge(sc_done, b + 1)
                step.up(nc.vector.tensor_reduce(mx[:, b, :],
                                                ps[:, 2 * (b % 2):2 * (b % 2) + 2, :].rearrange("p a (c j) -> p (a c) j", j=M),
                                                AX.X, ALU.max))
                done()
                nc.vector.tensor_scalar(nmx[:, b, :], mx[:, b, :], -(XD ** -0.5), None, ALU.mult).then_inc(mx_ready, 1)

            row_max(0)
            for b in range(TB):
                if b + 1 < TB:
                    row_max(b + 1)
                dve.wait_ge(exp_done, XH * (b + 1))
                step.up(nc.vector.reciprocal(rs[:, b, :], sm[:, b, :]))
                done()
                for h in range(XH):
                    nc.vector.tensor_scalar(probs[:, b % 2, h, :], probs[:, b % 2, h, :], rs[:, b, h:h + 1], None,
                                            ALU.mult).then_inc(*((p_ready, 1) if h == XH - 1 else (dve_step, 1)))
                    step.n += h < XH - 1
                if b >= 1:
                    probs_low(b - 1)
            probs_low(TB - 1)
            for e in range(KC):
                dve.wait_ge(o_hi, e + 1)
                low_part(a_lo[:, e, :], a_hi[:, e, :], ps[:, e, :], o_split)
            layer_norm(U_XO, ln2_full, 3, x2_ready)
            for b in range(TB):
                dve.wait_ge(x2_hi, b + 1)
                tk = slice(b * P, (b + 1) * P)
                low_part(b_lo[:, :, tk], b_hi[:, :, tk],
                         ps[:, 2 * b:2 * b + 2, :].rearrange("p a (c j) -> p (a c) j", j=P), x2_split)


def top_experts(nc, step, done, k, between, scores_free):
    w0, w1, v16, i16, i16f, top, flat = k["w0"], k["w1"], k["v16"], k["i16"], k["i16f"], k["top"], k["flat"]
    fi, fif, ab = k["fi"], k["fif"], k["ab"]
    for e in range(NS):
        step(nc.vector.max(v16[:, e, 0:8], w0[:, e, :]))
        if e % 2:
            between()
    done()
    for e in range(NS):
        step(nc.vector.max_index(i16[:, e, 0:8], v16[:, e, 0:8], w0[:, e, :]))
        step(nc.vector.match_replace(w1[:, e, :], v16[:, e, 0:8], w0[:, e, :], NEG))
        if e % 2:
            between()
    done()
    for e in range(NS):
        step(nc.vector.max(v16[:, e, 8:16], w1[:, e, :]))
        if e % 4 == 3:
            between()
    done()
    for e in range(NS):
        step(nc.vector.max_index(i16[:, e, 8:16], v16[:, e, 8:16], w1[:, e, :]))
        if e % 4 == 3:
            between()
    done()
    vs = v16[:].rearrange("p (h s) i -> p h s i", s=2)
    c0 = w0[:].rearrange("p (h s) n -> p h (s n)", s=2)
    c1 = w1[:].rearrange("p (h s) n -> p h (s n)", s=2)
    shape = [P, PH, TOPK, TOPK]
    step(nc.vector.tensor_tensor(c0.rearrange("p h (i j) -> p h i j", i=TOPK),
                                 vs[:, :, 0, :].unsqueeze(3).broadcast_to(shape),
                                 vs[:, :, 1, :].unsqueeze(2).broadcast_to(shape), ALU.add))
    done()
    for h in range(PH):
        step(nc.vector.max(top[:, h, 0:8], c0[:, h, :]))
        if h % 4 == 3:
            between()
    done()
    for h in range(PH):
        step(nc.vector.max_index(flat[:, h, 0:8], top[:, h, 0:8], c0[:, h, :]))
        step(nc.vector.match_replace(c1[:, h, :], top[:, h, 0:8], c0[:, h, :], NEG))
        if h % 4 == 3:
            between()
    done()
    for h in range(PH):
        step(nc.vector.max(top[:, h, 8:16], c1[:, h, :]))
        if h % 4 == 3:
            between()
    done()
    nc.vector.tensor_tensor(k["ex"][:], top[:], top[:, :, 0:1].broadcast_to([P, PH, TOPK]),
                            ALU.subtract).then_inc(k["exp_in"], 1)
    for h in range(PH):
        step(nc.vector.max_index(flat[:, h, 8:16], top[:, h, 8:16], c1[:, h, :]))
        if h % 4 == 3:
            between()
    step(nc.vector.tensor_copy(i16f[:], i16[:]))
    done()
    step(nc.vector.tensor_single_scalar(fi[:, 0], flat[:], 4, ALU.logical_shift_right))
    step(nc.vector.tensor_single_scalar(fi[:, 1], flat[:], TOPK - 1, ALU.bitwise_and))
    done()
    step(nc.vector.tensor_copy(fif[:], fi[:]))
    done()
    isd = i16f[:].rearrange("p (h s) i -> p h s i", s=2)
    pk = [x.rearrange("p h (k i) -> p h k i", k=TOPK) for x in (c0, c1)]
    for side in range(2):
        step(nc.vector.tensor_tensor(pk[side], fif[:, side].unsqueeze(3).broadcast_to(shape),
                                     k["iota"][:, 0:TOPK].unsqueeze(1).unsqueeze(1).broadcast_to(shape), ALU.is_equal))
    done()
    for side in range(2):
        step(nc.vector.tensor_tensor(pk[side], pk[side], isd[:, :, side, :].unsqueeze(2).broadcast_to(shape), ALU.mult))
    done()
    step(nc.vector.tensor_reduce(ab[:, 1], pk[1], AX.X, ALU.add))
    nc.vector.tensor_reduce(ab[:, 0], pk[0], AX.X, ALU.add).then_inc(scores_free, 1)


def gates(nc, step, done, k, out):
    step(nc.vector.tensor_reduce(k["gsum"][:], k["ex"][:], AX.X, ALU.add))
    done()
    step(nc.vector.reciprocal(k["gsum"][:], k["gsum"][:]))
    done()
    step(nc.vector.tensor_tensor(out, k["ex"][:], k["gsum"][:].unsqueeze(2).broadcast_to([P, PH, TOPK]), ALU.mult))


def scores_block(nc, t, units):
    b_hi, b_lo, ps = t["b_hi"], t["b_lo"], t["ps"]
    ctx = ExitStack()
    with ctx:
        def sb(name, shape, dt=F32):
            return ctx.enter_context(nc.sbuf_tensor(name, shape, dt))

        def sem(name):
            return ctx.enter_context(nc.semaphore(name))

        raw = sb("raw2", [P, RING, D])
        w_hi = sb("w_hi2", [P, RING, D], F32R)
        w_lo = sb("w_lo2", [P, RING, D], F32R)
        sc = sb("sc", [P, TB, NS, NK])
        skt = sb("skt", [P, NS, NK])
        qs = sb("qs", [P, RING, S])
        raw_full = [sem(f"raw2_full{i}") for i in range(RING)]
        skt_full = sem("skt_full")
        hi_done, split_done, unit_done = sem("hi2_done"), sem("split2_done"), sem("unit2_done")
        qs_ready, ss_done, sc_ready = sem("qs_ready"), sem("ss_done"), sem("sc_ready")
        passed_pool = sem("passed_pool2")
        sc_stored = sem("sc_stored")
        rounds = NS // RING
        block = ctx.enter_context(nc.Block())

        @block.sync
        def _(sp):
            for u in range(RING):
                sp.dma_start(raw[:, u, :], units[u]).then_inc(raw_full[u], 16)
            sp.dma_start(skt[:], t["skt"]).then_inc(skt_full, 16)
            with sp.Fori(1, rounds) as r:
                for s in range(RING):
                    sp.wait_ge(split_done, RING * r + (s + 1 - RING))
                    sp.dma_start(raw[:, s, :], units[bass.ds(RING * r + s, 1)].rearrange("o p n -> (o p) n")
                                 ).then_inc(raw_full[s], 16)
            sp.wait_ge(sc_ready, NS)
            for b in (TB - 1, 0, 1, 2):
                sp.dma_start(t["sc_d"][b], sc[:, b].rearrange("p s n -> p (s n)")).then_inc(sc_stored, 16)
            sp.wait_ge(sc_stored, 16 * TB)

        @block.gpsimd
        def _(pool):
            def split_low(r, s):
                u = RING * r + s
                held(pool, hi_done, u + 1, passed_pool)
                nc.gpsimd.tensor_tensor(w_lo[:, s, :], raw[:, s, :], w_hi[:, s, :].bitcast(F32),
                                        ALU.subtract).then_inc(split_done, 1)

            with pool.Fori(0, rounds) as r:
                for s in range(RING):
                    split_low(r, s)

        @block.tensor
        def _(pe):
            def queries(r, s):
                u = RING * r + s
                pe.wait_ge(split_done, u + 1)
                for k in range(KC):
                    c = slice(k * P, (k + 1) * P)
                    nc.tensor.matmul(ps[:, s, :], w_hi[:, s, c], b_hi[:, k, :], start=k == 0, stop=False)
                    nc.tensor.matmul(ps[:, s, :], w_hi[:, s, c], b_lo[:, k, :], start=False, stop=False)
                    last = nc.tensor.matmul(ps[:, s, :], w_lo[:, s, c], b_hi[:, k, :], start=False, stop=k == KC - 1)
                last.then_inc(unit_done, 1)

            def scores(r, s, first=False):
                u = RING * r + s
                pe.wait_ge(qs_ready, u + 1)
                if not first:
                    pe.wait_ge(sc_ready, u - (RING - 1))
                for b in range(TB):
                    last = nc.tensor.matmul(ps[:, 4 + s, b * P:(b + 1) * P], qs[:, s, b * P:(b + 1) * P],
                                            skt[:, bass.ds(u, 1), :].rearrange("p o n -> p (o n)"),
                                            start=True, stop=True, skip_group_check=True)
                last.then_inc(ss_done, 1)

            pe.wait_ge(skt_full, 16)
            queries(0, 0)
            for s in range(1, RING):
                queries(0, s)
                scores(0, s - 1, first=True)
            queries(1, 0)
            scores(0, RING - 1, first=True)
            for s in range(1, RING):
                queries(1, s)
                scores(1, s - 1)
            with pe.Fori(2, rounds) as r:
                for s in range(RING):
                    queries(r, s)
                    scores(r if s else r - 1, (s - 1) % RING)
            scores(rounds - 1, RING - 1)

        @block.scalar
        def _(act):
            def high_part(r, s, first=False):
                u = RING * r + s
                act.wait_ge(raw_full[s], 16 * r + 16)
                if not first:
                    act.wait_ge(unit_done, u - (RING - 1))
                nc.scalar.activation(w_hi[:, s, :], raw[:, s, :], ACT.Copy).then_inc(hi_done, 1)

            def queries_out(r, s, first):
                u = RING * r + s
                act.wait_ge(unit_done, u + 1)
                if not first:
                    act.wait_ge(ss_done, u - (RING - 1))
                nc.scalar.activation(qs[:, s, :], ps[:, s, :], ACT.Copy).then_inc(qs_ready, 1)

            for s in range(RING):
                high_part(0, s, first=True)
            for s in range(RING):
                high_part(1, s)
                queries_out(0, s, True)
            with act.Fori(1, rounds - 1) as r:
                for s in range(RING):
                    high_part(r + 1, s)
                    queries_out(r, s, False)
            for s in range(RING):
                queries_out(rounds - 1, s, False)

        @block.vector
        def _(dve):
            with dve.Fori(0, rounds) as r:
                for s in range(RING):
                    dve.wait_ge(ss_done, RING * r + (s + 1))
                    nc.vector.tensor_copy(sc[:, :, bass.ds(RING * r + s, 1), :].rearrange("p b o n -> p b (o n)"),
                                          ps[:, 4 + s, :].rearrange("p (b n) -> p b n", b=TB)).then_inc(sc_ready, 1)


DB = TB - 1
DT = DB * P
GB = TB - 1
HK = PH * TOPK
TILES = NK
W3 = 3
GS = 4
RT = 8
GSCALE = 2.0 ** 15

LEAD_TURNS, CHOICE_TURNS, GATE_TURNS, ROUNDS = 4, 8, 4, 4
BLOCK_TURNS = CHOICE_TURNS + GATE_TURNS
TAIL_TURN = LEAD_TURNS + DB * BLOCK_TURNS
END_TURN = TILES // W3


def down_block(nc, t):
    b_hi, b_lo, ps, ident = t["b_hi"], t["b_lo"], t["ps"], t["ident"]
    ctx = ExitStack()
    with ctx:
        def sb(name, shape, dt=F32):
            return ctx.enter_context(nc.sbuf_tensor(name, shape, dt))

        def sem(name):
            return ctx.enter_context(nc.semaphore(name))

        raw = sb("raw3", [P, W3, D])
        w_hi = sb("w_hi3", [P, W3, D], F32R)
        w_lo = sb("w_lo3", [P, W3, D], F32R)
        act_t = sb("act_t", [P, W3, DT])
        gmat = sb("gmat", [P, NK, P])
        k = {"w0": sb("w0", [P, NS, NK]), "w1": sb("w1", [P, NS, NK]), "v16": sb("v16", [P, NS, TOPK]),
             "i16": sb("i16", [P, NS, TOPK], U32), "i16f": sb("i16f", [P, NS, TOPK]), "top": sb("top", [P, PH, TOPK]),
             "flat": sb("flat", [P, PH, TOPK], U32), "fi": sb("fi", [P, 2, PH, TOPK], U32),
             "fif": sb("fif", [P, 2, PH, TOPK]), "ab": sb("ab", [P, 2, PH, TOPK]),
             "ex": sb("ex", [P, PH, TOPK]), "gsum": sb("gsum", [P, PH]), "iota": sb("iota", [P, P])}
        gate_h = sb("gate_h", [P, PH, TOPK], F16)
        gparts = sb("gparts", [P, 3, PH, TOPK])
        cols = sb("cols", [P, 4, P], F16)
        numbers = sb("numbers", [P, P, RT], F16)
        eq_a = sb("eq_a", [P, 2, P, RT], F16)
        eq_b = sb("eq_b", [P, P, RT], F16)
        gb = sb("gb", [P, 2, 2, P, RT], F16)
        rows = sb("rows", [P, GS, D])
        idx = sb("idx", [P, GS], U32)
        ef = sb("ef", [P, HK])
        expert, gate, dn, xb = t["expert"], t["gate"], t["dn"], sb("xb", [P, D])

        raw_full = [sem(f"raw3_full{i}") for i in range(W3)]
        hi_done, split_done, unit_done = sem("hi3_done"), sem("split3_done"), sem("unit3_done")
        gelu_done = sem("gelu3_done")
        act_stored = [sem(f"act_stored{i}") for i in range(W3)]
        w0_full, w0_free, exp_in, exp_out = sem("w0_full"), sem("w0_free"), sem("exp_in"), sem("exp_out")
        k["exp_in"] = exp_in
        const_full, xb_full = sem("const_full"), sem("xb_full")
        experts_ready, row_free, idx_ready = sem("experts_ready"), sem("row3_free"), sem("idx3_ready")
        row_full = [sem(f"row3_full{i}") for i in range(GS)]
        picks_ready, picks_turned, cols_ready = sem("picks_ready"), sem("picks_turned"), sem("cols_ready")
        eq_step, gb_step, gb_ready, round_done, round_free = (
            sem("eq_step"), sem("gb_step"), sem("gb_ready"), sem("round_done"), sem("round_free"))
        gmat_stored = sem("gmat_stored")
        dve_step, passed_dve, passed_pool = sem("dve3_step"), sem("passed_dve3"), sem("passed_pool3")
        block = ctx.enter_context(nc.Block())

        def ahead(n, s):
            return (s + 2) % W3, n + (s + 2) // W3

        @block.sync
        def _(sp):
            sp.dma_start(raw[:, 0, :], t["down_t"][0]).then_inc(raw_full[0], 16)
            sp.dma_start(raw[:, 1, :], t["down_t"][1]).then_inc(raw_full[1], 16)
            sp.dma_start(k["w0"][:].rearrange("p s n -> p (s n)"), t["sc_d"][GB]).then_inc(w0_full, 16)
            sp.dma_start(raw[:, 2, :], t["down_t"][2]).then_inc(raw_full[2], 16)
            sp.dma_start(k["iota"][:], t["iota"].partition_broadcast(P)).then_inc(const_full, 16)
            sp.dma_start(xb[:], t["x2_d"][GB]).then_inc(xb_full, 16)

            def load(n, s):
                sp.wait_ge(split_done, W3 * n + (s + 1 - W3))
                sp.dma_start(raw[:, s, :], t["down_t"][bass.ds(W3 * n + s, 1)].rearrange("o p n -> (o p) n")
                             ).then_inc(raw_full[s], 16)

            with sp.Fori(1, END_TURN) as n:
                for s in range(W3):
                    load(n, s)
            for s in range(TILES - W3 * END_TURN):
                load(END_TURN, s)

        @block.gpsimd
        def _(pool):
            def split_low(s, n):
                u = W3 * n + s
                if isinstance(n, int):
                    pool.wait_ge(hi_done, u + 1)
                else:
                    held(pool, hi_done, u + 1, passed_pool)
                nc.gpsimd.tensor_tensor(w_lo[:, s, :], raw[:, s, :], w_hi[:, s, :].bitcast(F32),
                                        ALU.subtract).then_inc(split_done, 1)

            def turn(n):
                for s in range(W3):
                    split_low(*ahead(n, s))

            def gather(n, j):
                m = GS * n + j
                held(pool, row_free, m + 1, passed_pool)
                nc.gpsimd.tensor_copy(idx[:, j:j + 1], expert[:, bass.ds(m, 1)]).then_inc(idx_ready, 1)
                held(pool, idx_ready, m + 1, passed_pool)
                nc.gpsimd.indirect_dma_start(rows[:, j, :], None, t["w_down"],
                                             bass.IndirectOffsetOnAxis(ap=idx[:, j:j + 1], axis=0)
                                             ).then_inc(row_full[j], 16)

            split_low(0, 0)
            split_low(1, 0)
            turn(0)
            with pool.Fori(1, LEAD_TURNS) as n:
                turn(n)
            pool.wait_ge(experts_ready, 1)
            with pool.Fori(0, DB) as b:
                with pool.Fori(0, CHOICE_TURNS) as r:
                    for s in range(W3):
                        split_low(*ahead(LEAD_TURNS + BLOCK_TURNS * b + r, s))
                        gather(CHOICE_TURNS * b + r, s)
                    gather(CHOICE_TURNS * b + r, W3)
                with pool.Fori(0, GATE_TURNS) as r:
                    for s in range(W3):
                        split_low(*ahead(LEAD_TURNS + CHOICE_TURNS + BLOCK_TURNS * b + r, s))
            with pool.Fori(0, END_TURN - TAIL_TURN) as r:
                for s in range(W3):
                    split_low(*ahead(TAIL_TURN + r, s))
                    gather(DB * CHOICE_TURNS + W3 * r + s, 0)
                    for j in range(1, GS):
                        gather(DB * CHOICE_TURNS + W3 * r + s, j)
            with pool.Fori(DB * CHOICE_TURNS + W3 * (END_TURN - TAIL_TURN), HK // GS) as n:
                for j in range(GS):
                    gather(n, j)

        @block.scalar
        def _(act):
            act.sem_inc(round_free, 2)

            def split_high(s, n):
                u = W3 * n + s
                act.wait_ge(raw_full[s], 16 * n + 16)
                if not isinstance(n, int) or n:
                    act.wait_ge(unit_done, u - (W3 - 1))
                nc.scalar.activation(w_hi[:, s, :], raw[:, s, :], ACT.Copy).then_inc(hi_done, 1)

            def gelu(n, s, first=False):
                u = W3 * n + s
                act.wait_ge(unit_done, u + 1)
                if not first:
                    act.wait_ge(act_stored[s], 16 * n)
                nc.scalar.activation(act_t[:, s, :], ps[:, s, 0:DT], ACT.Gelu).then_inc(gelu_done, 1)
                act.wait_ge(gelu_done, u + 1)
                act.dma_start(t["act_d"][bass.ds(u, 1)].rearrange("o p n -> (o p) n") if not isinstance(n, int)
                              else t["act_d"][u], act_t[:, s, :]).then_inc(act_stored[s], 16)

            def tile(n, s, first=False):
                split_high(*ahead(n, s))
                gelu(n, s, first)

            def turn(n, first=False):
                for s in range(W3):
                    tile(n, s, first)

            def exponent(i):
                act.wait_ge(exp_in, i)
                nc.scalar.activation(k["ex"][:], k["ex"][:], ACT.Exp).then_inc(exp_out, 1)

            def gate_out(b, r, q):
                rho = ROUNDS * (GATE_TURNS * b + r) + q
                act.wait_ge(round_done, rho + 3)
                for i in range(2):
                    c = bass.ds(RT * (ROUNDS * r + q) + 4 * i, 4)
                    ins = nc.scalar.activation(gmat[:, :, c].rearrange("p b j -> p j b"),
                                               ps[:, 4 + 2 * (q % 2) + i, :].rearrange("p (j b) -> p j b", j=4), ACT.Copy)
                ins.then_inc(round_free, 1)

            split_high(0, 0)
            split_high(1, 0)
            turn(0, first=True)
            with act.Fori(1, LEAD_TURNS) as n:
                turn(n)
            exponent(1)
            act.wait_ge(w0_free, 1)
            act.dma_start(k["w0"][:].rearrange("p s n -> p (s n)"), t["sc_d"][0]).then_inc(w0_full, 16)
            with act.Fori(0, DB) as b:
                with act.Fori(0, CHOICE_TURNS) as r:
                    turn(LEAD_TURNS + BLOCK_TURNS * b + r)
                exponent(b + 2)
                act.wait_ge(w0_free, b + 2)
                act.dma_start(k["w0"][:].rearrange("p s n -> p (s n)"),
                              t["sc_d"][bass.ds(b + 1, 1)].rearrange("o p n -> (o p) n")).then_inc(w0_full, 16)
                with act.Fori(0, GATE_TURNS) as r:
                    for s in range(W3):
                        tile(LEAD_TURNS + CHOICE_TURNS + BLOCK_TURNS * b + r, s)
                        gate_out(b, r, s)
                    gate_out(b, r, W3)
                act.wait_ge(round_free, ROUNDS * GATE_TURNS * (b + 1) + 2)
                act.dma_start(t["gate_d"][:, :, bass.ds(P * b, P)].rearrange("b a j -> a b j"), gmat[:]
                              ).then_inc(gmat_stored, 16)
            with act.Fori(TAIL_TURN, END_TURN) as n:
                turn(n)
            for s in range(TILES - W3 * END_TURN):
                gelu(END_TURN, s)
            for s in range(W3):
                act.wait_ge(act_stored[s], 16 * (END_TURN + (s < TILES - W3 * END_TURN)))
            act.wait_ge(gmat_stored, 16 * DB)
            act.wait_ge(w0_full, 16 * (DB + 2))

        @block.tensor
        def _(pe):
            pe.sem_inc(round_done, 2)

            def tile(n, s, first=False):
                u = W3 * n + s
                pe.wait_ge(split_done, u + 1)
                if not first:
                    pe.wait_ge(gelu_done, u - (W3 - 1))
                for c in range(KC):
                    w = slice(c * P, (c + 1) * P)
                    nc.tensor.matmul(ps[:, s, 0:DT], w_hi[:, s, w], b_hi[:, c, 0:DT], start=c == 0, stop=False)
                    nc.tensor.matmul(ps[:, s, 0:DT], w_hi[:, s, w], b_lo[:, c, 0:DT], start=False, stop=False)
                    last = nc.tensor.matmul(ps[:, s, 0:DT], w_lo[:, s, w], b_hi[:, c, 0:DT], start=False,
                                            stop=c == KC - 1)
                last.then_inc(unit_done, 1)

            def turn_picks(b):
                pe.wait_ge(picks_ready, b + 1)
                for i, src in enumerate((k["ab"][:, 0], k["ab"][:, 1], gparts[:, 1], gparts[:, 2])):
                    last = nc.tensor.transpose(ps[:, 3, i * P:(i + 1) * P], src.rearrange("p h k -> p (h k)"), ident[:])
                last.then_inc(picks_turned, 1)

            def gate_round(b, r, q):
                rho = ROUNDS * (GATE_TURNS * b + r) + q
                pe.wait_ge(gb_ready, rho + 1)
                pe.wait_ge(round_free, rho + 1)
                for j in range(RT):
                    out = ps[:, 4 + 2 * (q % 2) + j // 4, (j % 4) * P:(j % 4 + 1) * P]
                    nc.tensor.matmul(out, eq_a[:, q % 2, :, j], gb[:, q % 2, 0, :, j], start=True, stop=False,
                                     skip_group_check=True)
                    last = nc.tensor.matmul(out, eq_a[:, q % 2, :, j], gb[:, q % 2, 1, :, j], start=False, stop=True,
                                            skip_group_check=True)
                last.then_inc(round_done, 1)

            for s in range(W3):
                tile(0, s, first=True)
            with pe.Fori(1, LEAD_TURNS) as n:
                for s in range(W3):
                    tile(n, s)
            with pe.Fori(0, DB) as b:
                with pe.Fori(0, CHOICE_TURNS) as r:
                    for s in range(W3):
                        tile(LEAD_TURNS + BLOCK_TURNS * b + r, s)
                turn_picks(b)
                with pe.Fori(0, GATE_TURNS) as r:
                    for s in range(W3):
                        tile(LEAD_TURNS + CHOICE_TURNS + BLOCK_TURNS * b + r, s)
                        gate_round(b, r, s)
                    gate_round(b, r, W3)
            with pe.Fori(TAIL_TURN, END_TURN) as n:
                for s in range(W3):
                    tile(n, s)
            for s in range(TILES - W3 * END_TURN):
                tile(END_TURN, s)

        @block.vector
        def _(dve):
            n_steps = [0]

            def step(ins):
                ins.then_inc(dve_step, 1)
                n_steps[0] += 1

            def done():
                dve.wait_ge(dve_step, n_steps[0])

            def restart():
                dve.sem_clear(dve_step)
                n_steps[0] = 0

            def dot(n, j):
                held(dve, row_full[j], 16 * n + 16, passed_dve)
                nc.vector.scalar_tensor_tensor(out=rows[:, j, :], in0=rows[:, j, :], scalar=1.0, in1=xb[:],
                                               op0=ALU.mult, op1=ALU.mult,
                                               accum_out=dn[:, bass.ds(GS * n + j, 1)]).then_inc(row_free, 1)

            dve.sem_inc(row_free, GS)
            dve.wait_ge(const_full, 16)
            dve.wait_ge(xb_full, 16)
            dve.wait_ge(w0_full, 16)
            step(nc.vector.tensor_copy(numbers[:], k["iota"][:].unsqueeze(2).broadcast_to([P, P, RT])))
            top_experts(nc, step, done, k, lambda: None, w0_free)
            dve.wait_ge(w0_free, 1)
            done()
            step(nc.vector.scalar_tensor_tensor(out=ef[:], in0=k["ab"][:, 0].rearrange("p h k -> p (h k)"),
                                                scalar=float(NK), in1=k["ab"][:, 1].rearrange("p h k -> p (h k)"),
                                                op0=ALU.mult, op1=ALU.add))
            done()
            nc.vector.tensor_copy(expert[:], ef[:]).then_inc(experts_ready, 1)
            dve.wait_ge(exp_out, 1)
            gates(nc, step, done, k, gate[:])
            done()
            with dve.Fori(0, DB) as b:
                restart()
                held(dve, w0_full, 16 * b + 32, passed_dve)
                made = [0]

                def between():
                    dot(CHOICE_TURNS * b + made[0] // GS, made[0] % GS)
                    made[0] += 1

                top_experts(nc, step, done, k, between, w0_free)
                assert made[0] == CHOICE_TURNS * GS
                held(dve, exp_out, b + 2, passed_dve)
                gates(nc, step, done, k, gparts[:, 0])
                done()
                step(nc.vector.tensor_scalar(gparts[:, 0], gparts[:, 0], GSCALE, None, ALU.mult))
                done()
                step(nc.vector.tensor_copy(gate_h[:], gparts[:, 0]))
                done()
                step(nc.vector.tensor_copy(gparts[:, 1], gate_h[:]))
                done()
                nc.vector.tensor_tensor(gparts[:, 2], gparts[:, 0], gparts[:, 1], ALU.subtract).then_inc(picks_ready, 1)
                held(dve, picks_turned, b + 1, passed_dve)
                nc.vector.tensor_copy(cols[:], ps[:, 3, :].rearrange("p (i j) -> p i j", i=4)).then_inc(cols_ready, 1)
                held(dve, cols_ready, b + 1, passed_dve)
                with dve.Fori(0, GATE_TURNS) as r:
                    for q in range(ROUNDS):
                        rho = ROUNDS * (GATE_TURNS * b + r) + q
                        held(dve, round_done, rho + 1, passed_dve)
                        tok = bass.ds(RT * (ROUNDS * r + q), RT)
                        of = [cols[:, i, tok].unsqueeze(1).broadcast_to([P, P, RT]) for i in range(4)]
                        if q:
                            dve.wait_ge(gb_step, 2 * q)
                        nc.vector.tensor_tensor(eq_b[:], numbers[:], of[1], ALU.is_equal).then_inc(eq_step, 1)
                        nc.vector.tensor_tensor(eq_a[:, q % 2], numbers[:], of[0], ALU.is_equal).then_inc(eq_step, 1)
                        dve.wait_ge(eq_step, 2 * q + 1)
                        nc.vector.tensor_tensor(gb[:, q % 2, 0], eq_b[:], of[2], ALU.mult).then_inc(gb_step, 1)
                        nc.vector.tensor_tensor(gb[:, q % 2, 1], eq_b[:], of[3], ALU.mult).then_inc(gb_step, 1)
                        dve.wait_ge(eq_step, 2 * q + 2)
                        dve.wait_ge(gb_step, 2 * q + 2)
                        dve.sem_inc(gb_ready, 1)
                    dve.sem_clear(eq_step)
                    dve.sem_clear(gb_step)
            with dve.Fori(DB * CHOICE_TURNS, HK // GS) as n:
                for j in range(GS):
                    dot(n, j)


def up_block(nc, t, out):
    ps, expert, gate, dn = t["ps"], t["expert"], t["gate"], t["dn"]
    ctx = ExitStack()
    with ctx:
        def sb(name, shape, dt=F32):
            return ctx.enter_context(nc.sbuf_tensor(name, shape, dt))

        def sem(name):
            return ctx.enter_context(nc.semaphore(name))

        raw = sb("raw4", [P, W3, D])
        w_hi = sb("w_hi4", [P, W3, D], F32R)
        w_lo = sb("w_lo4", [P, W3, D], F32R)
        act_t = sb("act4", [P, W3, DT])
        gate_t = sb("gate4", [P, W3, DT])
        h_t = sb("h_t", [P, W3, DT])
        h_hi = sb("h_hi", [P, W3, DT], F32R)
        h_lo = sb("h_lo", [P, W3, DT], F32R)
        rows = sb("rows4", [P, W3, D])
        idx = sb("idx4", [P, W3], U32)
        acc = sb("acc", [P, W3, D])
        coef = sb("coef", [P, HK])
        xres = sb("xres4", [P, TB, D])
        lng, lnb = sb("ln3g", [P, D]), sb("ln3b", [P, D])
        bst, mv, vc, sd = sb("bst3", [P, 2 * TB, 6]), sb("mv3", [P, TB, 2]), sb("vc3", [P, TB]), sb("sd3", [P, TB])
        rc, nt = sb("rc3", [P, TB]), sb("nt3", [P, 2, TB])

        raw_full = [sem(f"raw4_full{i}") for i in range(W3)]
        ag_full = [sem(f"ag4_full{i}") for i in range(W3)]
        hi_done, split_done, unit_done = sem("hi4_done"), sem("split4_done"), sem("unit4_done")
        h_ready, h_hi_done, h_split = sem("h_ready"), sem("h_hi_done"), sem("h_split")
        row_free, idx_ready = sem("row4_free"), sem("idx4_ready")
        row_full = [sem(f"row4_full{i}") for i in range(W3)]
        gelu_done, x2_full, ln_full = sem("gelu4_done"), sem("x2_full"), sem("ln3_full")
        var_ready, sd_ready, res_ready, out_done = sem("var4_ready"), sem("sd4_ready"), sem("res_ready"), sem("out_done")
        dve_step, passed_dve, passed_pool = sem("dve4_step"), sem("passed_dve4"), sem("passed_pool4")
        block = ctx.enter_context(nc.Block())
        left = TILES - W3 * END_TURN

        def held_or(eng, semaphore, value, passed):
            if isinstance(value, int):
                eng.wait_ge(semaphore, value)
            else:
                held(eng, semaphore, value, passed)

        @block.sync
        def _(sp):
            def load(n, s, first=False):
                u = W3 * n + s
                sel = (lambda x: x[u]) if isinstance(n, int) else (
                    lambda x: x[bass.ds(u, 1)].rearrange("o p n -> (o p) n"))
                if not first:
                    sp.wait_ge(split_done, u - (W3 - 1))
                sp.dma_start(raw[:, s, :], sel(t["up_t"])).then_inc(raw_full[s], 16)
                if not first:
                    sp.wait_ge(h_ready, u - (W3 - 1))
                sp.dma_start(act_t[:, s, :], sel(t["act_d"])).then_inc(ag_full[s], 16)
                sp.dma_start(gate_t[:, s, :], sel(t["gate_d"])).then_inc(ag_full[s], 16)

            for s in range(W3):
                load(0, s, first=True)
            sp.dma_start(xres[:], t["x2_d"].rearrange("b p d -> p b d")).then_inc(x2_full, 16)
            sp.dma_start(lng[:], t["ln3_g"].partition_broadcast(P)).then_inc(ln_full, 16)
            sp.dma_start(lnb[:], t["ln3_b"].partition_broadcast(P)).then_inc(ln_full, 16)
            with sp.Fori(1, END_TURN) as n:
                for s in range(W3):
                    load(n, s)
            for s in range(left):
                load(END_TURN, s)
            for b in range(TB):
                sp.wait_ge(res_ready, b + 1)
                sp.dma_start(out[0, b * P:(b + 1) * P, :], xres[:, b, :]).then_inc(out_done, 16)
            sp.wait_ge(out_done, 16 * TB)

        @block.gpsimd
        def _(pool):
            def tile(n, s):
                u = W3 * n + s
                held_or(pool, hi_done, u + 1, passed_pool)
                nc.gpsimd.tensor_tensor(w_lo[:, s, :], raw[:, s, :], w_hi[:, s, :].bitcast(F32),
                                        ALU.subtract).then_inc(split_done, 1)
                held_or(pool, row_free, u + 1, passed_pool)
                nc.gpsimd.tensor_copy(idx[:, s:s + 1], expert[:, bass.ds(u, 1)]).then_inc(idx_ready, 1)
                held_or(pool, idx_ready, u + 1, passed_pool)
                nc.gpsimd.indirect_dma_start(rows[:, s, :], None, t["w_up"],
                                             bass.IndirectOffsetOnAxis(ap=idx[:, s:s + 1], axis=0)
                                             ).then_inc(row_full[s], 16)

            with pool.Fori(0, END_TURN) as n:
                for s in range(W3):
                    tile(n, s)
            for s in range(left):
                tile(END_TURN, s)

        @block.scalar
        def _(act):
            nc.scalar.activation(coef[:], dn[:], ACT.Gelu).then_inc(gelu_done, 1)

            def tile(n, s, first=False):
                u = W3 * n + s
                act.wait_ge(raw_full[s], 16 * n + 16)
                if not first:
                    act.wait_ge(unit_done, u - (W3 - 1))
                nc.scalar.activation(w_hi[:, s, :], raw[:, s, :], ACT.Copy).then_inc(hi_done, 1)
                act.wait_ge(h_ready, u + 1)
                nc.scalar.activation(h_hi[:, s, :], h_t[:, s, :], ACT.Copy).then_inc(h_hi_done, 1)

            for s in range(W3):
                tile(0, s, first=True)
            with act.Fori(1, END_TURN) as n:
                for s in range(W3):
                    tile(n, s)
            for s in range(left):
                tile(END_TURN, s)
            act.wait_ge(var_ready, 1)
            nc.scalar.activation(sd[:], vc[:], ACT.Sqrt).then_inc(sd_ready, 1)

        @block.tensor
        def _(pe):
            def tile(n, s, start=False, stop=False):
                u = W3 * n + s
                pe.wait_ge(split_done, u + 1)
                pe.wait_ge(h_split, u + 1)
                for b in range(DB):
                    for h in range(2):
                        c, tk = slice(h * HALF, (h + 1) * HALF), slice(b * P, (b + 1) * P)
                        o = ps[:, 2 * b + h, :]
                        nc.tensor.matmul(o, h_hi[:, s, tk], w_hi[:, s, c], start=start, stop=False)
                        nc.tensor.matmul(o, h_hi[:, s, tk], w_lo[:, s, c], start=False, stop=False)
                        last = nc.tensor.matmul(o, h_lo[:, s, tk], w_hi[:, s, c], start=False, stop=stop)
                last.then_inc(unit_done, 1)

            for s in range(W3):
                tile(0, s, start=s == 0)
            with pe.Fori(1, END_TURN) as n:
                for s in range(W3):
                    tile(n, s)
            for s in range(left):
                tile(END_TURN, s, stop=s == left - 1)

        @block.vector
        def _(dve):
            step_count = Count(dve_step)
            step = step_count.up

            def done():
                dve.wait_ge(dve_step, step_count.n)

            dve.sem_inc(row_free, W3)
            step(nc.vector.memset(acc[:], 0.0))
            dve.wait_ge(gelu_done, 1)
            step(nc.vector.tensor_tensor(coef[:], coef[:], gate[:].rearrange("p h k -> p (h k)"), ALU.mult))
            done()

            def gated(n, s, first=False):
                u = W3 * n + s
                held_or(dve, ag_full[s], 32 * n + 32, passed_dve)
                if not first:
                    held(dve, h_split, u - (W3 - 1), passed_dve) if not isinstance(n, int) else dve.wait_ge(
                        h_split, u - (W3 - 1))
                nc.vector.scalar_tensor_tensor(out=h_t[:, s, :], in0=act_t[:, s, :], scalar=1.0 / GSCALE,
                                               in1=gate_t[:, s, :], op0=ALU.mult, op1=ALU.mult).then_inc(h_ready, 1)

            def low(n, s, first=False):
                u = W3 * n + s
                held_or(dve, h_hi_done, u + 1, passed_dve)
                nc.vector.tensor_tensor(h_lo[:, s, :], h_t[:, s, :], h_hi[:, s, :].bitcast(F32),
                                        ALU.subtract).then_inc(h_split, 1)

            def row(n, s):
                u = W3 * n + s
                held_or(dve, row_full[s], 16 * n + 16, passed_dve)
                held_or(dve, row_free, u + 1, passed_dve)
                nc.vector.scalar_tensor_tensor(out=acc[:, s, :], in0=rows[:, s, :], scalar=coef[:, bass.ds(u, 1)],
                                               in1=acc[:, s, :], op0=ALU.mult, op1=ALU.add).then_inc(row_free, 1)

            gated(0, 0, first=True)
            for s in range(W3):
                if s + 1 < W3:
                    gated(0, s + 1, first=True)
                else:
                    gated(1, 0)
                low(0, s)
                row(0, s)
            with dve.Fori(1, END_TURN - 1) as n:
                for s in range(W3):
                    gated(n + (s + 1) // W3, (s + 1) % W3)
                    low(n, s)
                    row(n, s)
            for u in range(W3 * (END_TURN - 1), TILES):
                if u + 1 < TILES:
                    gated((u + 1) // W3, (u + 1) % W3)
                low(u // W3, u % W3)
                row(u // W3, u % W3)
            dve.wait_ge(row_free, TILES + W3)
            dve.wait_ge(x2_full, 16)
            dve.wait_ge(ln_full, 32)
            step(nc.vector.tensor_tensor(acc[:, 0, :], acc[:, 0, :], acc[:, 1, :], ALU.add))
            step(nc.vector.scalar_tensor_tensor(out=xres[:, GB, :], in0=xres[:, GB, :], scalar=ALPHA, in1=acc[:, 2, :],
                                                op0=ALU.mult, op1=ALU.add))
            done()
            step(nc.vector.tensor_tensor(xres[:, GB, :], xres[:, GB, :], acc[:, 0, :], ALU.add))
            dve.wait_ge(unit_done, TILES)
            for b in range(DB):
                for h in range(2):
                    c = slice(h * HALF, (h + 1) * HALF)
                    step(nc.vector.scalar_tensor_tensor(out=xres[:, b, c], in0=xres[:, b, c], scalar=ALPHA,
                                                        in1=ps[:, 2 * b + h, :], op0=ALU.mult, op1=ALU.add))
            done()
            for b in range(TB):
                for h in range(2):
                    step(nc.vector.bn_stats(bst[:, 2 * b + h, :], xres[:, b, h * HALF:(h + 1) * HALF]))
            done()
            for b in range(TB):
                step(nc.vector.bn_aggr(mv[:, b, :], bst[:, 2 * b:2 * b + 2, :]))
            done()
            nc.vector.tensor_scalar(vc[:], mv[:, :, 1], EPS, None, ALU.add).then_inc(var_ready, 1)
            dve.wait_ge(sd_ready, 1)
            step(nc.vector.reciprocal(rc[:], sd[:]))
            done()
            step(nc.vector.tensor_tensor(nt[:, 0], rc[:], rc[:], ALU.mult))
            done()
            step(nc.vector.tensor_tensor(nt[:, 1], nt[:, 0], vc[:], ALU.mult))
            done()
            step(nc.vector.tensor_scalar(nt[:, 0], nt[:, 1], -0.5, 1.5, ALU.mult, ALU.add))
            done()
            step(nc.vector.tensor_tensor(rc[:], rc[:], nt[:, 0], ALU.mult))
            done()
            for b in range(TB):
                step(nc.vector.scalar_tensor_tensor(out=xres[:, b, :], in0=xres[:, b, :], scalar=mv[:, b, 0:1],
                                                    in1=lng[:], op0=ALU.subtract, op1=ALU.mult))
                done()
                nc.vector.scalar_tensor_tensor(out=xres[:, b, :], in0=xres[:, b, :], scalar=rc[:, b:b + 1],
                                               in1=lnb[:], op0=ALU.mult, op1=ALU.add).then_inc(res_ready, 1)


def build(nc, ins, out):
    ctx = ExitStack()
    with ctx:
        def sb(name, shape, dt=F32):
            return ctx.enter_context(nc.sbuf_tensor(name, shape, dt))

        t = dict(ins)
        t["x2_d"] = nc.dram_tensor("x2_d", (TB, P, D), F32, kind="Internal").ap()
        t["sc_d"] = nc.dram_tensor("sc_d", (TB, P, NS * NK), F32, kind="Internal").ap()
        t["act_d"] = nc.dram_tensor("act_d", (TILES, P, DT), F32, kind="Internal").ap()
        t["gate_d"] = nc.dram_tensor("gate_d", (TILES, P, DT), F32, kind="Internal").ap()
        t["ident"] = sb("ident", [P, P])
        t["expert"], t["gate"], t["dn"] = sb("expert", [P, HK], U32), sb("gate", [P, PH, TOPK]), sb("dn", [P, HK])
        t["ps"] = ctx.enter_context(nc.psum_tensor("ps", [P, 8, HALF], F32))
        with ExitStack() as x2_scope:
            t["b_hi"] = x2_scope.enter_context(nc.sbuf_tensor("b_hi", [P, KC, S], F32R))
            t["b_lo"] = x2_scope.enter_context(nc.sbuf_tensor("b_lo", [P, KC, S], F32R))
            front_block(nc, t, ins["units"])
            scores_block(nc, t, ins["units"][FRONT_UNITS:])
            down_block(nc, t)
        up_block(nc, t, out)


def layout(x, mem, w_in, b_in, sgu_g, sgu_b, w_spatial, b_spatial, conv_w, w_mix_out, ln1_g, ln1_b, w_xq, w_xkv,
           w_xo, ln2_g, ln2_b, w_pq, sub_keys, w_down, w_up, ln3_g, ln3_b):
    import numpy as np
    c = np.ascontiguousarray

    def by_rows(w):
        return w.reshape(-1, P, D)

    def by_columns(w):
        return w.reshape(KC, P, -1, P).transpose(2, 1, 0, 3).reshape(-1, P, D)

    w = w_in[0]
    a = D // 2
    va = w[:, a:2 * a].reshape(4, 2, P, a).transpose(0, 2, 1, 3).reshape(4, P, D)
    h, gb, gc = (by_columns(w[:, 2 * a + i * a:2 * a + (i + 1) * a]) for i in range(3))
    conv = np.stack([h, gc, gb], 1).reshape(12, P, D)
    units = np.concatenate([by_rows(w_xkv[0][:, :D]), by_rows(w_xkv[0][:, D:]), va, conv, by_columns(w[:, :a]),
                            by_rows(w_mix_out[0]), by_columns(w_xq[0]), by_rows(w_xo[0]), by_columns(w_pq[0])])
    return {
        "units": units,
        "mem_t": c(mem[0].T.reshape(KC, P, M).transpose(1, 0, 2)),
        "x_t": c(x[0].T.reshape(KC, P, S).transpose(1, 0, 2)),
        "x_tok": c(x[0].reshape(TB, P, D).transpose(1, 0, 2)),
        "bcol": c(b_in[0].reshape(20, P).T),
        "cw": c(conv_w[0][:, 0].reshape(3, 4, P).transpose(2, 0, 1)),
        "wst": c(w_spatial[0].transpose(2, 0, 1)),
        "bias_va": c(b_in[0][a:2 * a]),
        "sgu_g": sgu_g[0].reshape(-1), "sgu_b": sgu_b[0].reshape(-1), "bsp": b_spatial[0].reshape(-1),
        "skt": c(sub_keys[0].reshape(NS, NK, P).transpose(2, 0, 1)),
        "iota": np.arange(P, dtype=np.float32),
        "down_t": c(w_down[0].reshape(NK, NK, KC, P).transpose(1, 3, 2, 0)).reshape(NK, P, D),
        "up_t": c(w_up[0].reshape(NK, NK, D).transpose(1, 0, 2)),
        "w_down": w_down[0], "w_up": w_up[0], "ln3_g": ln3_g[0], "ln3_b": ln3_b[0],
        "eye": np.eye(P, dtype=np.float32),
        "ln1_g": ln1_g[0], "ln1_b": ln1_b[0], "ln2_g": ln2_g[0], "ln2_b": ln2_b[0],
    }


def kernel(**inputs):
    import numpy as np
    import concourse.bacc as bacc
    from concourse.bass_utils import run_bass_kernel_spmd

    nc = bacc.Bacc("TRN2", target_bir_lowering=False, num_devices=1)
    arrays = {f"in_{k}": np.ascontiguousarray(v) for k, v in layout(**{k: np.asarray(v) for k, v in inputs.items()}).items()}
    ins = {k[3:]: nc.dram_tensor(k, v.shape, mybir.dt.from_np(v.dtype), kind="ExternalInput").ap()
           for k, v in arrays.items()}
    out = nc.dram_tensor("out", (1, S, D), F32, kind="ExternalOutput").ap()
    build(nc, ins, out)
    r = run_bass_kernel_spmd(nc, [arrays], core_ids=[0])
    return r.results[0]["out"]
```

```python
import concourse.bass as bass
from concourse import mybir
from contextlib import ExitStack

F32 = mybir.dt.float32
F32R = mybir.dt.float32r
BF16 = mybir.dt.bfloat16
F16 = mybir.dt.float16
U32 = mybir.dt.uint32
ALU = mybir.AluOpType
ACT = mybir.ActivationFunctionType
AX = mybir.AxisListType

P = 128
D = 1024
S = 512
M = 256
KC = D // P
TB = S // P
MB = M // P
AH = 4
XH = 4
XD = D // XH
PH = 8
NK = 128
NS = 2 * PH
TOPK = 16
EPS = 1e-5
ALPHA = 2.0 ** 0.25
HALF = D // 2
NEG = -3.0e38

U_K, U_VA, U_CONV, U_UA, U_MIX, U_V, U_XQ, U_XO, FRONT_UNITS = 0, 8, 12, 24, 28, 36, 44, 52, 60
LN1_ORDER = (2, 3, 0, 1)
RING = 4


class Count:

    def __init__(self, sem):
        self.sem, self.n = sem, 0

    def up(self, ins):
        ins.then_inc(self.sem, 1)
        self.n += 1
        return self.n


def held(eng, sem, value, passed):
    eng.wait_ge(sem, value)
    eng.sem_inc(passed, 1)


class Ring:

    def __init__(self, nc, ctx, name, t, units):
        self.nc, self.units, self.raw, self.w_hi, self.w_lo = nc, units, t["raw"], t["w_hi"], t["w_lo"]
        self.raw_full = [ctx.enter_context(nc.semaphore(f"{name}_raw_full{i}")) for i in range(RING)]
        self.hi_done = ctx.enter_context(nc.semaphore(f"{name}_hi_done"))
        self.split_done = ctx.enter_context(nc.semaphore(f"{name}_split_done"))

    def load_first(self, sp, s):
        sp.dma_start(self.raw[:, s, :], self.units[s]).then_inc(self.raw_full[s], 16)

    def high_first(self, act, s):
        act.wait_ge(self.raw_full[s], 16)
        self.nc.scalar.activation(self.w_hi[:, s, :], self.raw[:, s, :], ACT.Copy).then_inc(self.hi_done, 1)

    def low_first(self, pool, s):
        pool.wait_ge(self.hi_done, s + 1)
        self.nc.gpsimd.tensor_tensor(self.w_lo[:, s, :], self.raw[:, s, :], self.w_hi[:, s, :].bitcast(F32),
                                     ALU.subtract).then_inc(self.split_done, 1)


def front_block(nc, t, units, ring, next_ring):
    b_hi, b_lo, ps, ident = t["b_hi"], t["b_lo"], t["ps"], t["ident"]
    ctx = ExitStack()
    with ctx:
        def sb(name, shape, dt=F32):
            return ctx.enter_context(nc.sbuf_tensor(name, shape, dt))

        def sem(name):
            return ctx.enter_context(nc.semaphore(name))

        raw, w_hi, w_lo, raw_full, hi_done, split_done = (
            ring.raw, ring.w_hi, ring.w_lo, ring.raw_full, ring.hi_done, ring.split_done)
        xt_raw = sb("xt_raw", [P, KC, S])
        xres = sb("xres", [P, TB, D])
        a_hi = sb("a_hi", [P, KC, S], F32R)
        a_lo = sb("a_lo", [P, KC, S], F32R)
        kt = sb("kt", [P, KC, M])
        v_hi = sb("v_hi", [P, MB, D], F32R)
        v_lo = sb("v_lo", [P, MB, D], F32R)
        tok = sb("tok", [P, TB, HALF])
        lng = sb("lng", [P, D])
        lnb = sb("lnb", [P, D])
        bias_va = sb("bias_va", [P, HALF])
        sgu_g = sb("sgu_g", [P, HALF])
        sgu_b = sb("sgu_b", [P, HALF])
        bsp = sb("bsp", [P, AH, P])
        bcol = sb("bcol", [P, 20])
        cw = sb("cw", [P, 3, 4])
        wst = sb("wst", [P, AH, P])
        zc = sb("zc", [P, S + 2])
        bst = sb("bst", [P, 16, 6])
        mv = sb("mv", [P, 16, 2])
        vc = sb("vc", [P, 16])
        sd = sb("sd", [P, 16])
        rc = sb("rc", [P, 16])
        nt = sb("nt", [P, 2, 16])
        mx = sb("mx", [P, TB, XH])
        nmx = sb("nmx", [P, TB, XH])
        sm = sb("sm", [P, TB, XH])
        rs = sb("rs", [P, TB, XH])

        probs = tok[:].rearrange("p a b -> p (a b)").rearrange("p (m h j) -> p m h j", m=2, h=XH)
        mem_t_hi, mem_t_lo = (x[:].rearrange("p m d -> p (m d)").rearrange("p (c m) -> p c m", c=KC)
                              for x in (v_hi, v_lo))
        u_t = xt_raw[:, 0:4, :]
        h_t, c_t = xt_raw[:, 4, :], xt_raw[:, 5, :]
        y_t = xt_raw[:, 6:8, :]
        q_t = xt_raw

        unit_done = sem("unit_done")
        mem_full, x_full, xres_full, par_full, ln1_full, ln2_full = (
            sem("mem_full"), sem("x_full"), sem("xres_full"), sem("par_full"), sem("ln1_full"), sem("ln2_full"))
        block_done, res_added = sem("block_done"), sem("res_added")
        mem_hi, mem_split, x_hi, x_split = sem("mem_hi"), sem("mem_split"), sem("x_hi"), sem("x_split")
        kt_done = sem("kt_done")
        vhi_done, v_done = sem("vhi_done"), sem("v_done")
        ws_ready = sem("ws_ready")
        va_in, va_gelu, va_ready = sem("va_in"), sem("va_gelu"), sem("va_ready")
        z_read, y_made, yhi_done, y_split = sem("z_read"), sem("y_made"), sem("yhi_done"), sem("y_split")
        u_ready, mix_done, mix_read = sem("u_ready"), sem("mix_done"), sem("mix_read")
        var_ready, sd_ready = sem("var_ready"), sem("sd_ready")
        x1_ready, x1_tr, x1_hi, x1_split = sem("x1_ready"), sem("x1_tr"), sem("x1_hi"), sem("x1_split")
        q_ready, sc_done, mx_ready, exp_done, p_ready = (
            sem("q_ready"), sem("sc_done"), sem("mx_ready"), sem("exp_done"), sem("p_ready"))
        p_tr, p_hi, p_split = sem("p_tr"), sem("p_hi"), sem("p_split")
        o_done, o_hi, o_split = sem("o_done"), sem("o_hi"), sem("o_split")
        x2_ready, x2_tr, x2_hi, x2_split = sem("x2_ready"), sem("x2_tr"), sem("x2_hi"), sem("x2_split")
        dve_step = sem("dve_step")
        passed_pool = sem("passed_pool")
        block = ctx.enter_context(nc.Block())

        @block.sync
        def _(sp):
            sp.dma_start(kt[:], t["mem_t"]).then_inc(mem_full, 16)
            for u in range(RING):
                sp.dma_start(raw[:, u, :], units[u]).then_inc(raw_full[u], 16)
            sp.dma_start(xt_raw[:], t["x_t"]).then_inc(x_full, 16)
            with sp.Fori(1, FRONT_UNITS // RING) as r:
                for s in range(RING):
                    sp.wait_ge(split_done, RING * r + (s + 1 - RING))
                    sp.dma_start(raw[:, s, :], units[bass.ds(RING * r + s, 1)].rearrange("o p n -> (o p) n")
                                 ).then_inc(raw_full[s], 16)
            sp.wait_ge(x1_ready, TB)
            sp.dma_start(lng[:], t["ln2_g"].partition_broadcast(P)).then_inc(ln2_full, 16)
            sp.dma_start(lnb[:], t["ln2_b"].partition_broadcast(P)).then_inc(ln2_full, 16)
            for s in range(RING):
                sp.wait_ge(split_done, FRONT_UNITS + (s + 1 - RING))
                next_ring.load_first(sp, s)
            sp.wait_ge(x2_ready, TB)
            sp.dma_start(t["x2_d"].rearrange("b p d -> p b d"), xres[:]).then_inc(t["x2_stored"], 16)

        @block.gpsimd
        def _(pool):
            def split_low(r, s):
                u = RING * r + s
                held(pool, hi_done, u + 1, passed_pool)
                nc.gpsimd.tensor_tensor(w_lo[:, s, :], raw[:, s, :], w_hi[:, s, :].bitcast(F32),
                                        ALU.subtract).then_inc(split_done, 1)

            with pool.Fori(0, U_VA // RING) as r:
                for s in range(RING):
                    split_low(r, s)
            pool.wait_ge(par_full, 16 * 8)
            nc.gpsimd.affine_select(out=wst[:], in_=wst[:], pattern=[[0, AH], [1, P]], compare_op=ALU.is_ge,
                                    fill=0.0, base=0, channel_multiplier=-1).then_inc(ws_ready, 1)
            with pool.Fori(U_VA // RING, FRONT_UNITS // RING) as r:
                for s in range(RING):
                    split_low(r, s)
            for s in range(RING):
                pool.wait_ge(unit_done, FRONT_UNITS + (s + 1 - RING))
                next_ring.low_first(pool, s)

        @block.scalar
        def _(act):
            highs = iter(range(FRONT_UNITS))

            def high_parts(until):
                for u in highs:
                    s = u % RING
                    act.wait_ge(raw_full[s], 16 * (u // RING) + 16)
                    if u >= RING:
                        act.wait_ge(unit_done, u - RING + 1)
                    nc.scalar.activation(w_hi[:, s, :], raw[:, s, :], ACT.Copy).then_inc(hi_done, 1)
                    if u + 1 == until:
                        return

            act.wait_ge(mem_full, 16)
            nc.scalar.activation(mem_t_hi, kt[:], ACT.Copy).then_inc(mem_hi, 1)
            high_parts(RING)
            act.wait_ge(x_full, 16)
            nc.scalar.activation(a_hi[:], xt_raw[:], ACT.Copy).then_inc(x_hi, 1)
            act.dma_start(bcol[:], t["bcol"]).then_inc(par_full, 16)
            act.dma_start(cw[:], t["cw"]).then_inc(par_full, 16)
            act.dma_start(wst[:], t["wst"]).then_inc(par_full, 16)
            act.dma_start(bias_va[:], t["bias_va"].partition_broadcast(P)).then_inc(par_full, 16)
            act.dma_start(sgu_g[:], t["sgu_g"].partition_broadcast(P)).then_inc(par_full, 16)
            act.dma_start(sgu_b[:], t["sgu_b"].partition_broadcast(P)).then_inc(par_full, 16)
            act.dma_start(bsp[:].rearrange("p h t -> p (h t)"), t["bsp"].partition_broadcast(P)).then_inc(par_full, 16)
            act.dma_start(ident[:], t["eye"]).then_inc(par_full, 16)
            high_parts(U_VA + RING)
            act.dma_start(xres[:], t["x_tok"]).then_inc(xres_full, 16)
            act.dma_start(lng[:], t["ln1_g"].partition_broadcast(P)).then_inc(ln1_full, 16)
            act.dma_start(lnb[:], t["ln1_b"].partition_broadcast(P)).then_inc(ln1_full, 16)
            high_parts(U_VA + 4 + RING)
            for b in range(TB):
                act.wait_ge(va_in, b + 1)
                nc.scalar.activation(tok[:, b, :], tok[:, b, :], ACT.Gelu).then_inc(va_gelu, 1)
            act.wait_ge(var_ready, 1)
            nc.scalar.activation(sd[:], vc[:], ACT.Sqrt).then_inc(sd_ready, 1)
            for j in range(4):
                high_parts(U_CONV + 3 * (j + 1) + RING)
                act.wait_ge(z_read, 3 * j + 3)
                nc.scalar.activation(b_hi[:, 4 + j, :], y_t[:, j % 2, :], ACT.Copy).then_inc(yhi_done, 1)
            for j in range(4):
                high_parts(U_UA + j + 1 + RING)
                act.wait_ge(unit_done, U_UA + j + 1)
                nc.scalar.activation(u_t[:, j, :], ps[:, 4 + j, :], ACT.Gelu,
                                     bias=bcol[:, j:j + 1]).then_inc(u_ready, 1)
            for j in range(4):
                act.wait_ge(y_made, j + 1)
                nc.scalar.activation(b_hi[:, j, :], y_t[:, j % 2, :], ACT.Copy).then_inc(yhi_done, 1)
            high_parts(U_MIX + KC + RING + 2)
            act.wait_ge(var_ready, 2)
            nc.scalar.activation(sd[:, 0:TB], vc[:, 0:TB], ACT.Sqrt).then_inc(sd_ready, 1)
            high_parts(U_V + KC + RING)
            for b in range(TB):
                act.wait_ge(x1_tr, b + 1)
                nc.scalar.activation(a_hi[:, :, b * P:(b + 1) * P],
                                     ps[:, 2 * (b % 2):2 * (b % 2) + 2, :].rearrange("p a (c j) -> p (a c) j", j=P),
                                     ACT.Copy).then_inc(x1_hi, 1)
            for m in range(MB):
                nc.scalar.activation(v_hi[:, m, :], ps[:, 4 + 2 * m:6 + 2 * m, :], ACT.Copy).then_inc(vhi_done, 1)
            for e in range(KC):
                high_parts(U_XQ + e + 1 + RING)
                act.wait_ge(unit_done, U_XQ + e + 1)
                nc.scalar.activation(q_t[:, e, :], ps[:, e, :], ACT.Copy).then_inc(q_ready, 1)

            def probs_high(b):
                act.wait_ge(p_tr, b + 1)
                nc.scalar.activation(b_hi[:, :, b * P:(b + 1) * P],
                                     ps[:, 2 * b:2 * b + 2, :].rearrange("p a (c j) -> p (a c) j", j=P),
                                     ACT.Copy).then_inc(p_hi, 1)

            for b in range(TB):
                act.wait_ge(mx_ready, b + 1)
                if b >= 2:
                    act.wait_ge(p_tr, b - 1)
                for h in range(XH):
                    nc.scalar.activation(probs[:, b % 2, h, :],
                                         ps[:, 2 * b + h // 2, (h % 2) * M:(h % 2 + 1) * M], ACT.Exp,
                                         bias=nmx[:, b, h:h + 1], scale=XD ** -0.5,
                                         accum_out=sm[:, b, h:h + 1]).then_inc(exp_done, 1)
                if b >= 1:
                    probs_high(b - 1)
            probs_high(TB - 1)
            for e in range(KC):
                act.wait_ge(o_done, e + 1)
                nc.scalar.activation(a_hi[:, e, :], ps[:, e, :], ACT.Copy).then_inc(o_hi, 1)
            high_parts(FRONT_UNITS)
            for s in range(RING):
                act.wait_ge(unit_done, FRONT_UNITS + (s + 1 - RING))
                next_ring.high_first(act, s)
            act.wait_ge(var_ready, 3)
            nc.scalar.activation(sd[:, 0:TB], vc[:, 0:TB], ACT.Sqrt).then_inc(sd_ready, 1)
            for b in range(TB):
                act.wait_ge(x2_tr, b + 1)
                nc.scalar.activation(b_hi[:, :, b * P:(b + 1) * P],
                                     ps[:, 2 * b:2 * b + 2, :].rearrange("p a (c j) -> p (a c) j", j=P),
                                     ACT.Copy).then_inc(x2_hi, 1)

        @block.tensor
        def _(pe):
            def mm3(out, l_hi, l_lo, r_hi, r_lo, start, stop):
                nc.tensor.matmul(out, l_hi, r_hi, start=start, stop=False)
                nc.tensor.matmul(out, l_hi, r_lo, start=False, stop=False)
                return nc.tensor.matmul(out, l_lo, r_hi, start=False, stop=stop)

            def by_token(u0, n, banks, x_hi_, x_lo_, order, first=0, part_ready=None, blockwise=False):
                for i in range(n):
                    k = (first + i) % n
                    pe.wait_ge(split_done, u0 + i + 1)
                    if part_ready is not None:
                        pe.wait_ge(part_ready, i + 1)
                    s = (u0 + i) % RING
                    for b in order:
                        for h in range(2):
                            c, tk = slice(h * HALF, (h + 1) * HALF), slice(b * P, (b + 1) * P)
                            last = mm3(ps[:, banks + 2 * b + h, :], x_hi_[:, k, tk], x_lo_[:, k, tk],
                                       w_hi[:, s, c], w_lo[:, s, c], i == 0, i == n - 1)
                        if blockwise and i == n - 1 and b != order[-1]:
                            last.then_inc(block_done, 1)
                    last.then_inc(unit_done, 1)

            def by_channel(u, bank, x_hi_, x_lo_, tokens=S):
                pe.wait_ge(split_done, u + 1)
                s = u % RING
                for k in range(KC):
                    c = slice(k * P, (k + 1) * P)
                    last = mm3(ps[:, bank, 0:tokens], w_hi[:, s, c], w_lo[:, s, c], x_hi_[:, k, :], x_lo_[:, k, :],
                               k == 0, k == KC - 1)
                last.then_inc(unit_done, 1)

            pe.wait_ge(mem_split, 1)
            for e in range(KC):
                by_channel(U_K + e, e, mem_t_hi, mem_t_lo, M)
            pe.wait_ge(x_split, 1)
            pe.wait_ge(kt_done, 4)
            for u in range(4):
                pe.wait_ge(split_done, U_VA + u + 1)
                s = (U_VA + u) % RING
                for i in range(2):
                    k = 2 * u + i
                    c = slice(i * HALF, (i + 1) * HALF)
                    for b in range(TB):
                        tk = slice(b * P, (b + 1) * P)
                        last = mm3(ps[:, b, :], a_hi[:, k, tk], a_lo[:, k, tk], w_hi[:, s, c], w_lo[:, s, c],
                                   k == 0, k == KC - 1)
                last.then_inc(unit_done, 1)
            pe.wait_ge(kt_done, KC)
            for u in range(12):
                if u >= 4:
                    pe.wait_ge(z_read, u - 3)
                by_channel(U_CONV + u, 4 + u % 4, a_hi, a_lo)
            pe.wait_ge(ws_ready, 1)
            pe.wait_ge(va_ready, 1)
            for h in range(AH):
                for b in range(TB):
                    last = nc.tensor.matmul(ps[:, h, b * P:(b + 1) * P], tok[:, b, h * P:(h + 1) * P], wst[:, h, :],
                                            start=b == 0, stop=b == TB - 1, skip_group_check=True)
                last.then_inc(mix_done, 1)
            for u in range(4):
                pe.wait_ge(z_read, 8 + u + 1)
                by_channel(U_UA + u, 4 + u, a_hi, a_lo)
            pe.wait_ge(mix_read, 4)
            pe.wait_ge(u_ready, 4)
            by_token(U_MIX, KC, 0, b_hi, b_lo, LN1_ORDER, first=KC // 2, part_ready=y_split, blockwise=True)
            pe.wait_ge(res_added, 4)
            by_token(U_V, KC, 4, mem_t_hi, mem_t_lo, range(MB))
            pe.wait_ge(par_full, 16 * 8)
            for b in range(TB):
                pe.wait_ge(x1_ready, b + 1)
                if b >= 2:
                    pe.wait_ge(x1_split, b - 1)
                for e in range(KC):
                    last = nc.tensor.transpose(ps[:, 2 * (b % 2) + e // 4, (e % 4) * P:(e % 4 + 1) * P],
                                               xres[:, b, e * P:(e + 1) * P], ident[:])
                last.then_inc(x1_tr, 1)
            pe.wait_ge(x1_split, TB)
            for e in range(KC):
                if e == 4:
                    pe.wait_ge(v_done, MB)
                by_channel(U_XQ + e, e, a_hi, a_lo)

            def scores(b):
                for h in range(XH):
                    for c in range(2):
                        last = nc.tensor.matmul(ps[:, 2 * b + h // 2, (h % 2) * M:(h % 2 + 1) * M],
                                                q_t[:, 2 * h + c, b * P:(b + 1) * P], kt[:, 2 * h + c, :],
                                                start=c == 0, stop=c == 1)
                last.then_inc(sc_done, 1)

            def turn_probs(b):
                pe.wait_ge(p_ready, b + 1)
                for h in range(XH):
                    for m in range(MB):
                        i = MB * h + m
                        last = nc.tensor.transpose(ps[:, 2 * b + i // 4, (i % 4) * P:(i % 4 + 1) * P],
                                                   probs[:, b % 2, h, m * P:(m + 1) * P], ident[:])
                last.then_inc(p_tr, 1)

            pe.wait_ge(q_ready, KC)
            scores(0)
            scores(1)
            for b in range(2, TB):
                scores(b)
                turn_probs(b - 2)
            turn_probs(TB - 2)
            turn_probs(TB - 1)
            pe.wait_ge(p_split, TB)
            for e in range(KC):
                for m in range(MB):
                    i = MB * (e // 2) + m
                    c = slice(e * P, (e + 1) * P)
                    last = mm3(ps[:, e, :], v_hi[:, m, c], v_lo[:, m, c], b_hi[:, i, :], b_lo[:, i, :],
                               m == 0, m == MB - 1)
                last.then_inc(o_done, 1)
            pe.wait_ge(o_split, KC)
            by_token(U_XO, KC, 0, a_hi, a_lo, range(TB), blockwise=True)
            for b in range(TB):
                pe.wait_ge(x2_ready, b + 1)
                for e in range(KC):
                    last = nc.tensor.transpose(ps[:, 2 * b + e // 4, (e % 4) * P:(e % 4 + 1) * P],
                                               xres[:, b, e * P:(e + 1) * P], ident[:])
                last.then_inc(x2_tr, 1)

        @block.vector
        def _(dve):
            step, added = Count(dve_step), Count(res_added)

            def done():
                dve.wait_ge(dve_step, step.n)

            def inv_std(n, turn):
                done()
                nc.vector.tensor_scalar(vc[:, 0:n], mv[:, 0:n, 1], EPS, None, ALU.add).then_inc(var_ready, 1)
                dve.wait_ge(sd_ready, turn)
                step.up(nc.vector.reciprocal(rc[:, 0:n], sd[:, 0:n]))
                done()
                step.up(nc.vector.tensor_tensor(nt[:, 0, 0:n], rc[:, 0:n], rc[:, 0:n], ALU.mult))
                done()
                step.up(nc.vector.tensor_tensor(nt[:, 1, 0:n], nt[:, 0, 0:n], vc[:, 0:n], ALU.mult))
                done()
                step.up(nc.vector.tensor_scalar(nt[:, 0, 0:n], nt[:, 1, 0:n], -0.5, 1.5, ALU.mult, ALU.add))
                done()
                step.up(nc.vector.tensor_tensor(rc[:, 0:n], rc[:, 0:n], nt[:, 0, 0:n], ALU.mult))
                done()

            def layer_norm(u0, full, turn, ready, order):
                def statistics(b, ready):
                    dve.wait_ge(res_added, ready)
                    for h in range(2):
                        step.up(nc.vector.bn_stats(bst[:, 2 * b + h, :], xres[:, b, h * HALF:(h + 1) * HALF]))

                for i, b in enumerate(order):
                    if i < TB - 1:
                        dve.wait_ge(block_done, (TB - 1) * (turn - 2) + i + 1)
                    else:
                        dve.wait_ge(unit_done, u0 + KC)
                    for h in range(2):
                        c = slice(h * HALF, (h + 1) * HALF)
                        added.up(nc.vector.scalar_tensor_tensor(out=xres[:, b, c], in0=xres[:, b, c], scalar=ALPHA,
                                                                in1=ps[:, 2 * b + h, :], op0=ALU.mult, op1=ALU.add))
                    if i:
                        statistics(order[i - 1], added.n - 2)
                statistics(order[-1], added.n)
                done()
                for b in range(TB):
                    step.up(nc.vector.bn_aggr(mv[:, b, :], bst[:, 2 * b:2 * b + 2, :]))
                inv_std(TB, turn)
                dve.wait_ge(full, 32)
                for b in range(TB):
                    step.up(nc.vector.scalar_tensor_tensor(out=xres[:, b, :], in0=xres[:, b, :], scalar=mv[:, b, 0:1],
                                                           in1=lng[:], op0=ALU.subtract, op1=ALU.mult))
                    done()
                    nc.vector.scalar_tensor_tensor(out=xres[:, b, :], in0=xres[:, b, :], scalar=rc[:, b:b + 1],
                                                   in1=lnb[:], op0=ALU.mult, op1=ALU.add).then_inc(ready, 1)

            def low_part(lo_, hi_, src, sem_):
                nc.vector.tensor_tensor(lo_, src, hi_.bitcast(F32), ALU.subtract).then_inc(sem_, 1)

            dve.wait_ge(mem_hi, 1)
            low_part(mem_t_lo, mem_t_hi, kt[:], mem_split)
            dve.wait_ge(x_hi, 1)
            low_part(a_lo[:], a_hi[:], xt_raw[:], x_split)
            dve.wait_ge(mem_split, 1)
            for e in range(KC):
                dve.wait_ge(unit_done, U_K + e + 1)
                nc.vector.tensor_copy(kt[:, e, :], ps[:, e, 0:M]).then_inc(kt_done, 1)
            dve.wait_ge(par_full, 16 * 8)
            dve.wait_ge(unit_done, U_VA + 4)
            for b in range(TB):
                nc.vector.tensor_tensor(tok[:, b, :], ps[:, b, :], bias_va[:], ALU.add).then_inc(va_in, 1)
            for b in range(TB):
                dve.wait_ge(va_gelu, b + 1)
                for h in range(AH):
                    step.up(nc.vector.bn_stats(bst[:, AH * b + h, :], tok[:, b, h * P:(h + 1) * P]))
            done()
            for i in range(16):
                step.up(nc.vector.bn_aggr(mv[:, i, :], bst[:, i, :]))
            inv_std(16, 1)
            for b in range(TB):
                for h in range(AH):
                    i = AH * b + h
                    c = slice(h * P, (h + 1) * P)
                    step.up(nc.vector.tensor_scalar(tok[:, b, c], tok[:, b, c], mv[:, i, 0:1], rc[:, i:i + 1],
                                                    ALU.subtract, ALU.mult))
            done()
            step.up(nc.vector.tensor_tensor(tok[:], tok[:], sgu_g[:].unsqueeze(1).broadcast_to([P, TB, HALF]), ALU.mult))
            done()
            nc.vector.tensor_tensor(tok[:], tok[:], sgu_b[:].unsqueeze(1).broadcast_to([P, TB, HALF]),
                                    ALU.add).then_inc(va_ready, 1)
            step.up(nc.vector.memset(zc[:, 0:2], 0.0))
            dve.wait_ge(x_split, 1)

            def y_low(n):
                dve.wait_ge(yhi_done, n + 1)
                low_part(b_lo[:, (4 + n) % 8, :], b_hi[:, (4 + n) % 8, :], y_t[:, n % 2, :], y_split)

            for j in range(4):
                dve.wait_ge(unit_done, U_CONV + 3 * j + 1)
                if j:
                    dve.wait_ge(z_read, 3 * j)
                nc.vector.tensor_scalar(h_t, ps[:, 4 + 3 * j % 4, :], bcol[:, 8 + j:9 + j], None,
                                        ALU.add).then_inc(z_read, 1)
                dve.wait_ge(z_read, 3 * j + 1)
                dve.wait_ge(unit_done, U_CONV + 3 * j + 2)
                nc.vector.scalar_tensor_tensor(out=zc[:, 2:], in0=ps[:, 4 + (3 * j + 1) % 4, :],
                                               scalar=bcol[:, 16 + j:17 + j], in1=h_t,
                                               op0=ALU.add, op1=ALU.mult).then_inc(z_read, 1)
                dve.wait_ge(z_read, 3 * j + 2)
                done()
                step.up(nc.vector.tensor_scalar(c_t, zc[:, 0:S], cw[:, 0, j:j + 1], None, ALU.mult))
                for k in (1, 2):
                    done()
                    step.up(nc.vector.scalar_tensor_tensor(out=c_t, in0=zc[:, k:k + S], scalar=cw[:, k, j:j + 1],
                                                           in1=c_t, op0=ALU.mult, op1=ALU.add))
                done()
                if j >= 2:
                    dve.wait_ge(y_split, j - 1)
                dve.wait_ge(unit_done, U_CONV + 3 * j + 3)
                nc.vector.scalar_tensor_tensor(out=y_t[:, j % 2, :], in0=ps[:, 4 + (3 * j + 2) % 4, :],
                                               scalar=bcol[:, 12 + j:13 + j], in1=c_t,
                                               op0=ALU.add, op1=ALU.mult).then_inc(z_read, 1)
                dve.wait_ge(z_read, 3 * j + 3)
                if j:
                    y_low(j - 1)
            y_low(3)
            dve.wait_ge(mix_done, AH)
            for h in range(AH):
                nc.vector.tensor_tensor(tok[:, h, :].rearrange("p (b j) -> p b j", b=TB),
                                        ps[:, h, :].rearrange("p (b j) -> p b j", b=TB),
                                        bsp[:, h, :].unsqueeze(1).broadcast_to([P, TB, P]), ALU.add).then_inc(mix_read, 1)
            for h in range(AH):
                dve.wait_ge(mix_read, h + 1)
                dve.wait_ge(u_ready, h + 1)
                dve.wait_ge(y_split, 4 + h - 1)
                nc.vector.tensor_tensor(y_t[:, h % 2, :], u_t[:, h, :], tok[:, h, :], ALU.mult).then_inc(y_made, 1)
                dve.wait_ge(y_made, h + 1)
                if h:
                    y_low(4 + h - 1)
            y_low(7)
            dve.wait_ge(xres_full, 16)
            layer_norm(U_MIX, ln1_full, 2, x1_ready, LN1_ORDER)
            for b in range(TB):
                dve.wait_ge(x1_hi, b + 1)
                tk = slice(b * P, (b + 1) * P)
                low_part(a_lo[:, :, tk], a_hi[:, :, tk],
                         ps[:, 2 * (b % 2):2 * (b % 2) + 2, :].rearrange("p a (c j) -> p (a c) j", j=P), x1_split)
            for m in range(MB):
                dve.wait_ge(vhi_done, m + 1)
                low_part(v_lo[:, m, :].rearrange("p (a n) -> p a n", a=2), v_hi[:, m, :].rearrange("p (a n) -> p a n", a=2),
                         ps[:, 4 + 2 * m:6 + 2 * m, :], v_done)

            def probs_low(b):
                dve.wait_ge(p_hi, b + 1)
                tk = slice(b * P, (b + 1) * P)
                low_part(b_lo[:, :, tk], b_hi[:, :, tk],
                         ps[:, 2 * b:2 * b + 2, :].rearrange("p a (c j) -> p (a c) j", j=P), p_split)

            def row_max(b):
                dve.wait_ge(sc_done, b + 1)
                step.up(nc.vector.tensor_reduce(mx[:, b, :],
                                                ps[:, 2 * b:2 * b + 2, :].rearrange("p a (c j) -> p (a c) j", j=M),
                                                AX.X, ALU.max))
                done()
                nc.vector.tensor_scalar(nmx[:, b, :], mx[:, b, :], -(XD ** -0.5), None, ALU.mult).then_inc(mx_ready, 1)

            row_max(0)
            row_max(1)
            for b in range(TB):
                dve.wait_ge(exp_done, XH * (b + 1))
                step.up(nc.vector.reciprocal(rs[:, b, :], sm[:, b, :]))
                done()
                for h in range(XH):
                    nc.vector.tensor_scalar(probs[:, b % 2, h, :], probs[:, b % 2, h, :], rs[:, b, h:h + 1], None,
                                            ALU.mult).then_inc(*((p_ready, 1) if h == XH - 1 else (dve_step, 1)))
                    step.n += h < XH - 1
                if b + 2 < TB:
                    row_max(b + 2)
                if b >= 1:
                    probs_low(b - 1)
            probs_low(TB - 1)
            for e in range(KC):
                dve.wait_ge(o_hi, e + 1)
                low_part(a_lo[:, e, :], a_hi[:, e, :], ps[:, e, :], o_split)
            layer_norm(U_XO, ln2_full, 3, x2_ready, range(TB))
            for b in range(TB):
                dve.wait_ge(x2_hi, b + 1)
                tk = slice(b * P, (b + 1) * P)
                low_part(b_lo[:, :, tk], b_hi[:, :, tk],
                         ps[:, 2 * b:2 * b + 2, :].rearrange("p a (c j) -> p (a c) j", j=P), x2_split)


def top_subkeys(nc, k, step, done, s, scores):
    best, place, rest = k["best"], k["place"], k["rest"]
    for b in range(TB):
        step(nc.vector.max(best[:, s, b, 0:8], scores[:, b, :]))
    done()
    for b in range(TB):
        step(nc.vector.max_index(place[:, s, b, 0:8], best[:, s, b, 0:8], scores[:, b, :]))
        step(nc.vector.match_replace(rest[:, b, :], best[:, s, b, 0:8], scores[:, b, :], NEG))
    done()
    for b in range(TB):
        step(nc.vector.max(best[:, s, b, 8:16], rest[:, b, :]))
    done()
    for b in range(TB):
        step(nc.vector.max_index(place[:, s, b, 8:16], best[:, s, b, 8:16], rest[:, b, :]))


def top_experts(nc, step, done, k, b, between):
    top, flat, fi, fif, ab = k["top"], k["flat"], k["fi"], k["fif"], k["ab"]
    c0, c1 = k["c0"], k["c1"]
    vs, isd = (x[:, bass.ds(b, 1)].rearrange("p o (h s) i -> p (o h) s i", s=2) for x in (k["v16"], k["i16"]))
    shape = [P, PH, TOPK, TOPK]
    step(nc.vector.tensor_tensor(c0.rearrange("p h (i j) -> p h i j", i=TOPK),
                                 vs[:, :, 0, :].unsqueeze(3).broadcast_to(shape),
                                 vs[:, :, 1, :].unsqueeze(2).broadcast_to(shape), ALU.add))
    done()
    for h in range(PH):
        step(nc.vector.max(top[:, h, 0:8], c0[:, h, :]))
    done()
    for h in range(PH):
        step(nc.vector.max_index(flat[:, h, 0:8], top[:, h, 0:8], c0[:, h, :]))
        step(nc.vector.match_replace(c1[:, h, :], top[:, h, 0:8], c0[:, h, :], NEG))
    done()
    for h in range(PH):
        step(nc.vector.max(top[:, h, 8:16], c1[:, h, :]))
        if h % 4 == 3:
            between()
    done()
    nc.vector.tensor_tensor(k["ex"][:], top[:], top[:, :, 0:1].broadcast_to([P, PH, TOPK]),
                            ALU.subtract).then_inc(k["exp_in"], 1)
    for h in range(PH):
        step(nc.vector.max_index(flat[:, h, 8:16], top[:, h, 8:16], c1[:, h, :]))
        if h % 4 == 3:
            between()
    done()
    step(nc.vector.tensor_single_scalar(fi[:, 0], flat[:], 4, ALU.logical_shift_right))
    step(nc.vector.tensor_single_scalar(fi[:, 1], flat[:], TOPK - 1, ALU.bitwise_and))
    done()
    step(nc.vector.tensor_copy(fif[:], fi[:]))
    done()
    pk = [x.rearrange("p h (k i) -> p h k i", k=TOPK) for x in (c0, c1)]
    for side in range(2):
        step(nc.vector.tensor_tensor(pk[side], fif[:, side].unsqueeze(3).broadcast_to(shape),
                                     k["iota"][:, 0:TOPK].unsqueeze(1).unsqueeze(1).broadcast_to(shape), ALU.is_equal))
    done()
    for side in range(2):
        step(nc.vector.tensor_tensor(pk[side], pk[side], isd[:, :, side, :].unsqueeze(2).broadcast_to(shape), ALU.mult))
    done()
    for side in range(2):
        step(nc.vector.tensor_reduce(ab[:, side], pk[side], AX.X, ALU.add))
    done()


def gates(nc, step, done, k, out):
    step(nc.vector.tensor_reduce(k["gsum"][:], k["ex"][:], AX.X, ALU.add))
    done()
    step(nc.vector.reciprocal(k["gsum"][:], k["gsum"][:]))
    done()
    step(nc.vector.tensor_tensor(out, k["ex"][:], k["gsum"][:].unsqueeze(2).broadcast_to([P, PH, TOPK]), ALU.mult))


def scores_block(nc, t, units, ring, next_ring):
    b_hi, b_lo, ps = t["b_hi"], t["b_lo"], t["ps"]
    ctx = ExitStack()
    with ctx:
        def sb(name, shape, dt=F32):
            return ctx.enter_context(nc.sbuf_tensor(name, shape, dt))

        def sem(name):
            return ctx.enter_context(nc.semaphore(name))

        raw, w_hi, w_lo, raw_full, hi_done, split_done = (
            ring.raw, ring.w_hi, ring.w_lo, ring.raw_full, ring.hi_done, ring.split_done)
        sc = sb("sc", [P, RING, TB, NK])
        k = {"best": sb("best", [P, RING, TB, TOPK]), "place": sb("place", [P, RING, TB, TOPK], U32),
             "rest": sb("rest", [P, TB, NK])}
        skt = sb("skt", [P, NS, NK])
        qs = sb("qs", [P, RING, S])
        skt_full = sem("skt_full")
        unit_done = sem("unit2_done")
        qs_ready, ss_done, sc_ready = sem("qs_ready"), sem("ss_done"), sem("sc_ready")
        passed_pool, passed_dve = sem("passed_pool2"), sem("passed_dve2")
        dve_step = sem("dve2_step")
        rounds = NS // RING
        block = ctx.enter_context(nc.Block())

        @block.sync
        def _(sp):
            sp.wait_ge(t["x2_stored"], 16)
            sp.dma_start(skt[:], t["skt"]).then_inc(skt_full, 16)
            with sp.Fori(1, rounds) as r:
                for s in range(RING):
                    sp.wait_ge(split_done, RING * r + (s + 1 - RING))
                    sp.dma_start(raw[:, s, :], units[bass.ds(RING * r + s, 1)].rearrange("o p n -> (o p) n")
                                 ).then_inc(raw_full[s], 16)
            for s in range(RING):
                sp.wait_ge(split_done, NS + (s + 1 - RING))
                next_ring.load_first(sp, s)
            for s in range(RING):
                sp.wait_ge(next_ring.split_done, s + 1)
                sp.dma_start(raw[:, s, :], next_ring.units[RING + s]).then_inc(next_ring.raw_full[s], 16)

        @block.gpsimd
        def _(pool):
            def split_low(r, s):
                u = RING * r + s
                held(pool, hi_done, u + 1, passed_pool)
                nc.gpsimd.tensor_tensor(w_lo[:, s, :], raw[:, s, :], w_hi[:, s, :].bitcast(F32),
                                        ALU.subtract).then_inc(split_done, 1)

            with pool.Fori(1, rounds) as r:
                for s in range(RING):
                    split_low(r, s)
            for s in range(RING):
                pool.wait_ge(unit_done, NS + (s + 1 - RING))
                next_ring.low_first(pool, s)

        @block.tensor
        def _(pe):
            def queries(r, s):
                u = RING * r + s
                pe.wait_ge(split_done, u + 1)
                for k in range(KC):
                    c = slice(k * P, (k + 1) * P)
                    nc.tensor.matmul(ps[:, s, :], w_hi[:, s, c], b_hi[:, k, :], start=k == 0, stop=False)
                    nc.tensor.matmul(ps[:, s, :], w_hi[:, s, c], b_lo[:, k, :], start=False, stop=False)
                    last = nc.tensor.matmul(ps[:, s, :], w_lo[:, s, c], b_hi[:, k, :], start=False, stop=k == KC - 1)
                last.then_inc(unit_done, 1)

            def scores(r, s, first=False):
                u = RING * r + s
                pe.wait_ge(qs_ready, u + 1)
                if not first:
                    pe.wait_ge(sc_ready, u - (RING - 1))
                for b in range(TB):
                    last = nc.tensor.matmul(ps[:, 4 + s, b * P:(b + 1) * P], qs[:, s, b * P:(b + 1) * P],
                                            skt[:, bass.ds(u, 1), :].rearrange("p o n -> p (o n)"),
                                            start=True, stop=True, skip_group_check=True)
                last.then_inc(ss_done, 1)

            queries(0, 0)
            pe.wait_ge(skt_full, 16)
            for s in range(1, RING):
                queries(0, s)
                scores(0, s - 1, first=True)
            queries(1, 0)
            scores(0, RING - 1, first=True)
            for s in range(1, RING):
                queries(1, s)
                scores(1, s - 1)
            with pe.Fori(2, rounds) as r:
                for s in range(RING):
                    queries(r, s)
                    scores(r if s else r - 1, (s - 1) % RING)
            scores(rounds - 1, RING - 1)
            for s in range(RING):
                pe.wait_ge(next_ring.split_done, s + 1)
                pe.wait_ge(qs_ready, NS + (s + 1 - RING))
                down_tile(nc, t, next_ring, s).then_inc(t["down_done"], 1)

        @block.scalar
        def _(act):
            def high_part(r, s):
                u = RING * r + s
                act.wait_ge(raw_full[s], 16 * r + 16)
                act.wait_ge(unit_done, u - (RING - 1))
                nc.scalar.activation(w_hi[:, s, :], raw[:, s, :], ACT.Copy).then_inc(hi_done, 1)

            def queries_out(r, s, first):
                u = RING * r + s
                act.wait_ge(unit_done, u + 1)
                if not first:
                    act.wait_ge(ss_done, u - (RING - 1))
                nc.scalar.activation(qs[:, s, :], ps[:, s, :], ACT.Copy).then_inc(qs_ready, 1)

            for s in range(RING):
                high_part(1, s)
                queries_out(0, s, True)
            with act.Fori(1, rounds - 1) as r:
                for s in range(RING):
                    high_part(r + 1, s)
                    queries_out(r, s, False)
            for s in range(RING):
                queries_out(rounds - 1, s, False)
                next_ring.high_first(act, s)

        @block.vector
        def _(dve):
            steps = Count(dve_step)

            def done():
                dve.wait_ge(dve_step, steps.n)

            with dve.Fori(0, rounds) as r:
                dve.sem_clear(dve_step)
                steps.n = 0
                for s in range(RING):
                    dve.wait_ge(ss_done, RING * r + (s + 1))
                    nc.vector.tensor_copy(sc[:, s], ps[:, 4 + s, :].rearrange("p (b n) -> p b n", b=TB)
                                          ).then_inc(sc_ready, 1)
                    held(dve, sc_ready, RING * r + (s + 1), passed_dve)
                    top_subkeys(nc, k, steps.up, done, s, sc[:, s])
                    done()
                    unit = bass.ds(RING * r + s, 1)
                    steps.up(nc.vector.tensor_copy(t["v16"][:, :, unit, :].rearrange("p b o n -> p b (o n)"),
                                                   k["best"][:, s]))
                    steps.up(nc.vector.tensor_copy(t["i16"][:, :, unit, :].rearrange("p b o n -> p b (o n)"),
                                                   k["place"][:, s]))
                done()


DB = TB - 1
DT = DB * P
GB = TB - 1
HK = PH * TOPK
TILES = NK
GS = 4
RT = 8
GSCALE = 2.0 ** 15

W4 = RING
TURNS = TILES // W4
LEAD_TURNS, CHOICE_TURNS, GATE_TURNS, ROUNDS = 2, 4, 4, 4
BLOCK_TURNS = CHOICE_TURNS + GATE_TURNS
TAIL_TURN = LEAD_TURNS + DB * BLOCK_TURNS
BLOCK_ROUNDS = GATE_TURNS * ROUNDS
CHOICE_SETS, PAIR_SETS = 2, 3
PAIR_ROWS = (2, 1, 2, 1, 2, 1, 2, 1)
BLOCK_SETS = CHOICE_SETS + PAIR_SETS * GATE_TURNS // 2 + 1
PIECES = 16
PB = NK // PIECES


def down_tile(nc, t, ring, s):
    out, b_hi, b_lo = t["ps"][:, s, 0:DT], t["b_hi"], t["b_lo"]
    for c in range(KC):
        w = slice(c * P, (c + 1) * P)
        nc.tensor.matmul(out, ring.w_hi[:, s, w], b_hi[:, c, 0:DT], start=c == 0, stop=False)
        nc.tensor.matmul(out, ring.w_hi[:, s, w], b_lo[:, c, 0:DT], start=False, stop=False)
        last = nc.tensor.matmul(out, ring.w_lo[:, s, w], b_hi[:, c, 0:DT], start=False, stop=c == KC - 1)
    return last


def down_block(nc, t, ring, next_ring, up):
    b_hi, b_lo, ps, ident = t["b_hi"], t["b_lo"], t["ps"], t["ident"]
    ctx = ExitStack()
    with ctx:
        def sb(name, shape, dt=F32):
            return ctx.enter_context(nc.sbuf_tensor(name, shape, dt))

        def sem(name):
            return ctx.enter_context(nc.semaphore(name))

        raw, w_hi, w_lo, raw_full, hi_done, split_done = (
            ring.raw, ring.w_hi, ring.w_lo, ring.raw_full, ring.hi_done, ring.split_done)
        act_t = sb("act_t", [P, 2, DT])
        gmat = t["gmat"]
        c0 = sb("c0", [P, PH, TOPK * TOPK])
        gb = sb("gb", [P, 2, 2, P, RT], F16)
        c1 = gb[:].rearrange("p q i n j -> p (q i n j)").bitcast(F32).rearrange("p (h i) -> p h i", h=PH)
        k = {"v16": t["v16"], "i16": t["i16"], "c0": c0[:], "c1": c1, "top": sb("top", [P, PH, TOPK]),
             "flat": sb("flat", [P, PH, TOPK], U32), "fi": sb("fi", [P, 2, PH, TOPK], U32),
             "fif": sb("fif", [P, 2, PH, TOPK]), "ab": sb("ab", [P, 2, PH, TOPK]),
             "ex": sb("ex", [P, PH, TOPK]), "gsum": sb("gsum", [P, PH]), "iota": sb("iota", [P, P])}
        gate_h = sb("gate_h", [P, PH, TOPK], F16)
        gparts = sb("gparts", [P, 3, PH, TOPK])
        cols = sb("cols", [P, 4, P], F16)
        numbers = sb("numbers", [P, P, RT], F16)
        eq_a = sb("eq_a", [P, 2, P, RT], F16)
        eq_b = sb("eq_b", [P, P, RT], F16)
        rows = sb("rows", [P, GS, D])
        idx = sb("idx", [P, GS], U32)
        ef = sb("ef", [P, HK])
        expert, gate, dn = t["expert"], t["gate"], t["dn"]
        xb = b_hi[:, :, DT:].bitcast(F32)

        unit_done = t["down_done"]
        gelu_done = sem("gelu3_done")
        act_stored = [sem(f"act_stored{i}") for i in range(2)]
        exp_in, exp_out = sem("exp_in"), sem("exp_out")
        k["exp_in"] = exp_in
        const_full = sem("const_full")
        experts_ready, row_free, idx_ready = sem("experts_ready"), sem("row3_free"), sem("idx3_ready")
        row_full = [sem(f"row3_full{i}") for i in range(GS)]
        picks_ready, picks_turned, cols_ready = sem("picks_ready"), sem("picks_turned"), sem("cols_ready")
        eq_step, gb_step, gb_ready, round_done, round_free = (
            sem("eq_step"), sem("gb_step"), sem("gb_ready"), sem("round_done"), sem("round_free"))
        gmat_free = sem("gmat_free")
        dve_step, passed_dve, passed_pool = sem("dve3_step"), sem("passed_dve3"), sem("passed_pool3")
        block = ctx.enter_context(nc.Block())

        @block.sync
        def _(sp):
            def load(n, s):
                sp.dma_start(raw[:, s, :], t["down_t"][bass.ds(W4 * n + s, 1)].rearrange("o p n -> (o p) n")
                             ).then_inc(raw_full[s], 16)

            def store(n, s):
                u = W4 * n + s
                dst = t["act_d"][u] if isinstance(n, int) else t["act_d"][bass.ds(u, 1)].rearrange("o p n -> (o p) n")
                sp.wait_ge(gelu_done, u + 1)
                sp.dma_start(dst, act_t[:, s % 2, :]).then_inc(act_stored[s % 2], 16)

            sp.dma_start(k["iota"][:], t["iota"].partition_broadcast(P)).then_inc(const_full, 16)
            sp.dma_start(xb, t["x2_d"][GB].rearrange("p (c j) -> p c j", c=KC)).then_inc(const_full, 16)
            with sp.Fori(0, TURNS - 2) as n:
                for s in range(W4):
                    store(n, s)
                    sp.wait_ge(split_done, W4 * n + (W4 + s + 1))
                    load(n + 2, s)
            sp.wait_ge(gmat_free, 16 * PIECES * (DB + 1))
            for i in range(2):
                sp.wait_ge(act_stored[i], 32)
            for s in range(W4):
                sp.dma_start(up.act_t[:, s, :], t["act_d"][s]).then_inc(up.ag_full[s], 16)
                sp.dma_start(up.gate_t[:, s, :], t["gate_d"][s]).then_inc(up.ag_full[s], 16)
            for s in range(W4):
                store(TURNS - 2, s)
                sp.wait_ge(split_done, TILES + (s + 1 - W4))
                next_ring.load_first(sp, s)
            for s in range(W4):
                store(TURNS - 1, s)
            for i in range(2):
                sp.wait_ge(act_stored[i], 16 * TILES // 2)

        @block.gpsimd
        def _(pool):
            def split_low(n, s):
                u = W4 * n + s
                held(pool, hi_done, u + 1, passed_pool)
                nc.gpsimd.tensor_tensor(w_lo[:, s, :], raw[:, s, :], w_hi[:, s, :].bitcast(F32),
                                        ALU.subtract).then_inc(split_done, 1)

            def gather(n, j):
                m = GS * n + j
                held(pool, row_free, m + 1, passed_pool)
                nc.gpsimd.tensor_copy(idx[:, j:j + 1], expert[:, bass.ds(m, 1)]).then_inc(idx_ready, 1)
                held(pool, idx_ready, m + 1, passed_pool)
                nc.gpsimd.indirect_dma_start(rows[:, j, :], None, t["w_down"],
                                             bass.IndirectOffsetOnAxis(ap=idx[:, j:j + 1], axis=0)
                                             ).then_inc(row_full[j], 16)

            with pool.Fori(1, LEAD_TURNS + 1) as n:
                for s in range(W4):
                    split_low(n, s)
            pool.wait_ge(experts_ready, 1)
            with pool.Fori(0, DB) as b:
                t1 = LEAD_TURNS + 1 + BLOCK_TURNS * b
                with pool.Fori(0, CHOICE_SETS) as r:
                    for s in range(W4):
                        split_low(t1 + r, s)
                        gather(BLOCK_SETS * b + r, s)
                for s in range(W4):
                    split_low(t1 + CHOICE_SETS, s)
                with pool.Fori(0, GATE_TURNS // 2) as r:
                    made = 0
                    for i, rows_now in enumerate(PAIR_ROWS):
                        split_low(t1 + CHOICE_SETS + 1 + 2 * r + i // W4, i % W4)
                        for _ in range(rows_now):
                            gather(BLOCK_SETS * b + CHOICE_SETS + PAIR_SETS * r + made // GS, made % GS)
                            made += 1
                for s in range(W4):
                    split_low(t1 + BLOCK_TURNS - 1, s)
                    gather(BLOCK_SETS * b + BLOCK_SETS - 1, s)
            with pool.Fori(0, TURNS - TAIL_TURN - 1) as r:
                for s in range(W4):
                    split_low(TAIL_TURN + 1 + r, s)
                    gather(DB * BLOCK_SETS + r, s)
            for s in range(W4 - 1):
                pool.wait_ge(unit_done, TILES + (s + 1 - W4))
                next_ring.low_first(pool, s)

        @block.scalar
        def _(act):
            act.sem_inc(round_free, 2)
            act.sem_inc(gmat_free, 16 * PIECES)

            def high_part(n, s):
                act.wait_ge(raw_full[s], 16 * n + 16)
                act.wait_ge(unit_done, W4 * n + (s + 1 - W4))
                nc.scalar.activation(w_hi[:, s, :], raw[:, s, :], ACT.Copy).then_inc(hi_done, 1)

            def gelu(n, s, first=False):
                act.wait_ge(unit_done, W4 * n + (s + 1))
                if not first:
                    act.wait_ge(act_stored[s % 2], 32 * n + 16 * (s // 2))
                nc.scalar.activation(act_t[:, s % 2, :], ps[:, s, 0:DT], ACT.Gelu).then_inc(gelu_done, 1)

            def store_piece(b, i):
                act.dma_start(t["gate_d"][bass.ds(PB * i, PB), :, bass.ds(P * b, P)].rearrange("b a j -> a b j"),
                              gmat[:, bass.ds(PB * i, PB), :]).then_inc(gmat_free, 16)

            def first_pieces(b):
                for i in range(W4):
                    store_piece(b, i)

            def turn(n, b=None, i=None):
                for s in range(W4):
                    gelu(n, s)
                    high_part(n + 1, s)
                    if b is not None:
                        store_piece(b, i + s)

            def exponent(i):
                act.wait_ge(exp_in, i)
                nc.scalar.activation(k["ex"][:], k["ex"][:], ACT.Exp).then_inc(exp_out, 1)

            def gate_out(b, r, q):
                act.wait_ge(round_done, ROUNDS * (GATE_TURNS * b + r) + (q + 3))
                for i in range(2):
                    c = bass.ds(RT * (ROUNDS * r + q) + 4 * i, 4)
                    ins = nc.scalar.activation(gmat[:, :, c].rearrange("p b j -> p j b"),
                                               ps[:, 4 + 2 * (q % 2) + i, :].rearrange("p (j b) -> p j b", j=4), ACT.Copy)
                ins.then_inc(round_free, 1)

            def dense_block(b, first=False):
                t0 = LEAD_TURNS + BLOCK_TURNS * b
                stored = {} if first else {"b": b - 1}
                if not first:
                    first_pieces(b - 1)
                with act.Fori(0, CHOICE_TURNS - 2) as r:
                    turn(t0 + r, **stored, i=W4 * (r + 1))
                exponent(b + 2)
                turn(t0 + CHOICE_TURNS - 2, **stored, i=W4 * (CHOICE_TURNS - 1))
                turn(t0 + CHOICE_TURNS - 1)
                with act.Fori(0, GATE_TURNS) as r:
                    for s in range(W4):
                        gelu(t0 + CHOICE_TURNS + r, s)
                        high_part(t0 + CHOICE_TURNS + 1 + r, s)
                        act.wait_ge(gmat_free, 16 * PIECES * b + 16 * PIECES)
                        gate_out(b, r, s)
                act.wait_ge(round_free, BLOCK_ROUNDS * b + (BLOCK_ROUNDS + 2))

            for s in range(W4):
                gelu(0, s, first=s < 2)
                high_part(1, s)
            with act.Fori(1, LEAD_TURNS) as n:
                turn(n)
            exponent(1)
            dense_block(0, first=True)
            with act.Fori(1, DB) as b:
                dense_block(b)
            first_pieces(DB - 1)
            with act.Fori(0, PIECES // W4 - 1) as r:
                turn(TAIL_TURN + r, DB - 1, W4 * (r + 1))
            with act.Fori(TAIL_TURN + PIECES // W4 - 1, TURNS - 1) as n:
                turn(n)
            for s in range(W4):
                gelu(TURNS - 1, s)
                next_ring.high_first(act, s)
            act.wait_ge(gmat_free, 16 * PIECES * (DB + 1))

        @block.tensor
        def _(pe):
            pe.sem_inc(round_done, 2)

            def tile(n, s):
                u = W4 * n + s
                pe.wait_ge(split_done, u + 1)
                pe.wait_ge(gelu_done, u - (W4 - 1))
                down_tile(nc, t, ring, s).then_inc(unit_done, 1)

            def turn(n):
                for s in range(W4):
                    tile(n, s)

            def turn_picks(b):
                pe.wait_ge(picks_ready, b + 1)
                pe.wait_ge(round_free, BLOCK_ROUNDS * b + 2)
                for i, src in enumerate((k["ab"][:, 0], k["ab"][:, 1], gparts[:, 1], gparts[:, 2])):
                    last = nc.tensor.transpose(ps[:, 4, i * P:(i + 1) * P], src.rearrange("p h k -> p (h k)"), ident[:])
                last.then_inc(picks_turned, 1)

            def gate_round(b, r, q):
                rho = ROUNDS * (GATE_TURNS * b + r) + q
                pe.wait_ge(gb_ready, rho + 1)
                pe.wait_ge(round_free, rho + 1)
                for j in range(RT):
                    out = ps[:, 4 + 2 * (q % 2) + j // 4, (j % 4) * P:(j % 4 + 1) * P]
                    nc.tensor.matmul(out, eq_a[:, q % 2, :, j], gb[:, q % 2, 0, :, j], start=True, stop=False,
                                     skip_group_check=True)
                    last = nc.tensor.matmul(out, eq_a[:, q % 2, :, j], gb[:, q % 2, 1, :, j], start=False, stop=True,
                                            skip_group_check=True)
                last.then_inc(round_done, 1)

            with pe.Fori(1, LEAD_TURNS) as n:
                turn(n)
            with pe.Fori(0, DB) as b:
                t0 = LEAD_TURNS + BLOCK_TURNS * b
                with pe.Fori(0, CHOICE_TURNS - 1) as r:
                    turn(t0 + r)
                for s in range(W4):
                    if s == W4 - 1:
                        turn_picks(b)
                    tile(t0 + CHOICE_TURNS - 1, s)
                with pe.Fori(0, GATE_TURNS) as r:
                    for s in range(W4):
                        tile(t0 + CHOICE_TURNS + r, s)
                        gate_round(b, r, s)
            with pe.Fori(TAIL_TURN, TURNS) as n:
                turn(n)

        @block.vector
        def _(dve):
            n_steps = [0]

            def step(ins):
                ins.then_inc(dve_step, 1)
                n_steps[0] += 1

            def done():
                dve.wait_ge(dve_step, n_steps[0])

            def restart():
                dve.sem_clear(dve_step)
                n_steps[0] = 0

            def dot(n, j):
                if isinstance(n, int):
                    dve.wait_ge(row_full[j], 16 * n + 16)
                else:
                    held(dve, row_full[j], 16 * n + 16, passed_dve)
                row = rows[:, j, :].rearrange("p (c i) -> p c i", c=KC)
                nc.vector.scalar_tensor_tensor(out=row, in0=row, scalar=1.0, in1=xb,
                                               op0=ALU.mult, op1=ALU.mult,
                                               accum_out=dn[:, bass.ds(GS * n + j, 1)]).then_inc(row_free, 1)

            def dots(n):
                for j in range(GS):
                    dot(n, j)

            dve.sem_inc(row_free, GS)
            dve.wait_ge(const_full, 32)
            step(nc.vector.tensor_copy(numbers[:], k["iota"][:].unsqueeze(2).broadcast_to([P, P, RT])))
            top_experts(nc, step, done, k, GB, lambda: None)
            step(nc.vector.scalar_tensor_tensor(out=ef[:], in0=k["ab"][:, 0].rearrange("p h k -> p (h k)"),
                                                scalar=float(NK), in1=k["ab"][:, 1].rearrange("p h k -> p (h k)"),
                                                op0=ALU.mult, op1=ALU.add))
            done()
            nc.vector.tensor_copy(expert[:], ef[:]).then_inc(experts_ready, 1)
            dve.wait_ge(exp_out, 1)
            gates(nc, step, done, k, gate[:])
            done()
            with dve.Fori(0, DB) as b:
                restart()
                made = [0]

                def between():
                    dot(BLOCK_SETS * b, made[0])
                    made[0] += 1

                held(dve, round_done, BLOCK_ROUNDS * b + 2, passed_dve)
                top_experts(nc, step, done, k, b, between)
                assert made[0] == GS
                held(dve, exp_out, b + 2, passed_dve)
                gates(nc, step, done, k, gparts[:, 0])
                done()
                step(nc.vector.tensor_scalar(gparts[:, 0], gparts[:, 0], GSCALE, None, ALU.mult))
                done()
                step(nc.vector.tensor_copy(gate_h[:], gparts[:, 0]))
                done()
                step(nc.vector.tensor_copy(gparts[:, 1], gate_h[:]))
                done()
                nc.vector.tensor_tensor(gparts[:, 2], gparts[:, 0], gparts[:, 1], ALU.subtract).then_inc(picks_ready, 1)
                for i in range(1, CHOICE_SETS):
                    dots(BLOCK_SETS * b + i)
                held(dve, picks_turned, b + 1, passed_dve)
                nc.vector.tensor_copy(cols[:], ps[:, 4, :].rearrange("p (i j) -> p i j", i=4)).then_inc(cols_ready, 1)
                held(dve, cols_ready, b + 1, passed_dve)
                with dve.Fori(0, GATE_TURNS // 2) as r:
                    made_rows = 0
                    for i in range(2 * ROUNDS):
                        rho = BLOCK_ROUNDS * b + 2 * ROUNDS * r + i
                        q = i % 2
                        held(dve, round_done, rho + 1, passed_dve)
                        tok = bass.ds(RT * (2 * ROUNDS * r + i), RT)
                        of = [cols[:, j, tok].unsqueeze(1).broadcast_to([P, P, RT]) for j in range(4)]
                        nc.vector.tensor_tensor(eq_b[:], numbers[:], of[1], ALU.is_equal).then_inc(eq_step, 1)
                        nc.vector.tensor_tensor(eq_a[:, q], numbers[:], of[0], ALU.is_equal).then_inc(eq_step, 1)
                        dve.wait_ge(eq_step, 2 * i + 1)
                        nc.vector.tensor_tensor(gb[:, q, 0], eq_b[:], of[2], ALU.mult).then_inc(gb_step, 1)
                        nc.vector.tensor_tensor(gb[:, q, 1], eq_b[:], of[3], ALU.mult).then_inc(gb_step, 1)
                        dve.wait_ge(eq_step, 2 * i + 2)
                        dve.wait_ge(gb_step, 2 * i + 2)
                        dve.sem_inc(gb_ready, 1)
                        for _ in range(PAIR_ROWS[i]):
                            dot(BLOCK_SETS * b + CHOICE_SETS + PAIR_SETS * r + made_rows // GS, made_rows % GS)
                            made_rows += 1
                    dve.sem_clear(eq_step)
                    dve.sem_clear(gb_step)
                dots(BLOCK_SETS * b + (BLOCK_SETS - 1))
            with dve.Fori(DB * BLOCK_SETS, HK // GS - 1) as n:
                dots(n)
            for s in range(W4):
                dve.wait_ge(up.ag_full[s], 32)
                up.product(s)
            for j in range(GS):
                dot(HK // GS - 1, j)


class Gated:

    def __init__(self, nc, ctx, gmat, b_hi, b_lo):
        self.nc = nc

        def slots(flat, i):
            return flat[:, i * W4 * DT:(i + 1) * W4 * DT].rearrange("p (s j) -> p s j", s=W4)

        self.act_t, self.gate_t, self.h_t = (slots(gmat[:].rearrange("p b j -> p (b j)"), i) for i in range(3))
        self.h_hi, self.h_lo = (slots(x[:].rearrange("p c j -> p (c j)"), 0) for x in (b_hi, b_lo))
        self.ag_full = [ctx.enter_context(nc.semaphore(f"ag_full{i}")) for i in range(W4)]
        self.h_ready, self.h_hi_done, self.h_split = (
            ctx.enter_context(nc.semaphore(name)) for name in ("h_ready", "h_hi_done", "h_split"))

    def product(self, s):
        self.nc.vector.scalar_tensor_tensor(out=self.h_t[:, s, :], in0=self.act_t[:, s, :], scalar=1.0 / GSCALE,
                                            in1=self.gate_t[:, s, :], op0=ALU.mult, op1=ALU.mult).then_inc(self.h_ready, 1)

    def high(self, act, s, ready):
        act.wait_ge(self.h_ready, ready)
        self.nc.scalar.activation(self.h_hi[:, s, :], self.h_t[:, s, :], ACT.Copy).then_inc(self.h_hi_done, 1)

    def low(self, s):
        self.nc.vector.tensor_tensor(self.h_lo[:, s, :], self.h_t[:, s, :], self.h_hi[:, s, :].bitcast(F32),
                                     ALU.subtract).then_inc(self.h_split, 1)


def up_block(nc, t, out, ring, up):
    ps, expert, gate, dn = t["ps"], t["expert"], t["gate"], t["dn"]
    ctx = ExitStack()
    with ctx:
        def sb(name, shape, dt=F32):
            return ctx.enter_context(nc.sbuf_tensor(name, shape, dt))

        def sem(name):
            return ctx.enter_context(nc.semaphore(name))

        raw, w_hi, w_lo, raw_full, hi_done, split_done = (
            ring.raw, ring.w_hi, ring.w_lo, ring.raw_full, ring.hi_done, ring.split_done)
        rows = sb("rows4", [P, W4, D])
        idx = sb("idx4", [P, W4], U32)
        acc = sb("acc", [P, 2, D])
        coef = sb("coef", [P, HK])
        xres = sb("xres4", [P, TB, D])
        lng, lnb = sb("ln3g", [P, D]), sb("ln3b", [P, D])
        bst, mv, vc, sd = sb("bst3", [P, 2 * TB, 6]), sb("mv3", [P, TB, 2]), sb("vc3", [P, TB]), sb("sd3", [P, TB])
        rc, nt = sb("rc3", [P, TB]), sb("nt3", [P, 2, TB])

        unit_done, block_done, res_added = sem("unit4_done"), sem("block4_done"), sem("res4_added")
        h_ready, h_hi_done, h_split, h_hi, h_lo = up.h_ready, up.h_hi_done, up.h_split, up.h_hi, up.h_lo
        row_free, idx_ready = sem("row4_free"), sem("idx4_ready")
        row_full = [sem(f"row4_full{i}") for i in range(W4)]
        gelu_done, xg_full, x2_full, ln_full = sem("gelu4_done"), sem("xg_full"), sem("x2_full"), sem("ln3_full")
        var_ready, sd_ready, res_ready, out_done = sem("var4_ready"), sem("sd4_ready"), sem("res_ready"), sem("out_done")
        dve_step, passed_dve, passed_pool = sem("dve4_step"), sem("passed_dve4"), sem("passed_pool4")
        block = ctx.enter_context(nc.Block())

        def held_or(eng, semaphore, value, passed):
            if isinstance(value, int):
                eng.wait_ge(semaphore, value)
            else:
                held(eng, semaphore, value, passed)

        @block.sync
        def _(sp):
            def load(n, s):
                u = W4 * n + s
                w, a, g = (t[name][bass.ds(u, 1)].rearrange("o p n -> (o p) n") for name in ("up_t", "act_d", "gate_d"))
                sp.wait_ge(split_done, u - (W4 - 1))
                sp.dma_start(raw[:, s, :], w).then_inc(raw_full[s], 16)
                sp.wait_ge(h_ready, u - (W4 - 1))
                sp.dma_start(up.act_t[:, s, :], a).then_inc(up.ag_full[s], 16)
                sp.dma_start(up.gate_t[:, s, :], g).then_inc(up.ag_full[s], 16)

            sp.dma_start(xres[:, GB, :], t["x2_d"][GB]).then_inc(xg_full, 16)
            with sp.Fori(1, TURNS) as n:
                for s in range(W4):
                    load(n, s)
            sp.dma_start(xres[:, 0:DB, :], t["x2_d"][0:DB].rearrange("b p d -> p b d")).then_inc(x2_full, 16)
            sp.dma_start(lng[:], t["ln3_g"].partition_broadcast(P)).then_inc(ln_full, 16)
            sp.dma_start(lnb[:], t["ln3_b"].partition_broadcast(P)).then_inc(ln_full, 16)
            for b in range(TB):
                sp.wait_ge(res_ready, b + 1)
                sp.dma_start(out[0, b * P:(b + 1) * P, :], xres[:, b, :]).then_inc(out_done, 16)
            sp.wait_ge(out_done, 16 * TB)

        @block.gpsimd
        def _(pool):
            def split_low(n, s):
                held(pool, hi_done, W4 * n + (s + 1), passed_pool)
                nc.gpsimd.tensor_tensor(w_lo[:, s, :], raw[:, s, :], w_hi[:, s, :].bitcast(F32),
                                        ALU.subtract).then_inc(split_done, 1)

            def gather(n, s):
                u = W4 * n + s
                held_or(pool, row_free, u + 1, passed_pool)
                nc.gpsimd.tensor_copy(idx[:, s:s + 1], expert[:, bass.ds(u, 1)]).then_inc(idx_ready, 1)
                held_or(pool, idx_ready, u + 1, passed_pool)
                nc.gpsimd.indirect_dma_start(rows[:, s, :], None, t["w_up"],
                                             bass.IndirectOffsetOnAxis(ap=idx[:, s:s + 1], axis=0)
                                             ).then_inc(row_full[s], 16)

            ring.low_first(pool, W4 - 1)
            for s in range(W4):
                gather(0, s)
            with pool.Fori(1, TURNS) as n:
                for s in range(W4):
                    split_low(n, s)
                    gather(n, s)

        @block.scalar
        def _(act):
            for s in range(W4):
                up.high(act, s, s + 1)
            nc.scalar.activation(coef[:], dn[:], ACT.Gelu).then_inc(gelu_done, 1)
            with act.Fori(1, TURNS) as n:
                for s in range(W4):
                    act.wait_ge(raw_full[s], 16 * n + 16)
                    act.wait_ge(unit_done, W4 * n + (s + 1 - W4))
                    nc.scalar.activation(w_hi[:, s, :], raw[:, s, :], ACT.Copy).then_inc(hi_done, 1)
                    up.high(act, s, W4 * n + (s + 1))
            act.wait_ge(var_ready, 1)
            nc.scalar.activation(sd[:], vc[:], ACT.Sqrt).then_inc(sd_ready, 1)

        @block.tensor
        def _(pe):
            def tile(n, s, start=False, stop=False):
                u = W4 * n + s
                pe.wait_ge(split_done, u + 1)
                pe.wait_ge(h_split, u + 1)
                for b in range(DB):
                    for h in range(2):
                        c, tk = slice(h * HALF, (h + 1) * HALF), slice(b * P, (b + 1) * P)
                        o = ps[:, 2 * b + h, :]
                        nc.tensor.matmul(o, h_hi[:, s, tk], w_hi[:, s, c], start=start, stop=False)
                        nc.tensor.matmul(o, h_hi[:, s, tk], w_lo[:, s, c], start=False, stop=False)
                        last = nc.tensor.matmul(o, h_lo[:, s, tk], w_hi[:, s, c], start=False, stop=stop)
                    if stop and b < DB - 1:
                        last.then_inc(block_done, 1)
                last.then_inc(unit_done, 1)

            for s in range(W4):
                tile(0, s, start=s == 0)
            with pe.Fori(1, TURNS - 1) as n:
                for s in range(W4):
                    tile(n, s)
            for s in range(W4):
                tile(TURNS - 1, s, stop=s == W4 - 1)

        @block.vector
        def _(dve):
            step_count = Count(dve_step)
            step = step_count.up

            def done():
                dve.wait_ge(dve_step, step_count.n)

            dve.sem_inc(row_free, W4)
            for s in range(W4 - 1):
                dve.wait_ge(h_hi_done, s + 1)
                up.low(s)
            step(nc.vector.memset(acc[:, 1, :], 0.0))
            dve.wait_ge(xg_full, 16)
            step(nc.vector.tensor_scalar(acc[:, 0, :], xres[:, GB, :], ALPHA, None, ALU.mult))
            dve.wait_ge(gelu_done, 1)
            step(nc.vector.tensor_tensor(coef[:], coef[:], gate[:].rearrange("p h k -> p (h k)"), ALU.mult))
            done()

            def gated(n, s):
                held(dve, up.ag_full[s], 32 * n + 32, passed_dve)
                held(dve, h_split, W4 * n + (s + 1 - W4), passed_dve)
                up.product(s)

            def low(n, s):
                held_or(dve, h_hi_done, W4 * n + (s + 1), passed_dve)
                up.low(s)

            def row(n, s):
                held_or(dve, row_full[s], 16 * n + 16, passed_dve)
                held_or(dve, row_free, W4 * n + (s + 3), passed_dve)
                nc.vector.scalar_tensor_tensor(out=acc[:, s % 2, :], in0=rows[:, s, :],
                                               scalar=coef[:, bass.ds(W4 * n + s, 1)], in1=acc[:, s % 2, :],
                                               op0=ALU.mult, op1=ALU.add).then_inc(row_free, 1)

            with dve.Fori(0, TURNS - 1) as n:
                for s in range(W4):
                    gated(n + 1, s)
                    low(n + (s + 3) // W4, (s + 3) % W4)
                    row(n, s)
            low(TURNS - 1, W4 - 1)
            for s in range(W4):
                row(TURNS - 1, s)
            dve.wait_ge(row_free, TILES + W4)
            step(nc.vector.tensor_tensor(xres[:, GB, :], acc[:, 0, :], acc[:, 1, :], ALU.add))
            done()

            def statistics(b):
                for h in range(2):
                    step(nc.vector.bn_stats(bst[:, 2 * b + h, :], xres[:, b, h * HALF:(h + 1) * HALF]))

            statistics(GB)
            dve.wait_ge(x2_full, 16)
            for b in range(DB):
                if b < DB - 1:
                    dve.wait_ge(block_done, b + 1)
                else:
                    dve.wait_ge(unit_done, TILES)
                for h in range(2):
                    c = slice(h * HALF, (h + 1) * HALF)
                    nc.vector.scalar_tensor_tensor(out=xres[:, b, c], in0=xres[:, b, c], scalar=ALPHA,
                                                   in1=ps[:, 2 * b + h, :], op0=ALU.mult, op1=ALU.add
                                                   ).then_inc(res_added, 1)
                if b:
                    dve.wait_ge(res_added, 2 * b)
                    statistics(b - 1)
            dve.wait_ge(res_added, 2 * DB)
            statistics(DB - 1)
            dve.wait_ge(ln_full, 32)
            done()
            for b in range(TB):
                step(nc.vector.bn_aggr(mv[:, b, :], bst[:, 2 * b:2 * b + 2, :]))
            done()
            nc.vector.tensor_scalar(vc[:], mv[:, :, 1], EPS, None, ALU.add).then_inc(var_ready, 1)
            dve.wait_ge(sd_ready, 1)
            step(nc.vector.reciprocal(rc[:], sd[:]))
            done()
            step(nc.vector.tensor_tensor(nt[:, 0], rc[:], rc[:], ALU.mult))
            done()
            step(nc.vector.tensor_tensor(nt[:, 1], nt[:, 0], vc[:], ALU.mult))
            done()
            step(nc.vector.tensor_scalar(nt[:, 0], nt[:, 1], -0.5, 1.5, ALU.mult, ALU.add))
            done()
            step(nc.vector.tensor_tensor(rc[:], rc[:], nt[:, 0], ALU.mult))
            done()
            for b in range(TB):
                step(nc.vector.scalar_tensor_tensor(out=xres[:, b, :], in0=xres[:, b, :], scalar=mv[:, b, 0:1],
                                                    in1=lng[:], op0=ALU.subtract, op1=ALU.mult))
                done()
                nc.vector.scalar_tensor_tensor(out=xres[:, b, :], in0=xres[:, b, :], scalar=rc[:, b:b + 1],
                                               in1=lnb[:], op0=ALU.mult, op1=ALU.add).then_inc(res_ready, 1)


def build(nc, ins, out):
    ctx = ExitStack()
    with ctx:
        def sb(name, shape, dt=F32):
            return ctx.enter_context(nc.sbuf_tensor(name, shape, dt))

        t = dict(ins)
        t["x2_d"] = nc.dram_tensor("x2_d", (TB, P, D), F32, kind="Internal").ap()
        t["act_d"] = nc.dram_tensor("act_d", (TILES, P, DT), F32, kind="Internal").ap()
        t["gate_d"] = nc.dram_tensor("gate_d", (TILES, P, DT), F32, kind="Internal").ap()
        t["ident"] = sb("ident", [P, P])
        t["expert"], t["gate"], t["dn"] = sb("expert", [P, HK], U32), sb("gate", [P, PH, TOPK]), sb("dn", [P, HK])
        t["ps"] = ctx.enter_context(nc.psum_tensor("ps", [P, 8, HALF], F32))
        t["raw"], t["w_hi"], t["w_lo"] = (sb("raw", [P, RING, D]), sb("w_hi", [P, RING, D], F32R),
                                          sb("w_lo", [P, RING, D], F32R))
        t["x2_stored"], t["down_done"] = (ctx.enter_context(nc.semaphore(name)) for name in ("x2_stored", "down_done"))
        rings = [Ring(nc, ctx, name, t, units) for name, units in (
            ("front", ins["units"]), ("query", ins["units"][FRONT_UNITS:]), ("down", ins["down_t"]), ("up", ins["up_t"]))]
        with ExitStack() as x2_scope:
            t["v16"] = x2_scope.enter_context(nc.sbuf_tensor("v16", [P, TB, NS, TOPK], F32))
            t["i16"] = x2_scope.enter_context(nc.sbuf_tensor("i16", [P, TB, NS, TOPK], F32))
            t["b_hi"] = x2_scope.enter_context(nc.sbuf_tensor("b_hi", [P, KC, S], F32R))
            t["b_lo"] = x2_scope.enter_context(nc.sbuf_tensor("b_lo", [P, KC, S], F32R))
            front_block(nc, t, ins["units"], rings[0], rings[1])
            scores_block(nc, t, ins["units"][FRONT_UNITS:], rings[1], rings[2])
            t["gmat"] = x2_scope.enter_context(nc.sbuf_tensor("gmat", [P, NK, P], F32))
            up = Gated(nc, ctx, t["gmat"], t["b_hi"], t["b_lo"])
            down_block(nc, t, rings[2], rings[3], up)
            up_block(nc, t, out, rings[3], up)


def layout(x, mem, w_in, b_in, sgu_g, sgu_b, w_spatial, b_spatial, conv_w, w_mix_out, ln1_g, ln1_b, w_xq, w_xkv,
           w_xo, ln2_g, ln2_b, w_pq, sub_keys, w_down, w_up, ln3_g, ln3_b):
    import numpy as np
    c = np.ascontiguousarray

    def by_rows(w):
        return w.reshape(-1, P, D)

    def by_columns(w):
        return w.reshape(KC, P, -1, P).transpose(2, 1, 0, 3).reshape(-1, P, D)

    w = w_in[0]
    a = D // 2
    va = w[:, a:2 * a].reshape(4, 2, P, a).transpose(0, 2, 1, 3).reshape(4, P, D)
    h, gb, gc = (by_columns(w[:, 2 * a + i * a:2 * a + (i + 1) * a]) for i in range(3))
    conv = np.stack([h, gc, gb], 1).reshape(12, P, D)
    mix = by_rows(w_mix_out[0])
    units = np.concatenate([by_columns(w_xkv[0][:, :D]), va, conv, by_columns(w[:, :a]), mix[KC // 2:], mix[:KC // 2],
                            by_rows(w_xkv[0][:, D:]), by_columns(w_xq[0]), by_rows(w_xo[0]), by_columns(w_pq[0])])
    return {
        "units": units,
        "mem_t": c(mem[0].T.reshape(KC, P, M).transpose(1, 0, 2)),
        "x_t": c(x[0].T.reshape(KC, P, S).transpose(1, 0, 2)),
        "x_tok": c(x[0].reshape(TB, P, D).transpose(1, 0, 2)),
        "bcol": c(b_in[0].reshape(20, P).T),
        "cw": c(conv_w[0][:, 0].reshape(3, 4, P).transpose(2, 0, 1)),
        "wst": c(w_spatial[0].transpose(2, 0, 1)),
        "bias_va": c(b_in[0][a:2 * a]),
        "sgu_g": sgu_g[0].reshape(-1), "sgu_b": sgu_b[0].reshape(-1), "bsp": b_spatial[0].reshape(-1),
        "skt": c(sub_keys[0].reshape(NS, NK, P).transpose(2, 0, 1)),
        "iota": np.arange(P, dtype=np.float32),
        "down_t": c(w_down[0].reshape(NK, NK, KC, P).transpose(1, 3, 2, 0)).reshape(NK, P, D),
        "up_t": c(w_up[0].reshape(NK, NK, D).transpose(1, 0, 2)),
        "w_down": w_down[0], "w_up": w_up[0], "ln3_g": ln3_g[0], "ln3_b": ln3_b[0],
        "eye": np.eye(P, dtype=np.float32),
        "ln1_g": ln1_g[0], "ln1_b": ln1_b[0], "ln2_g": ln2_g[0], "ln2_b": ln2_b[0],
    }


def kernel(**inputs):
    import numpy as np
    import concourse.bacc as bacc
    from concourse.bass_utils import run_bass_kernel_spmd

    nc = bacc.Bacc("TRN2", target_bir_lowering=False, num_devices=1)
    arrays = {f"in_{k}": np.ascontiguousarray(v) for k, v in layout(**{k: np.asarray(v) for k, v in inputs.items()}).items()}
    ins = {k[3:]: nc.dram_tensor(k, v.shape, mybir.dt.from_np(v.dtype), kind="ExternalInput").ap()
           for k, v in arrays.items()}
    out = nc.dram_tensor("out", (1, S, D), F32, kind="ExternalOutput").ap()
    build(nc, ins, out)
    r = run_bass_kernel_spmd(nc, [arrays], core_ids=[0])
    return r.results[0]["out"]
```
